# Optimizing a Trainium2 kernel written in Bass

```python
import math
import jax
import jax.numpy as jnp
from jax import lax
import numpy as np

D_MODEL = 1024
BATCH = 1
SEQ = 512
DEPTH = 1
DEC_BATCH = 8
DEC_SEQ = 1
PAST_LEN = 2048
PAGE_SIZE = 128

MLA_HEADS = 8
MLA_NOPE = 64
MLA_ROPE = 32
MLA_V = 64
MLA_Q_RANK = 384
MLA_KV_RANK = 256
MLA_ROW = MLA_KV_RANK + MLA_ROPE
DSA_HEADS = 8
DSA_KV_HEADS = 2
DSA_HEAD_DIM = 64
DSA_GROUP = DSA_HEADS // DSA_KV_HEADS
IDX_HEADS = 8
IDX_DIM = 64
TOPK_MAX = 256
D_MIX = MLA_HEADS * MLA_V + DSA_HEADS * DSA_HEAD_DIM
N_BUCKETS = 32
MAX_DISTANCE = 128
ROPE_THETA = 10000.0
D_FF = ((8 * D_MODEL + 3 * 256 - 1) // (3 * 256)) * 256
Q_BLOCK = 128
EPS = 1e-6
IN_SPLITS = (MLA_Q_RANK, MLA_KV_RANK, MLA_ROPE,
             DSA_HEADS * DSA_HEAD_DIM, DSA_KV_HEADS * DSA_HEAD_DIM, DSA_KV_HEADS * DSA_HEAD_DIM,
             IDX_HEADS * IDX_DIM, IDX_DIM, IDX_HEADS)
D_IN = sum(IN_SPLITS)
MLA_SCALE = (MLA_NOPE + MLA_ROPE) ** -0.5
DSA_SCALE = DSA_HEAD_DIM ** -0.5
IDX_SCALE = (IDX_DIM * IDX_HEADS) ** -0.5

kernel_name = 'hymba_mla_dsa_adaln_decode_step'

def rms_norm(x, g):
    xf = x.astype(jnp.float32)
    y = xf * lax.rsqrt(jnp.mean(xf * xf, axis=-1, keepdims=True) + EPS)
    return (y * g.astype(jnp.float32)).astype(x.dtype)

def rope(x, pos):
    half = x.shape[-1] // 2
    freq = ROPE_THETA ** (-jnp.arange(half, dtype=jnp.float32) / half)
    ang = pos.astype(jnp.float32)[:, None] * freq[None, :]
    ang = ang.reshape((ang.shape[0],) + (1,) * (x.ndim - 3) + (half,))
    cos, sin = jnp.cos(ang), jnp.sin(ang)
    xf = x.astype(jnp.float32)
    x1, x2 = xf[..., :half], xf[..., half:]
    return jnp.concatenate([x1 * cos - x2 * sin, x1 * sin + x2 * cos], axis=-1).astype(x.dtype)

def t5_bucket(dist):
    max_exact = N_BUCKETS // 2
    d = jnp.maximum(dist, 0)
    log_ratio = jnp.log(jnp.maximum(d, max_exact).astype(jnp.float32) / max_exact) / math.log(MAX_DISTANCE / max_exact)
    large = jnp.minimum(max_exact + (log_ratio * (N_BUCKETS - max_exact)).astype(jnp.int32), N_BUCKETS - 1)
    return jnp.where(d < max_exact, d, large)

def to_blocks(a, n_blocks):
    return a.reshape((a.shape[0], n_blocks, Q_BLOCK) + a.shape[2:]).swapaxes(0, 1)

def gather_rows(a, idx):
    return jax.vmap(lambda ab, ib: ab[ib])(a, idx)

def mla_expand(lat, w_ukv, g_k_nope):
    kv = jnp.einsum('btr,rhd->bthd', lat, w_ukv)
    return rms_norm(kv[..., :MLA_NOPE], g_k_nope), kv[..., MLA_NOPE:]

def mla_partial(q_nope, q_rope, k_nope, k_rope, v, mask):
    s = (jnp.einsum('bqhd,bkhd->bhqk', q_nope, k_nope)
         + jnp.einsum('bqhd,bkd->bhqk', q_rope, k_rope)).astype(jnp.float32) * MLA_SCALE
    if mask is not None:
        s = jnp.where(mask, s, -jnp.inf)
    m = jnp.max(s, axis=-1)
    p = jnp.exp(s - m[..., None])
    o = jnp.einsum('bhqk,bkhd->bqhd', p, v.astype(jnp.float32))
    return m, jnp.sum(p, axis=-1), o

def mla_prompt(q_nope, q_rope, lat, k_rope, w_ukv, g_k_nope):
    b, s = q_nope.shape[:2]
    nb = s // Q_BLOCK
    k_nope, v = mla_expand(lat, w_ukv, g_k_nope)
    k_pos = jnp.arange(s)

    def block(args):
        qn, qr, i = args
        q_pos = i * Q_BLOCK + jnp.arange(Q_BLOCK)
        m, l, o = mla_partial(qn, qr, k_nope, k_rope, v, k_pos[None, :] <= q_pos[:, None])
        return o / jnp.swapaxes(l, 1, 2)[..., None]

    out = lax.map(block, (to_blocks(q_nope, nb), to_blocks(q_rope, nb), jnp.arange(nb)))
    return out.swapaxes(0, 1).reshape(b, s, MLA_HEADS * MLA_V).astype(q_nope.dtype)

def mla_sample(q_nope, q_rope, lat_new, krope_new, cache_mla, page_table, w_ukv, g_k_nope):
    b, t = q_nope.shape[:2]

    def page(j):
        rows = cache_mla[page_table[:, j]]
        k_nope, v = mla_expand(rows[..., :MLA_KV_RANK], w_ukv, g_k_nope)
        return mla_partial(q_nope, q_rope, k_nope, rows[..., MLA_KV_RANK:], v, None)

    m_p, l_p, o_p = lax.map(page, jnp.arange(page_table.shape[1]))
    k_nope_n, v_n = mla_expand(lat_new, w_ukv, g_k_nope)
    causal = jnp.tril(jnp.ones((t, t), dtype=bool))
    m_n, l_n, o_n = mla_partial(q_nope, q_rope, k_nope_n, krope_new, v_n, causal)
    m_all = jnp.maximum(jnp.max(m_p, axis=0), m_n)
    a_p = jnp.exp(m_p - m_all)
    a_n = jnp.exp(m_n - m_all)
    l = jnp.sum(a_p * l_p, axis=0) + a_n * l_n
    o = jnp.einsum('nbhq,nbqhd->bqhd', a_p, o_p) + jnp.swapaxes(a_n, 1, 2)[..., None] * o_n
    o = o / jnp.swapaxes(l, 1, 2)[..., None]
    return o.reshape(b, t, MLA_HEADS * MLA_V).astype(q_nope.dtype)

def index_scores(q_idx, w_idx, k_idx):
    dots = jnp.einsum('bqhd,bkd->bqhk', q_idx, k_idx).astype(jnp.float32)
    return jnp.einsum('bqhk,bqh->bqk', jax.nn.relu(dots), w_idx.astype(jnp.float32)) * IDX_SCALE

def dsa_attend(q, q_pos, k_sel, v_sel, sel, valid, rel_bias):
    b, t = q.shape[:2]
    n = sel.shape[-1]
    qg = q.reshape(b, t, DSA_KV_HEADS, DSA_GROUP, DSA_HEAD_DIM)
    s = jnp.einsum('bqcgd,bqncd->bqcgn', qg, k_sel).astype(jnp.float32) * DSA_SCALE
    bias = rel_bias[t5_bucket(q_pos[None, :, None] - sel)]
    bias = bias.reshape(b, t, n, DSA_KV_HEADS, DSA_GROUP).transpose(0, 1, 3, 4, 2)
    s = jnp.where(valid[:, :, None, None, :], s + bias.astype(jnp.float32), -jnp.inf)
    p = jax.nn.softmax(s, axis=-1)
    o = jnp.einsum('bqcgn,bqncd->bqcgd', p, v_sel.astype(jnp.float32))
    return o.reshape(b, t, DSA_HEADS * DSA_HEAD_DIM).astype(q.dtype)

def dsa_prompt(q, k, v, q_idx, w_idx, k_idx, rel_bias):
    b, s = q.shape[:2]
    nb = s // Q_BLOCK
    n_sel = min(TOPK_MAX, s // 4)
    k_pos = jnp.arange(s)

    def block(args):
        q_b, qi_b, w_b, i = args
        q_pos = i * Q_BLOCK + jnp.arange(Q_BLOCK)
        sc = jnp.where(k_pos[None, None, :] <= q_pos[None, :, None], index_scores(qi_b, w_b, k_idx), -jnp.inf)
        _, sel = lax.top_k(sc, n_sel)
        valid = sel <= q_pos[None, :, None]
        return dsa_attend(q_b, q_pos, gather_rows(k, sel), gather_rows(v, sel), sel, valid, rel_bias)

    out = lax.map(block, (to_blocks(q, nb), to_blocks(q_idx, nb), to_blocks(w_idx, nb), jnp.arange(nb)))
    return out.swapaxes(0, 1).reshape(b, s, DSA_HEADS * DSA_HEAD_DIM)

def dsa_sample(q, kv_new, q_idx, w_idx, k_idx_new, cache_kv, cache_idx, page_table, rel_bias):
    b, t = q.shape[:2]
    past = page_table.shape[1] * PAGE_SIZE
    n_keys = past + t
    n_sel = min(TOPK_MAX, n_keys // 4)
    kidx_past = cache_idx[page_table].reshape(b, past, IDX_DIM)
    kidx_all = jnp.concatenate([kidx_past, k_idx_new], axis=1)
    q_pos = past + jnp.arange(t)
    sc = jnp.where(jnp.arange(n_keys)[None, None, :] <= q_pos[None, :, None],
                   index_scores(q_idx, w_idx, kidx_all), -jnp.inf)
    _, sel = lax.top_k(sc, n_sel)
    valid = sel <= q_pos[None, :, None]
    in_past = sel < past
    pidx = jnp.minimum(sel, past - 1)
    phys = jnp.take_along_axis(page_table, (pidx // PAGE_SIZE).reshape(b, -1), axis=1).reshape(sel.shape)
    rows_past = cache_kv[phys, pidx % PAGE_SIZE]
    rows_new = gather_rows(kv_new, jnp.clip(sel - past, 0, t - 1))
    kv_sel = jnp.where(in_past[..., None, None, None], rows_past, rows_new)
    return dsa_attend(q, q_pos, kv_sel[:, :, :, 0], kv_sel[:, :, :, 1], sel, valid, rel_bias)

def mixer_projections(h, pos, lw):
    b, t = h.shape[:2]
    split_at = np.cumsum(IN_SPLITS)[:-1].tolist()
    q_lat, kv_lat, k_rope, q, k, v, q_idx, k_idx, w_idx = jnp.split(h @ lw['w_in'], split_at, axis=-1)
    qm = jnp.einsum('btr,rhd->bthd', rms_norm(q_lat, lw['g_q_lat']), lw['w_uq'])
    q_nope = rms_norm(qm[..., :MLA_NOPE], lw['g_mla_q_nope'])
    q_rope = rope(rms_norm(qm[..., MLA_NOPE:], lw['g_mla_q_rope']), pos)
    lat = rms_norm(kv_lat, lw['g_kv_lat'])
    k_rope = rope(rms_norm(k_rope, lw['g_mla_k_rope']), pos)
    q = rms_norm(q.reshape(b, t, DSA_HEADS, DSA_HEAD_DIM), lw['g_dsa_q'])
    k = rms_norm(k.reshape(b, t, DSA_KV_HEADS, DSA_HEAD_DIM), lw['g_dsa_k'])
    v = v.reshape(b, t, DSA_KV_HEADS, DSA_HEAD_DIM)
    q_idx = q_idx.reshape(b, t, IDX_HEADS, IDX_DIM)
    kv = jnp.stack([k, v], axis=2)
    return (q_nope, q_rope, lat, k_rope), (q, kv, q_idx, w_idx, k_idx)

def merge_groups(o_mla, o_dsa, g_out, w_out):
    g_a, g_b = jnp.split(g_out, [MLA_HEADS * MLA_V])
    return jnp.concatenate([rms_norm(o_mla, g_a), rms_norm(o_dsa, g_b)], axis=-1) @ w_out

def swiglu(h, w_ffn_in, w_ffn_out):
    g, u = jnp.split(h @ w_ffn_in, 2, axis=-1)
    return (jax.nn.silu(g) * u) @ w_ffn_out

def decoder_layer(x, c, pos, attend, lw):
    mod = jax.nn.silu(c) @ lw['w_ada'] + lw['b_ada']
    shift_m, scale_m, gate_m, shift_f, scale_f, gate_f = jnp.split(mod[:, None, :], 6, axis=-1)
    h = rms_norm(x, lw['g_norm_mix']) * (1 + scale_m) + shift_m
    mla_t, dsa_t = mixer_projections(h, pos, lw)
    o_mla, o_dsa = attend(mla_t, dsa_t)
    x = x + gate_m * merge_groups(o_mla, o_dsa, lw['g_out'], lw['w_out'])
    h = rms_norm(x, lw['g_norm_ffn']) * (1 + scale_f) + shift_f
    x = x + gate_f * swiglu(h, lw['w_ffn_in'], lw['w_ffn_out'])
    rows = (jnp.concatenate([mla_t[2], mla_t[3]], axis=-1), dsa_t[1], dsa_t[4])
    return x, rows

def setup_inputs(seed: int = 0) -> dict:
    key = jax.random.key(seed)
    ks = iter(jax.random.split(key, 40))

    def nrm(shape, scale):
        return jax.random.normal(next(ks), shape, jnp.float32) * scale

    def gain(shape):
        return 1.0 + 0.05 * jax.random.normal(next(ks), shape, jnp.float32)

    n_pages = PAST_LEN // PAGE_SIZE
    n_used = DEC_BATCH * n_pages
    n_pool = n_used + max(1, n_used // 4)
    return {
        'x_prompt': nrm((BATCH, SEQ, D_MODEL), 1.0),
        'x_sample': nrm((DEC_BATCH, DEC_SEQ, D_MODEL), 1.0),
        'c_prompt': nrm((BATCH, D_MODEL), 1.0),
        'c_sample': nrm((DEC_BATCH, D_MODEL), 1.0),
        'cache_mla': nrm((DEPTH, n_pool, PAGE_SIZE, MLA_ROW), 1.0),
        'cache_kv': nrm((DEPTH, n_pool, PAGE_SIZE, 2, DSA_KV_HEADS, DSA_HEAD_DIM), 1.0),
        'cache_idx': nrm((DEPTH, n_pool, PAGE_SIZE, IDX_DIM), 1.0),
        'page_table': jax.random.permutation(next(ks), n_pool)[:n_used].reshape(DEC_BATCH, n_pages).astype(jnp.int32),
        'rel_bias': nrm((N_BUCKETS, DSA_HEADS), 0.5),
        'w_ada': nrm((DEPTH, D_MODEL, 6 * D_MODEL), 0.5 * D_MODEL ** -0.5),
        'b_ada': nrm((DEPTH, 6 * D_MODEL), 0.01),
        'g_norm_mix': gain((DEPTH, D_MODEL)),
        'g_norm_ffn': gain((DEPTH, D_MODEL)),
        'w_in': nrm((DEPTH, D_MODEL, D_IN), D_MODEL ** -0.5),
        'g_q_lat': gain((DEPTH, MLA_Q_RANK)),
        'w_uq': nrm((DEPTH, MLA_Q_RANK, MLA_HEADS, MLA_NOPE + MLA_ROPE), MLA_Q_RANK ** -0.5),
        'g_kv_lat': gain((DEPTH, MLA_KV_RANK)),
        'w_ukv': nrm((DEPTH, MLA_KV_RANK, MLA_HEADS, MLA_NOPE + MLA_V), MLA_KV_RANK ** -0.5),
        'g_mla_q_nope': gain((DEPTH, MLA_NOPE)),
        'g_mla_q_rope': gain((DEPTH, MLA_ROPE)),
        'g_mla_k_nope': gain((DEPTH, MLA_NOPE)),
        'g_mla_k_rope': gain((DEPTH, MLA_ROPE)),
        'g_dsa_q': gain((DEPTH, DSA_HEAD_DIM)),
        'g_dsa_k': gain((DEPTH, DSA_HEAD_DIM)),
        'g_out': gain((DEPTH, D_MIX)),
        'w_out': nrm((DEPTH, D_MIX, D_MODEL), D_MIX ** -0.5),
        'w_ffn_in': nrm((DEPTH, D_MODEL, 2 * D_FF), D_MODEL ** -0.5),
        'w_ffn_out': nrm((DEPTH, D_FF, D_MODEL), D_FF ** -0.5),
    }

def reference(x_prompt, x_sample, c_prompt, c_sample, cache_mla, cache_kv, cache_idx, page_table,
              rel_bias, w_ada, b_ada, g_norm_mix, g_norm_ffn, w_in, g_q_lat, w_uq, g_kv_lat, w_ukv,
              g_mla_q_nope, g_mla_q_rope, g_mla_k_nope, g_mla_k_rope, g_dsa_q, g_dsa_k, g_out, w_out,
              w_ffn_in, w_ffn_out):
    past_len = page_table.shape[1] * PAGE_SIZE
    pos_p = jnp.arange(x_prompt.shape[1])
    pos_s = past_len + jnp.arange(x_sample.shape[1])
    xp, xs = x_prompt, x_sample
    rows_p, rows_s = [], []
    for layer in range(DEPTH):
        lw = {
            'w_ada': w_ada[layer], 'b_ada': b_ada[layer],
            'g_norm_mix': g_norm_mix[layer], 'g_norm_ffn': g_norm_ffn[layer],
            'w_in': w_in[layer], 'g_q_lat': g_q_lat[layer], 'w_uq': w_uq[layer],
            'g_kv_lat': g_kv_lat[layer], 'w_ukv': w_ukv[layer],
            'g_mla_q_nope': g_mla_q_nope[layer], 'g_mla_q_rope': g_mla_q_rope[layer],
            'g_mla_k_nope': g_mla_k_nope[layer], 'g_mla_k_rope': g_mla_k_rope[layer],
            'g_dsa_q': g_dsa_q[layer], 'g_dsa_k': g_dsa_k[layer],
            'g_out': g_out[layer], 'w_out': w_out[layer],
            'w_ffn_in': w_ffn_in[layer], 'w_ffn_out': w_ffn_out[layer],
        }

        def attend_prompt(mla_t, dsa_t, lw=lw):
            q_nope, q_rope, lat, k_rope = mla_t
            q, kv, q_idx, w_idx, k_idx = dsa_t
            return (mla_prompt(q_nope, q_rope, lat, k_rope, lw['w_ukv'], lw['g_mla_k_nope']),
                    dsa_prompt(q, kv[:, :, 0], kv[:, :, 1], q_idx, w_idx, k_idx, rel_bias))

        def attend_sample(mla_t, dsa_t, lw=lw, layer=layer):
            q_nope, q_rope, lat, k_rope = mla_t
            q, kv, q_idx, w_idx, k_idx = dsa_t
            return (mla_sample(q_nope, q_rope, lat, k_rope, cache_mla[layer], page_table,
                               lw['w_ukv'], lw['g_mla_k_nope']),
                    dsa_sample(q, kv, q_idx, w_idx, k_idx, cache_kv[layer], cache_idx[layer],
                               page_table, rel_bias))

        xp, rp = decoder_layer(xp, c_prompt, pos_p, attend_prompt, lw)
        xs, rs = decoder_layer(xs, c_sample, pos_s, attend_sample, lw)
        rows_p.append(rp)
        rows_s.append(rs)
    new_mla_prompt = jnp.stack([r[0] for r in rows_p])
    new_kv_prompt = jnp.stack([r[1] for r in rows_p])
    new_idx_prompt = jnp.stack([r[2] for r in rows_p])
    new_mla_sample = jnp.stack([r[0] for r in rows_s])
    new_kv_sample = jnp.stack([r[1] for r in rows_s])
    new_idx_sample = jnp.stack([r[2] for r in rows_s])
    return (xp, xs, new_mla_prompt, new_kv_prompt, new_idx_prompt, new_mla_sample, new_kv_sample, new_idx_sample)


_drawn_inputs = setup_inputs


def setup_inputs(seed=0):
    import zlib

    import numpy as np

    out = dict(_drawn_inputs(seed))
    spreads = {}
    factors = {'g_norm_ffn': 3.88,
     'g_q_lat': 5.691,
     'g_mla_q_nope': 6.127,
     'g_mla_q_rope': 8.0,
     'g_mla_k_nope': 6.19,
     'g_mla_k_rope': 5.33,
     'g_dsa_q': 7.029,
     'g_out': 3.627}
    for name, (base, spread) in spreads.items():
        noise = np.random.default_rng([zlib.crc32(name.encode()), seed]).standard_normal(out[name].shape)
        drawn = base * np.exp(spread * noise) if base else spread * noise
        out[name] = jnp.asarray(drawn.astype(out[name].dtype))
    for name, factor in factors.items():
        out[name] = (out[name] * factor).astype(out[name].dtype)
    return out
```

```python
from contextlib import ExitStack

import numpy as np

import concourse.bass as bass
from concourse import mybir

F32 = mybir.dt.float32
I32 = mybir.dt.int32
ALU = mybir.AluOpType
ACT = mybir.ActivationFunctionType
AXX = mybir.AxisListType.X
RMAX = bass.bass_isa.ReduceOp.max
RADD = bass.bass_isa.ReduceOp.add

D, SEQ, NB, PAST, PAGE = 1024, 512, 8, 2048, 128
NPG = PAST // PAGE
H, NOPE, ROPE, VD = 8, 64, 32, 64
QK = NOPE + ROPE
QR, KVR = 384, 256
ROW = KVR + ROPE
HD, IDX = 64, 64
TOPK_P, TOPK_S = min(256, SEQ // 4), min(256, (PAST + 1) // 4)
NBUCK, MAXD = 32, 128
DFF = 2816
EPS = 1e-6
T = SEQ + NB
HT = T // 2
KD = D // 128
KF = DFF // 128
MLA_SCALE = float(QK) ** -0.5
DSA_SCALE = float(HD) ** -0.5
IDX_SCALE = float(IDX * 8) ** -0.5
NEG = -1e30
TAKEN = -3e38
C_KV, C_KR, C_Q, C_K, C_V, C_QI, C_KI, C_WI = 384, 640, 672, 1184, 1312, 1440, 1952, 2016
PER_TURN = 22
G_MIX, G_FFN, G_OUT, G_QL, G_KVL, G_Q, G_KN, G_KR, G_DQ, G_DK, N_GAIN = 0, 8, 16, 24, 27, 29, 30, 30, 31, 32, 33


def shape_constants():
    f = np.float32
    mats = np.zeros((6, 128, 128), f)
    mats[0] = np.eye(128)
    mats[1] = np.eye(128)[::-1]
    mats[2] = 1.0
    mats[3, :64, :64] = mats[3, 64:, 64:] = 1.0
    mats[4, :64, :64] = 1.0 / NOPE
    mats[4, 64:96, 64:96] = 1.0 / ROPE
    half = ROPE // 2
    for j in range(half):
        mats[5, 64 + half + j, 64 + j] = -1.0
        mats[5, 64 + j, 64 + half + j] = 1.0
    pos = np.concatenate([np.arange(SEQ), np.full(NB, PAST)]).astype(f)
    freq = (f(10000.0) ** (-np.arange(half, dtype=f) / f(half))).astype(f)
    ang = pos[None, :] * freq[:, None]
    rope = np.zeros((QK, 2, T), f)
    for r in range(ROPE):
        rope[NOPE + r, 0] = np.cos(ang[r % half])
        rope[NOPE + r, 1] = np.sin(ang[r % half])
    def bucket(d):
        d = np.maximum(d, 0)
        lr = np.log((np.maximum(d, 16).astype(f) / f(16)).astype(f)) / f(np.log(MAXD / 16))
        large = np.minimum(16 + (lr * f(16)).astype(np.int32), NBUCK - 1)
        return np.where(d < 16, d, large)
    near = bucket(255 - np.arange(384))
    far = bucket(PAST - np.arange(PAST + 1))
    onehot = (np.concatenate([near, far])[None, :] == np.arange(NBUCK)[:, None]).astype(f)
    cext = np.zeros((128, 512), f)
    cext[:, 384:] = np.where(np.arange(128)[None, :] <= np.arange(128)[:, None], 0.0, NEG)
    only = np.where(np.arange(128)[:, None] == np.arange(NB)[None, :], 0.0, NEG).astype(f)
    rows = np.arange(128)
    sel = np.zeros((128, 192), f)
    sel[rows, ((rows // 8) % 2) * 32 + rows // 16] = 1.0
    sel[rows, 64 + rows % 8] = 1.0

    r64 = np.arange(64)
    sel[r64, 72 + r64 // 8] = 1.0
    sel_b = (np.arange(NB)[:, None] == (rows // 16)[None, :]).astype(f)
    return {"k_sel": sel, "k_selb": sel_b, "k_mats": mats.transpose(1, 0, 2).copy(), "k_rope": rope, "k_onehot": onehot,
            "k_cext": cext, "k_only": only}


def units():
    u = [("qlat", 3, 128), ("v", 1, 128), ("kvlat", 2, 128), ("kidx", 1, 128), ("krope", 1, 96)]
    u += [(f"q{t}", 1, 128) for t in range(4)] + [("k", 1, 128)]
    u += [(f"qi{t}", 1, 128) for t in range(4)] + [("widx", 1, 8)]
    u += [(f"qc{h}", 1, QK) for h in range(H)] + [(f"kn{h}", 1, NOPE) for h in range(H)]
    return u


def kind(name):
    return name.rstrip("0123456789")


NORMED = {"qlat", "kvlat", "krope", "q", "k", "qc", "kn"}
ROPED = {"krope", "qc"}


def build(nc, a, o):
    U = units()
    stack = ExitStack()
    with stack as ctx:
        sb = lambda name, shape, dt=F32: ctx.enter_context(nc.sbuf_tensor(name, shape, dt))
        sems = {}

        def sem(name):
            if name not in sems:
                sems[name] = ctx.enter_context(nc.semaphore(name))
            return sems[name]

        xT = sb("xT", [128, KD, T])
        hT = sb("hT", [128, KD, T])
        wide = sb("wide", [128, 24, T])
        r1 = sb("r1", [128, 8320])
        qiz = sb("qiz", [128, 8, T])
        wring = sb("wring", [128, 5632])
        latT = sb("latT", [128, 2, T])
        kT = sb("kT", [128, T])
        vT = sb("vT", [128, T])
        kidxT = sb("kidxT", [128, T])
        krF = sb("krF", [QK, T])
        tok = sb("tok", [128, 5, 608])
        msk = sb("msk", [128, 1152])
        wukv = sb("wukv", [128, 2, H * 128])
        rope = sb("rope", [QK, 2, T])
        mats = sb("mats", [128, 6, 128])
        modT = sb("modT", [128, 48, 9])
        amod = sb("amod", [128, 2, 8, 9])
        gT = sb("gT", [128, N_GAIN])
        epsc = sb("epsc", [128, 1])
        cext = sb("cext", [128, 512])
        wtok = sb("wtok", [128, 5, 8])
        psA = ctx.enter_context(nc.psum_tensor("psA", [128, 2, 2, 512], F32))
        psV = ctx.enter_context(nc.psum_tensor("psV", [128, 2, 2, 512], F32))

        ident, flip, ones = mats[:, 0, :], mats[:, 1, :], mats[:, 2, :]
        block64, block96, rot96 = mats[:, 3, :], mats[0:QK, 4, 0:QK], mats[0:QK, 5, 0:QK]
        qcat, kcat, qz = wide[:, 0:8, :], wide[:, 8:16, :], wide[:, 16:24, :]
        wflat = wide[:].rearrange("p a t -> p (a t)")
        ada9, bada9 = wflat[0:9, 0:6144], wflat[0:9, 6144:12288]
        xtok = hT[:].rearrange("p a t -> p (a t)")[:, 0:4096].rearrange("p (t d) -> p t d", t=4)
        xs9 = qiz[:].rearrange("p a t -> p (a t)")
        xsam, cin, csil, gin = xs9[0:8, 0:1024], xs9[0:9, 1024:2048], xs9[0:9, 2048:3072], xs9[0:N_GAIN, 3072:3200]
        cT = r1[:, 8000:8072].rearrange("p (k c) -> p k c", k=8)
        sqx = r1[:, 0:KD * T].rearrange("p (k t) -> p k t", k=KD)
        sq = r1[:, 0:4 * T].rearrange("p (k t) -> p k t", k=4)
        raw = r1[:, 4 * T:6 * T].rearrange("p (k t) -> p k t", k=2)
        sd = r1[:, 8 * T:10 * T].rearrange("p (k t) -> p k t", k=2)
        wuq = r1[:, 10 * T:10 * T + 2304].rearrange("p (k n) -> p k n", k=3)

        qlatT = wflat[:, 8 * T:11 * T].rearrange("p (k t) -> p k t", k=3)
        rtmp = r1[:, 6 * T:7 * T]
        halves = lambda ap: ap.rearrange("p (h t) -> p h t", h=2)

        nA = 0
        A_XT = [nA + i for i in range(7)]; nA += 7
        A_MOD = nA; nA += 1
        A_SS = nA; nA += 1
        A_proj, A_norm, V_rot = {}, {}, {}
        nV = 24
        for i in range(len(U) + 2):
            if i < len(U):
                A_proj[i] = [nA + t for t in range(U[i][1])]
                nA += U[i][1]
            if 1 <= i <= len(U) and kind(U[i - 1][0]) in NORMED:
                A_norm[i - 1] = nA; nA += 1
            if i >= 2 and kind(U[i - 2][0]) in ROPED:
                V_rot[i - 2] = nV; nV += 1
        A_TOK = nA; nA += 5
        A_WT = nA; nA += 1
        IQ = [(qt, h) for qt in range(1, 4) for h in range(H)]
        A_IQ = nA; nA += len(IQ)
        V_BIAS = nV; nV += 3
        A_VM = nA; nA += 4
        A_QS = nA; nA += 1
        V_KN = nV; nV += 1
        V_WC = nV; nV += 2
        A_IP = nA; nA += 16
        V_IS = nV; nV += 1
        V_ISW = nV; nV += 1
        AT = [(g, qt, h) for g in range(2) for qt in range(4) for h in range(H)]
        A_PT, V_S = nA, nV
        nA += len(AT); nV += len(AT)
        V_BF = nV; nV += 3
        A_LT, V_KX = nA, nV
        nA += NB * NPG; nV += NB * NPG
        A_OL = nA; nA += 1
        V_OV = nV; nV += 1
        A_KD, V_SD = nA, nV
        nA += 4 * NB; nV += 4
        V_SN = nV; nV += 1
        A_PD = nA; nA += 3
        A_OD = nA; nA += 1
        A_MIX = nA; nA += 2
        V_OUT = nV; nV += 8
        A_SS2 = nA; nA += 1
        PADA, PADV = nA % 2, nV % 2
        nA += PADA; nV += PADV
        A_G, V_U = nA, nV
        nA += KF; nV += KF
        V_DN = nV; nV += 8
        A_Y = nA; nA += 5
        win_tiles = [(i, t) for i in range(15) for t in range(U[i][1])]

        rb = r1[:, 0:1024].rearrange("p (s n) -> p s n", s=2)
        vm = r1[:, 1024:3072].rearrange("p (t n) -> p t n", t=4)
        sS = r1[:, 3072:4608].rearrange("p (s n) -> p s n", s=3)
        sP = r1[:, 4608:6144].rearrange("p (s n) -> p s n", s=3)
        sPT = r1[:, 6144:7680].rearrange("p (s n) -> p s n", s=3)
        ohn, g8, rbias = r1[0:32, 3072:3456], r1[0:8, 3456:3840], r1[0:32, 3840:3848]
        stat = sb("stat", [128, 3, 4])
        gated = sb("gated", [128, 2, 8])
        top8 = sb("top8", [128, 8])
        trev, toep = wring[:, 0:2048], wring[:, 2050:4098]
        sc8 = wring[0:NB, 0:PAST + 1]
        ip = r1[:, 4096:5120].rearrange("p (s n) -> p s n", s=2)
        kiT = r1[:, 5120:6144].rearrange("p (s n) -> p s n", s=2)
        irel = r1[:, 6144:7168]
        w1 = r1[:, 7168:8320]
        sel = sb("sel", [128, 192])
        selb = sb("selb", [NB, 128])
        ptab = sb("ptab", [1, NB * NPG], I32)
        wz = sb("wz", [128, 64])
        small = sb("small", [128, 64])
        rb64 = sb("rb64", [NBUCK, 64])
        qd = sb("qd", [128, 64])
        qdz = sb("qdz", [128, 576])
        ropeflat = rope[:].rearrange("p a t -> p (a t)")
        knew, pnsq = ropeflat[0:NB, 0:512], ropeflat[0:NB, 512:1024]
        ssnew = sb("ssnew", [NB, 8])
        qflat = qiz[:].rearrange("p a t -> p (a t)")
        bm64, s64, ohf = qflat[0:64, 0:2049], qflat[0:64, 2049:4098], qflat[0:32, 2049:4098]
        qs8 = r1[0:NB, 3072:3840]
        qbc = r1[:, 0:6144].rearrange("p (b h d) -> p b h d", b=NB, h=H)
        rp = r1[:, 6144:8192].rearrange("p (s j h d) -> p s j h d", s=2, j=4, h=H)
        pgs = wflat[:, 0:9216].rearrange("p (s j n) -> p s j n", s=2, j=NPG)
        lT = wflat[:, 9216:9728].rearrange("p (s k n) -> p s k n", s=2, k=2)
        pr = wflat[:, 9728:10752].rearrange("p (s n) -> p s n", s=2)
        sqk = wflat[:, 10752:11776].rearrange("p (s n) -> p s n", s=2)
        ol = wflat[0:8, 11776:12288]
        m8 = lambda x: msk[:, x * 136:(x + 1) * 136].rearrange("p (j h) -> p j h", h=8)
        dots, sums, sfull, pm = [m8(0), m8(1)], [m8(2), m8(3)], [m8(4), m8(5)], [m8(6), m8(7)]
        newp = krF[0:NB, 0:512].rearrange("p (h d) -> p h d", h=H)
        onlyc = sb("onlyc", [128, NB])
        drope = [vT[:, x * 136:(x + 1) * 136].rearrange("p (j h) -> p j h", h=8) for x in range(2)]
        hstat = sb("hstat", [128, 4, 8])
        kp = wring[:, 2048:3072].rearrange("p (s j n) -> p s j n", s=2, j=4)
        kdT = wring[:, 3072:4096].rearrange("p (s n) -> p s n", s=2)
        ptd = wring[:, 4096:5184].rearrange("p (j r) -> p j r", j=17)
        ptb = wring[:, 5184:5456].rearrange("p (s j h) -> p s j h", s=2, j=17)
        olb = r1[0:8, 0:2048].rearrange("p (b r) -> p b r", b=NB)
        olT = wflat[:, 11776:11904].rearrange("p (k r) -> p k r", k=2)
        vp = wflat[:, 0:4096].rearrange("p (s j n) -> p s j n", s=2, j=NPG)
        od = wflat[0:8, 4096:5120].rearrange("p (b n) -> p b n", b=NB)
        odT = wflat[:, 5120:5184].rearrange("p (b h) -> p b h", b=NB)
        q_rows = nc.dram_tensor("q_rows", [NB, 768], F32, kind="Internal").ap()
        mask_rows = nc.dram_tensor("mask_rows", [NB, PAST + 1], F32, kind="Internal").ap()
        toepv = toep.rearrange("p (h n) -> p h n", h=H)
        mixT = hT
        bias_rows = nc.dram_tensor("bias_rows", [8, 384], F32, kind="Internal").ap()
        MQ = {1: (0, 256), 2: (256, 640), 3: (640, 1152)}
        actT = wide[:, 0:KF, :]
        yt = hT[:].rearrange("p a t -> p (a t)")[:, 0:2048].rearrange("p (s n) -> p s n", s=2)

        sa = lambda n: psA[:, n % 2]
        sv = lambda n: psV[:, n % 2]
        a_full, a_free, v_full, v_free = sem("a_full"), sem("a_free"), sem("v_full"), sem("v_free")
        in_loaded, const_loaded, bada_loaded, wres_loaded = sem("in_loaded"), sem("const_loaded"), sem("bada_loaded"), sem("wres_loaded")
        ada_w = [sem(f"ada_w{s}") for s in range(2)]
        win_w = [sem(f"win_w{s}") for s in range(4)]
        c_silu, eps_set, amod_done, hT_scaled, hT_done = sem("c_silu"), sem("eps_set"), sem("amod_done"), sem("hT_scaled"), sem("hT_done")
        zeroed, norm_done, rope_done, dve_chain, act_chain = sem("zeroed"), sem("norm_done"), sem("rope_done"), sem("dve_chain"), sem("act_chain")
        kr_spread, tokens_stored = sem("kr_spread"), sem("tokens_stored")
        sq_written = sem("sq_written")
        idx_acc, bias_loaded, bias_out, trev_loaded, toep_done = sem("idx_acc"), sem("bias_loaded"), sem("bias_out"), sem("trev_loaded"), sem("toep_done")
        mask_done, stats_ready, exp_done, p_ready, pv_done, o_free = (sem(x) for x in ("mask_done", "stats_ready", "exp_done", "p_ready", "pv_done", "o_free"))
        mixed, sq2_written, x_new, h2_scaled, h2_done = (sem(x) for x in ("mixed", "sq2_written", "x_new", "h2_scaled", "h2_done"))
        y_stored = [sem(f"y_stored{s}") for s in range(2)]
        ptab_loaded, qs_gained, qs_out, qbc_loaded, w1_ready, irel_ready, wz_ready, pn_ready = (sem(x) for x in (
            "ptab_loaded", "qs_gained", "qs_out", "qbc_loaded", "w1_ready", "irel_ready", "wz_ready", "pn_ready"))
        far_loaded, mask_out, mask_back, top_done, bm_ready = (sem(x) for x in ("far_loaded", "mask_out", "mask_back", "top_done", "bm_ready"))
        idx_pages = [sem(f"idx_pages{x}") for x in range(2)]
        mla_pages = [sem(f"mla_pages{x}") for x in range(2)]
        k_pages = [sem(f"k_pages{x}") for x in range(2)]
        v_pages = [sem(f"v_pages{x}") for x in range(2)]
        squared, page_sums, rope_mul, rope_sum, ss_ready, rstd_in = (sem(x) for x in ("squared", "page_sums", "rope_mul", "rope_sum", "ss_ready", "rstd_in"))
        smax, gmax, shifted, p_exp, psum_ready, gsum, pm_ready = (sem(x) for x in ("smax", "gmax", "shifted", "p_exp", "psum_ready", "gsum", "pm_ready"))
        lat_pv, lat_out, s64_ready, p64_exp, p64_ready, ptb_ready, d_pv, d_out = (sem(x) for x in (
            "lat_pv", "lat_out", "s64_ready", "p64_exp", "p64_ready", "ptb_ready", "d_pv", "d_out"))
        mix_s, neg_set, new_sums = sem("mix_s"), sem("neg_set"), sem("new_sums")
        out_w = [sem(f"out_w{s}") for s in range(2)]
        fin_w = [sem(f"fin_w{s}") for s in range(2)]
        fout_w = [sem(f"fout_w{s}") for s in range(2)]
        normed = [i for i in range(len(U)) if kind(U[i][0]) in NORMED]
        roped = [i for i in range(len(U)) if kind(U[i][0]) in ROPED]
        UI = {U[i][0]: i for i in range(len(U))}

        def gain_col(name, t):
            k = kind(name)
            c = {"qlat": G_QL + t, "kvlat": G_KVL + t, "krope": G_KR, "q": G_DQ, "k": G_DK, "qc": G_Q, "kn": G_KN}[k]
            return c

        def sp_program(sp):
            for t in range(4):
                sp.dma_start(xtok[:, t, :], a["x_prompt"][0, t * 128:(t + 1) * 128, :]).then_inc(in_loaded, 16)
            sp.dma_start(xsam, a["x_sample"][:, 0, :]).then_inc(in_loaded, 16)
            sp.dma_start(cin[0:1, :], a["c_prompt"]).then_inc(in_loaded, 16)
            sp.dma_start(cin[1:9, :], a["c_sample"]).then_inc(in_loaded, 16)
            sp.wait_ge(eps_set, 1)
            row = lambda name: a[name].rearrange("l (k n) -> (l k) n", n=128)
            for c, name, n in ((G_MIX, "g_norm_mix", 8), (G_FFN, "g_norm_ffn", 8), (G_OUT, "g_out", 8),
                               (G_QL, "g_q_lat", 3), (G_KVL, "g_kv_lat", 2)):
                sp.dma_start(gin[c:c + n, :], row(name)).then_inc(in_loaded, 16)
            for c, o0, name in ((G_Q, 0, "g_mla_q_nope"), (G_Q, 64, "g_mla_q_rope"), (G_KN, 0, "g_mla_k_nope"),
                                (G_KN, 64, "g_mla_k_rope"), (G_DQ, 0, "g_dsa_q"), (G_DQ, 64, "g_dsa_q"),
                                (G_DK, 0, "g_dsa_k"), (G_DK, 64, "g_dsa_k")):
                n = a[name].shape[1]
                sp.dma_start(gin[c:c + 1, o0:o0 + n], a[name]).then_inc(in_loaded, 16)
            sp.dma_start(mats[:], a["k_mats"]).then_inc(in_loaded, 16)
            sp.dma_start(bada9, a["b_ada"].broadcast_to([9, 6144])).then_inc(bada_loaded, 16)
            wada = a["w_ada"][0].rearrange("(k p) n -> p k n", p=128)
            aslot = lambda s: wring[:, s * 2048:(s + 1) * 2048].rearrange("p (k n) -> p k n", k=KD)
            for s in range(2):
                sp.dma_start(aslot(s), wada[:, :, s * 256:(s + 1) * 256]).then_inc(ada_w[s], 16)
            sp.dma_start(rope[:], a["k_rope"]).then_inc(const_loaded, 16)
            sp.dma_start(cext[:], a["k_cext"]).then_inc(const_loaded, 16)
            sp.dma_start(sel[:], a["k_sel"]).then_inc(const_loaded, 16)
            sp.dma_start(selb[:], a["k_selb"]).then_inc(const_loaded, 16)
            sp.dma_start(onlyc[:], a["k_only"]).then_inc(const_loaded, 16)
            sp.dma_start(ptab[:], a["page_table"].rearrange("(o b) j -> o (b j)", o=1)).then_inc(ptab_loaded, 16)
            with sp.Fori(1, 12) as i:
                for s in range(2):
                    sp.wait_ge(v_full, i * 2 + (s - 1))
                    sp.dma_start(aslot(s), wada[:, :, bass.ds(i * 512 + s * 256, 256)]).then_inc(ada_w[s], 16)
            sp.wait_ge(a_full, A_SS + 1)
            sp.dma_start(wuq, a["w_uq"][0].rearrange("(k p) h d -> p k (h d)", p=128)).then_inc(wres_loaded, 16)
            sp.dma_start(wukv[:], a["w_ukv"][0].rearrange("(k p) h d -> p k (h d)", p=128)).then_inc(wres_loaded, 16)
            win = a["w_in"][0].rearrange("(k p) n -> p k n", p=128)
            sp.wait_ge(v_full, 24)
            for n, (i, t) in enumerate(win_tiles):
                if n >= 4:
                    pi, pt = win_tiles[n - 4]
                    sp.wait_ge(a_full, A_proj[pi][pt] + 1)
                dst = wring[:, (n % 4) * 1024:(n % 4 + 1) * 1024].rearrange("p (k n) -> p k n", k=KD)
                name = U[i][0]
                k = kind(name)
                j = int(name[-1]) if name[-1].isdigit() else 0
                if k == "q":
                    parts = [(0, C_Q + j * 64, 64), (64, C_Q + (j + 4) * 64, 64)]
                elif k == "kidx":
                    parts = [(0, C_KI, 64), (64, C_KI, 64)]
                else:
                    c = {"qlat": t * 128, "v": C_V, "kvlat": C_KV + t * 128, "krope": C_KR - 64, "k": C_K,
                         "qi": C_QI + j * 128, "widx": C_WI}[k]
                    parts = [(0, c, U[i][2])]
                for d0, c0, w in parts:
                    for kk in range(0, KD, 4):
                        sp.dma_start(dst[:, kk:kk + 4, d0:d0 + w], win[:, kk:kk + 4, c0:c0 + w]).then_inc(win_w[n % 4], 16)

            sp.wait_ge(norm_done, len(normed))
            sp.wait_ge(a_free, A_WT + 1)
            sp.dma_start(ohn, a["k_onehot"][:, 0:384]).then_inc(bias_loaded, 16)
            sp.dma_start(rbias, a["rel_bias"]).then_inc(bias_loaded, 16)
            sp.wait_ge(v_free, V_BIAS + 1)
            sp.dma_start(bias_rows, g8).then_inc(bias_out, 16)
            sp.wait_ge(bias_out, 16)
            sp.dma_start(trev.rearrange("p (h n) -> p h n", h=H),
                         bass.AP(bias_rows.tensor, 0, [[1, 128], [384, 8], [1, 256]])).then_inc(trev_loaded, 16)
            sp_decode(sp)
            self_sp_tail(sp)

        class Link:

            def __init__(self, v):
                self.v, self.n, self.turn = v, 0, None

            def __call__(self, ins):
                self.n += 1
                ins.then_inc(dve_chain, 1)
                self.v.wait_ge(dve_chain, self.n if self.turn is None else self.turn * PER_TURN + self.n)

            def per_loop(self, i, start, body):
                first = self.n
                self.turn, self.n = i, first - start * PER_TURN
                body()
                assert self.n - (first - start * PER_TURN) == PER_TURN, self.n - (first - start * PER_TURN)
                self.first = first

            def after_loop(self, turns=3):
                self.turn, self.n = None, self.first + turns * PER_TURN

        def at(b, k, c):
            if isinstance(b, tuple):
                return b[0] * (2 * k) + (b[1] * k + c)
            return b * k + c

        def sp_decode(sp):
            sp.wait_ge(ptab_loaded, 16)

            def page(b, j):
                i = at(b, NPG, j)
                cell = ptab[0:1, bass.ds(i, 1)] if isinstance(b, tuple) else ptab[0:1, i:i + 1]
                return sp.value_load(cell, min_val=0, max_val=a["cache_idx"].shape[1] - 1)

            cidx = a["cache_idx"][0].rearrange("n (p two) d -> n p (two d)", two=2)

            def idx_group(b, par, half, need=None):
                if need is not None:
                    sp.wait_ge(a_full, need)
                for x in range(8):
                    dst = ip[(x % 2) * 64:(x % 2) * 64 + 64, par, (x // 2) * 128:(x // 2 + 1) * 128]
                    sp.dma_start(dst, cidx[bass.ds(page(b, half * 8 + x), 1)].rearrange("n p d -> (n p) d")).then_inc(idx_pages[par], 16)

            sp.wait_ge(a_full, A_QS + 1)
            for half in range(2):
                if half == 0:
                    idx_group(0, 0, 0)
                    idx_group(1, 1, 0)
                with sp.Fori(1 - half, 4) as i:
                    for par in range(2):
                        idx_group((i, par), par, half, i * 2 + (A_IP + 8 * half + par - 1))
            sp.wait_ge(a_free, A_QS + 1)
            sp.dma_start(q_rows, qs8).then_inc(qs_out, 16)
            sp.dma_start(ohf, a["k_onehot"][:, 384:384 + PAST + 1]).then_inc(far_loaded, 16)
            sp.wait_ge(qs_out, 16)
            sp.wait_ge(o_free, len(AT) // 2)
            sp.wait_ge(p_ready, len(AT))
            sp.dma_start(qbc.rearrange("p b h d -> p (b h d)"),
                         bass.AP(q_rows.tensor, 0, [[0, 128], [1, NB * 768]])).then_inc(qbc_loaded, 16)

            def mla_group(b, par, need=None):
                if need is not None:
                    sp.wait_ge(lat_pv, need)
                for j in range(NPG):
                    sp.dma_start(pgs[:, par, j, :], a["cache_mla"][0][bass.ds(page(b, j), 1)].rearrange("n p d -> (n p) d")
                                 ).then_inc(mla_pages[par], 16)

            mla_group(0, 0)
            mla_group(1, 1)
            sp.wait_ge(top_done, 1)
            sp.dma_start(mask_rows, sc8).then_inc(mask_out, 16)
            sp.wait_ge(mask_out, 16)
            sp.wait_ge(v_free, V_BF + 3)
            sp.dma_start(s64, bass.AP(mask_rows.tensor, 0, [[PAST + 1, NB], [0, 8], [1, PAST + 1]])).then_inc(mask_back, 16)
            with sp.Fori(1, 4) as i:
                for par in range(2):
                    mla_group((i, par), par, i * 2 + (par - 1))
            ckv = a["cache_kv"][0].rearrange("n p a c d -> n p (a c d)")

            def k_group(c4, b, par, need=None):
                if need is not None:
                    sp.wait_ge(a_full, need)
                for x in range(4):
                    pg = page(b, c4 * 4 + x)
                    sp.dma_start(kp[:, par, x, :], ckv[bass.ds(pg, 1), :, 0:128].rearrange("n p d -> (n p) d")).then_inc(k_pages[par], 16)

            for c4 in range(4):
                if c4 == 0:
                    k_group(0, 0, 0)
                    k_group(0, 1, 1)
                with sp.Fori(1 if c4 == 0 else 0, 4) as i:
                    for par in range(2):
                        k_group(c4, (i, par), par, i * 2 + (A_KD + 8 * c4 + par - 1))

            def v_group(b, par, need=None):
                if need is not None:
                    sp.wait_ge(d_pv, need)
                for j in range(NPG):
                    sp.dma_start(vp[:, par, j, :], ckv[bass.ds(page(b, j), 1), :, 128:256].rearrange("n p d -> (n p) d")).then_inc(v_pages[par], 16)

            sp.wait_ge(lat_pv, NB)
            v_group(0, 0)
            v_group(1, 1)
            with sp.Fori(1, 4) as i:
                for par in range(2):
                    v_group((i, par), par, i * 2 + (par - 1))

        def self_sp_tail(sp):
            wo = a["w_out"][0].rearrange("(k p) n -> p k n", p=128)
            oslot = lambda s: wring[:, s * 1024:(s + 1) * 1024].rearrange("p (k n) -> p k n", k=KD)
            sp.wait_ge(p_ready, len(AT))
            for s in range(2):
                sp.dma_start(oslot(s), wo[:, :, s * 128:(s + 1) * 128]).then_inc(out_w[s], 16)
            with sp.Fori(1, 4) as i:
                for s in range(2):
                    sp.wait_ge(v_full, i * 2 + (V_OUT + s - 1))
                    sp.dma_start(oslot(s), wo[:, :, bass.ds(i * 256 + s * 128, 128)]).then_inc(out_w[s], 16)
            wf = a["w_ffn_in"][0].rearrange("(k p) n -> p k n", p=128)
            fslot = lambda s, c: wring[:, s * 2048 + c * 1024:s * 2048 + (c + 1) * 1024].rearrange("p (k n) -> p k n", k=KD)
            sp.wait_ge(v_full, V_OUT + 8)
            for s in range(2):
                for c in range(2):
                    sp.dma_start(fslot(s, c), wf[:, :, c * DFF + s * 128:c * DFF + (s + 1) * 128]).then_inc(fin_w[s], 16)
            with sp.Fori(1, KF // 2) as i:
                for s in range(2):
                    sp.wait_ge(v_full, i * 2 + (V_U + s - 1))
                    for c in range(2):
                        sp.dma_start(fslot(s, c), wf[:, :, bass.ds(i * 256 + (c * DFF + s * 128), 128)]).then_inc(fin_w[s], 16)
            wd = a["w_ffn_out"][0].rearrange("(k p) n -> p k n", p=128)
            dslot = lambda s: wring[:, s * 2816:(s + 1) * 2816].rearrange("p (k n) -> p k n", k=KF)
            sp.wait_ge(v_full, V_U + KF)
            for s in range(2):
                sp.dma_start(dslot(s), wd[:, :, s * 128:(s + 1) * 128]).then_inc(fout_w[s], 16)
            with sp.Fori(1, 4) as i:
                for s in range(2):
                    sp.wait_ge(v_full, i * 2 + (V_DN + s - 1))
                    sp.dma_start(dslot(s), wd[:, :, bass.ds(i * 256 + s * 128, 128)]).then_inc(fout_w[s], 16)
            for t in range(5):
                w = 128 if t < 4 else NB
                sp.wait_ge(a_free, A_Y + t + 1)
                dst = o["y_p"][0, t * 128:(t + 1) * 128, :] if t < 4 else o["y_s"][:, 0, :]
                sp.dma_start(dst, yt[0:w, t % 2, :]).then_inc(y_stored[t % 2], 16)
            sp.wait_ge(y_stored[0], 48)
            sp.wait_ge(y_stored[1], 32)

        def win_count(n):
            c = 0
            for m in range(n % 4, n + 1, 4):
                k = kind(U[win_tiles[m][0]][0])
                c += 4 if k in ("q", "kidx") else 2
            return 16 * c

        def pe_program(pe):
            def sumsq(job, src, need, count):
                if job >= 2:
                    pe.wait_ge(a_free, job - 1)
                pe.wait_ge(need, count)
                for hf in range(2):
                    for k in range(KD):
                        mm = pe.matmul(sa(job)[:, hf, 0:HT], ones, src[:, k, hf * HT:(hf + 1) * HT],
                                       start=(k == 0), stop=(k == KD - 1))
                mm.then_inc(a_full, 1)

            pe.wait_ge(in_loaded, 16 * 21)
            for j, n in enumerate(A_XT):
                if n >= 2:
                    pe.wait_ge(a_free, n - 1)
                out = sa(n).rearrange("p b n -> p (b n)")
                if j < 4:
                    for k in range(KD):
                        mm = pe.transpose(out[:, k * 128:(k + 1) * 128], xtok[:, j, k * 128:(k + 1) * 128], ident)
                elif j == 4:
                    for k in range(KD):
                        mm = pe.transpose(out[:, k * 8:k * 8 + 8], xsam[:, k * 128:(k + 1) * 128], ident[0:8, 0:8])
                elif j == 5:
                    pe.wait_ge(c_silu, 1)
                    for k in range(KD):
                        mm = pe.transpose(out[:, k * 9:k * 9 + 9], csil[:, k * 128:(k + 1) * 128], ident[0:9, 0:9])
                else:
                    mm = pe.transpose(out[:, 0:N_GAIN], gin, ident[0:N_GAIN, 0:N_GAIN])
                mm.then_inc(a_full, 1)
            pe.wait_ge(a_free, A_XT[5] + 1)

            def ada_chunk(s, loads, n=None):
                pe.wait_ge(ada_w[s], loads)
                if n is not None:
                    pe.wait_ge(v_free, n)
                w = wring[:, s * 2048:(s + 1) * 2048].rearrange("p (k n) -> p k n", k=KD)
                for k in range(KD):
                    mm = pe.matmul(psV[0:9, s, 0, 0:256], cT[:, k, :], w[:, k, :], start=(k == 0), stop=(k == KD - 1))
                mm.then_inc(v_full, 1)

            ada_chunk(0, 16)
            ada_chunk(1, 16)
            with pe.Fori(1, 12) as i:
                for s in range(2):
                    ada_chunk(s, i * 16 + 16, i * 2 + (s - 1))
            pe.wait_ge(a_free, A_MOD - 1)
            pe.wait_ge(v_free, 24)
            for m in range(48):
                mm = pe.transpose(sa(A_MOD)[:, 0, m * 9:m * 9 + 9], ada9[:, m * 128:(m + 1) * 128], ident[0:9, 0:9])
            mm.then_inc(a_full, 1)
            sumsq(A_SS, sqx, sq_written, 8)

            pe.wait_ge(hT_done, 9)
            wn = 0
            for i in range(len(U) + 2):
                if i < len(U):
                    name, nt, rows = U[i]
                    k = kind(name)
                    j = int(name[-1]) if name[-1].isdigit() else 0
                    for t in range(nt):
                        n = A_proj[i][t]
                        pe.wait_ge(a_free, n - 1)
                        if i < 15:
                            pe.wait_ge(win_w[wn % 4], win_count(wn))
                            w = wring[:, (wn % 4) * 1024:(wn % 4 + 1) * 1024].rearrange("p (k n) -> p k n", k=KD)
                            wn += 1
                            src, nk = hT, KD
                            lhs = lambda kk: w[:, kk, 0:rows]
                        elif k == "qc":
                            pe.wait_ge(wres_loaded, 32)
                            pe.wait_ge(norm_done, normed.index(UI["qlat"]) + 1)
                            src, nk = qlatT, 3
                            lhs = lambda kk: wuq[:, kk, j * QK:(j + 1) * QK]
                        else:
                            pe.wait_ge(norm_done, normed.index(UI["kvlat"]) + 1)
                            src, nk = latT, 2
                            lhs = lambda kk: wukv[:, kk, j * 128:j * 128 + 64]
                        for kk in range(nk):
                            for hf in range(2):
                                mm = pe.matmul(sa(n)[0:rows, hf, 0:HT], lhs(kk), src[:, kk, hf * HT:(hf + 1) * HT],
                                               start=(kk == 0), stop=(kk == nk - 1), skip_group_check=True)
                        mm.then_inc(a_full, 1)
                if i - 1 in A_norm:
                    name, nt, rows = U[i - 1]
                    k = kind(name)
                    n = A_norm[i - 1]
                    pe.wait_ge(a_free, max(n - 1, A_proj[i - 1][-1] + 1))
                    blk = {"qlat": ones, "kvlat": ones, "krope": block96, "qc": block96, "q": block64, "k": block64,
                           "kn": block96[0:64, 0:64]}[k]
                    for hf in range(2):
                        for t in range(nt):
                            s = SQ[i - 1] + t
                            mm = pe.matmul(sa(n)[0:rows, hf, 0:HT], blk, sq[0:rows, s % 4, hf * HT:(hf + 1) * HT],
                                           start=(t == 0), stop=(t == nt - 1))
                    mm.then_inc(a_full, 1)
                if i - 2 in V_rot:
                    n = V_rot[i - 2]
                    pe.wait_ge(v_free, n - 1)
                    pe.wait_ge(norm_done, normed.index(i - 2) + 1)
                    src = krF[:] if U[i - 2][0] == "krope" else qcat[0:QK, int(U[i - 2][0][-1]), :]
                    for hf in range(2):
                        mm = pe.matmul(sv(n)[0:QK, hf, 0:HT], rot96, src[:, hf * HT:(hf + 1) * HT], start=True, stop=True)
                    mm.then_inc(v_full, 1)
            pe.wait_ge(rope_done, 1)
            pe.wait_ge(norm_done, len(normed))
            for t in range(5):
                n = A_TOK + t
                pe.wait_ge(a_free, n - 1)
                c, w = t * 128, (128 if t < 4 else NB)
                for k in range(2):
                    pe.transpose(sa(n)[0:w, 0, k * 128:(k + 1) * 128], latT[:, k, c:c + w], ident)
                pe.transpose(sa(n)[0:w, 0, 256:256 + QK], krF[:, c:c + w], ident[0:QK, 0:QK])
                for j, src in enumerate((kT, vT, kidxT)):
                    mm = pe.transpose(sa(n)[0:w, 1, j * 128:(j + 1) * 128], src[:, c:c + w], ident)
                mm.then_inc(a_full, 1)
            n = A_WT
            pe.wait_ge(a_free, n - 1)
            for t in range(5):
                w = 128 if t < 4 else NB
                mm = pe.transpose(sa(n)[0:w, 0, t * 8:t * 8 + 8], widxT[:, t * 128:t * 128 + w], ident[0:8, 0:8])
            mm.then_inc(a_full, 1)

            for j, (qt, h) in enumerate(IQ):
                n = A_IQ + j
                pe.wait_ge(a_free, n - 1)
                mm = pe.matmul(sa(n)[:, 0, 0:(qt + 1) * 128], qiz[:, h, qt * 128:(qt + 1) * 128],
                               kidxT[:, 0:(qt + 1) * 128], start=True, stop=True)
                mm.then_inc(a_full, 1)
            pe.wait_ge(bias_loaded, 32)
            pe.wait_ge(v_free, V_BIAS - 1)
            pe.matmul(sv(V_BIAS)[0:8, 0, 0:384], rbias, ohn, start=True, stop=True).then_inc(v_full, 1)
            for t in range(4):
                n = A_VM + t
                pe.wait_ge(a_free, n - 1)
                for k in range(2):
                    mm = pe.matmul(sa(n)[:, 0, :], latT[:, k, t * 128:(t + 1) * 128],
                                   wukv[:, k, :].rearrange("p (h d) -> p h d", h=H)[:, :, 64:128], start=(k == 0), stop=(k == 1))
                mm.then_inc(a_full, 1)
            pe.wait_ge(trev_loaded, 16)
            for j in range(2):
                n = V_BIAS + 1 + j
                pe.wait_ge(v_free, n - 1)
                for b in range(2):
                    c = j * 1024 + b * 512
                    mm = pe.matmul(sv(n)[:, b, :], flip, trev[:, c:c + 512], start=True, stop=True)
                mm.then_inc(v_full, 1)
            pe.wait_ge(kr_spread, 1)
            pe.wait_ge(rope_done, len(roped))
            n = A_QS
            pe.wait_ge(a_free, n - 1)
            pe.wait_ge(qs_gained, 1)
            for h in range(H):
                mm = pe.transpose(sa(n)[0:NB, h // 4, (h % 4) * QK:(h % 4 + 1) * QK], qcat[0:QK, h, SEQ:T], ident[0:QK, 0:QK])
            mm.then_inc(a_full, 1)
            pe.wait_ge(v_free, V_KN - 1)
            for k in range(2):
                mm = pe.matmul(sv(V_KN)[0:NB, 0, :], latT[:, k, SEQ:T],
                               wukv[:, k, :].rearrange("p (h d) -> p h d", h=H)[:, :, 0:64], start=(k == 0), stop=(k == 1))
            mm.then_inc(v_full, 1)
            pe.wait_ge(const_loaded, 80)
            pe.wait_ge(v_free, V_WC - 1)
            pe.matmul(sv(V_WC)[:, 0, 0:8], selb[:], wtok[0:NB, 4, :], start=True, stop=True).then_inc(v_full, 1)
            pe.wait_ge(v_free, V_WC)
            pe.wait_ge(pn_ready, 1)
            for h in range(H):
                mm = pe.matmul(sv(V_WC + 1)[0:NB, 0, h:h + 1], irel[:, h * 8:h * 8 + 8], ones[:, 0:1], start=True, stop=True,
                               skip_group_check=True)
            mm.then_inc(v_full, 1)
            pe.wait_ge(w1_ready, 5)

            def idx_product(n):
                g, b = divmod(n, 8)
                pe.wait_ge(a_free, A_IP + n + 1)
                return pe.matmul(sv(V_IS)[:, g, :], w1[:, b * 128:(b + 1) * 128], kiT[:, n % 2, :], start=(b == 0), stop=(b == 7),
                                 skip_group_check=True)

            for x in range(17):
                if x < 16:
                    pe.wait_ge(idx_pages[x % 2], 128 * (x // 2 + 1))
                    pe.wait_ge(a_free, A_IP + x - 1)
                    for y in range(4):
                        mm = pe.transpose(sa(A_IP + x)[:, 0, y * 128:(y + 1) * 128], ip[:, x % 2, y * 128:(y + 1) * 128], ident)
                    mm.then_inc(a_full, 1)
                if x == 1:
                    pe.wait_ge(v_free, V_IS - 1)
                if x >= 1:
                    mm = idx_product(x - 1)
            mm.then_inc(v_full, 1)
            pe.wait_ge(irel_ready, 1)
            pe.wait_ge(wz_ready, 1)
            pe.wait_ge(v_free, V_ISW - 1)
            for g in range(2):
                mm = pe.matmul(sv(V_ISW)[0:64, g, :], wz[:], irel[:, g * 512:(g + 1) * 512], start=True, stop=True)
            mm.then_inc(v_full, 1)
            NA = len(AT)
            for u in range(NA + 2):
                if u < NA:
                    g, qt, h = AT[u]
                    n, qs, W = V_S + u, slice(qt * 128, (qt + 1) * 128), (qt + 1) * 128
                    pe.wait_ge(v_free, n - 1)
                    lhs, rhs = (qcat[0:QK, h, qs], kcat[0:QK, h, 0:W]) if g == 0 else (qz[:, h, qs], kT[:, 0:W])
                    pe.matmul(sv(n)[:, 0, 0:W], lhs, rhs, start=True, stop=True).then_inc(v_full, 1)
                if 1 <= u <= NA:
                    g, qt, h = AT[u - 1]
                    n = A_PT + u - 1
                    pe.wait_ge(a_free, n - 1)
                    pe.wait_ge(p_ready, u)
                    for kt in range(qt + 1):
                        mm = pe.transpose(sa(n)[:, 0, kt * 128:(kt + 1) * 128], sP[:, (u - 1) % 3, kt * 128:(kt + 1) * 128], ident)
                    mm.then_inc(a_full, 1)
                if u >= 2:
                    g, qt, h = AT[u - 2]
                    pair, p0 = (u - 2) // 2, (h % 2) * 64
                    pe.wait_ge(a_free, A_PT + u - 1)
                    if pair >= 2 and h % 2 == 0:
                        pe.wait_ge(o_free, pair - 1)
                    for kt in range(qt + 1):
                        vv = vm[:, kt, h * 64:(h + 1) * 64] if g == 0 else tok[:, kt, 416 + (h // 4) * 64:480 + (h // 4) * 64]
                        mm = pe.matmul(psV[p0:p0 + 64, pair % 2, 1, 0:128], vv, sPT[:, (u - 2) % 3, kt * 128:(kt + 1) * 128],
                                       start=(kt == 0), stop=(kt == qt), skip_group_check=True)
                    mm.then_inc(pv_done, 1)
            pe_decode(pe)
            pe_tail(pe)

        def pe_decode(pe):
            pe.wait_ge(far_loaded, 16)
            pe.wait_ge(pn_ready, 2)
            pe.wait_ge(o_free, len(AT) // 2)
            for x in range(3):
                n = V_BF + x
                pe.wait_ge(v_free, n - 1)
                for b in range(2):
                    c = (x * 2 + b) * 512
                    if c < PAST + 1:
                        w = min(512, PAST + 1 - c)
                        mm = pe.matmul(sv(n)[0:64, b, 0:w], rb64[:], ohf[:, c:c + w], start=True, stop=True)
                mm.then_inc(v_full, 1)

            def turn(b, par, j):
                n = A_LT + j
                pe.wait_ge(a_free, at(b, NPG, n - 1))
                for k in range(2):
                    mm = pe.transpose(sa(n)[:, 0, k * 128:(k + 1) * 128], pgs[:, par, j, k * 128:(k + 1) * 128], ident)
                mm.then_inc(a_full, 1)

            def expand(b, j):
                n = V_KX + j
                pe.wait_ge(a_free, at(b, NPG, A_LT + j + 1))
                pe.wait_ge(v_free, at(b, NPG, n - 1))
                for k in range(2):
                    mm = pe.matmul(sv(n)[:, 0, :], lT[:, j % 2, k, :], wukv[:, k, :].rearrange("p (h d) -> p h d", h=H)[:, :, 0:64],
                                   start=(k == 0), stop=(k == 1), skip_group_check=True)
                mm.then_inc(v_full, 1)

            def pages(b, par, loads):
                pe.wait_ge(mla_pages[par], loads)
                for j in range(NPG + 1):
                    if j < NPG:
                        turn(b, par, j)
                    if j >= 1:
                        expand(b, j - 1)

            def weigh(b, par):
                pe.wait_ge(pm_ready, at(b, 1, 1))
                pe.wait_ge(lat_out, at(b, 1, -1)) if not (isinstance(b, int) and b < 2) else None
                for j in range(NPG + 1):
                    rows = pgs[:, par, j, 0:KVR] if j < NPG else tok[:, 4, 0:KVR]
                    mm = pe.matmul(psV[0:8, par, 1, 0:KVR], pm[par][:, j, :], rows, start=(j == 0), stop=(j == NPG), skip_group_check=True)
                mm.then_inc(lat_pv, 1)

            pages(0, 0, 256)
            pages(1, 1, 256)
            weigh(0, 0)
            with pe.Fori(1, 4) as i:
                pages((i, 0), 0, i * 256 + 256)
                weigh((i, -1), 1)
                pages((i, 1), 1, i * 256 + 256)
                weigh((i, 0), 0)
            weigh(7, 1)
            n = A_OL
            pe.wait_ge(a_free, n - 1)
            pe.wait_ge(lat_out, NB)
            for k in range(2):
                for b in range(NB):
                    c = k * 64 + b * 8
                    mm = pe.transpose(sa(n)[:, 0, c:c + 8], olb[:, b, k * 128:(k + 1) * 128], ident[0:8, 0:8])
            mm.then_inc(a_full, 1)
            pe.wait_ge(a_free, n + 1)
            pe.wait_ge(v_free, V_OV - 1)
            for h in range(H):
                for k in range(2):
                    mm = pe.matmul(sv(V_OV)[(h % 2) * 64:(h % 2) * 64 + 64, 0, (h // 2) * 8:(h // 2) * 8 + 8],
                                   wukv[:, k, h * 128 + 64:(h + 1) * 128], olT[:, k, :].rearrange("p (b h) -> p h b", b=NB)[:, h, :],
                                   start=(k == 0), stop=(k == 1), skip_group_check=True)
            mm.then_inc(v_full, 1)

            def k_turn(c4, b):
                n = A_KD + c4 * 8 + b
                pe.wait_ge(k_pages[b % 2], 64 * (c4 * 4 + b // 2 + 1))
                pe.wait_ge(a_free, n - 1)
                for x in range(4):
                    mm = pe.transpose(sa(n)[:, 0, x * 128:(x + 1) * 128], kp[:, b % 2, x, :], ident)
                mm.then_inc(a_full, 1)

            def k_product(c4, b):
                n = V_SD + c4
                if b == 0:
                    pe.wait_ge(v_free, n - 1)
                pe.wait_ge(a_free, A_KD + c4 * 8 + b + 1)
                mm = pe.matmul(sv(n)[0:64, 0, :], qdz[:, b * 64:(b + 1) * 64], kdT[:, b % 2, :], start=(b == 0), stop=(b == 7),
                               skip_group_check=True)
                if b == 7:
                    mm.then_inc(v_full, 1)

            for x in range(33):
                if x < 32:
                    k_turn(*divmod(x, 8))
                if x >= 1:
                    k_product(*divmod(x - 1, 8))
            pe.wait_ge(v_free, V_SN - 1)
            pe.matmul(sv(V_SN)[0:64, 0, 0:8], qd[:], kT[:, SEQ:T], start=True, stop=True).then_inc(v_full, 1)
            pe.wait_ge(p64_ready, 1)
            for x in range(3):
                n = A_PD + x
                pe.wait_ge(a_free, n - 1)
                if x < 2:
                    for j in range(8):
                        mm = pe.transpose(sa(n)[:, 0, j * 64:(j + 1) * 64], s64[:, (x * 8 + j) * 128:(x * 8 + j + 1) * 128], ident[0:64, 0:64])
                else:
                    mm = pe.transpose(sa(n)[0:NB, 0, 0:64], small[0:64, 0:8], ident[0:64, 0:64])
                mm.then_inc(a_full, 1)

            def d_weigh(b, par, loads):
                pe.wait_ge(v_pages[par], loads)
                pe.wait_ge(ptb_ready, at(b, 1, 1))
                pe.wait_ge(d_out, at(b, 1, -1)) if not (isinstance(b, int) and b < 2) else None
                for j in range(NPG):
                    pe.matmul(psV[0:8, par, 1, 0:128], ptb[:, par, j, :], vp[:, par, j, :], start=(j == 0), stop=False, skip_group_check=True)
                pe.matmul(psV[0:8, par, 1, 0:128], ptb[0:NB, par, NPG, :], tok[0:NB, 4, 416:544], start=False, stop=True,
                          skip_group_check=True).then_inc(d_pv, 1)

            d_weigh(0, 0, 256)
            d_weigh(1, 1, 256)
            with pe.Fori(1, 4) as i:
                for par in range(2):
                    d_weigh((i, par), par, i * 256 + 256)
            n = A_OD
            pe.wait_ge(a_free, n - 1)
            pe.wait_ge(d_out, NB)
            for b in range(NB):
                mm = pe.transpose(sa(n)[:, 0, b * 8:b * 8 + 8], od[:, b, :], ident[0:8, 0:8])
            mm.then_inc(a_full, 1)

        def pe_tail(pe):
            pe.wait_ge(sq2_written, 8)
            for g in range(2):
                n = A_MIX + g
                pe.wait_ge(a_free, n - 1)
                for hf in range(2):
                    for k in range(4):
                        mm = pe.matmul(sa(n)[:, hf, 0:HT], ones, sqx[:, 4 * g + k, hf * HT:(hf + 1) * HT], start=(k == 0), stop=(k == 3))
                mm.then_inc(a_full, 1)
            pe.wait_ge(mixed, 8)

            def through(w, src, nk, out, need, ring_free, count, full):
                pe.wait_ge(need[0], need[1])
                pe.wait_ge(ring_free, count)
                for k in range(nk):
                    for hf in range(2):
                        mm = pe.matmul(out[:, hf, 0:HT], w[:, k, :], src[:, k, hf * HT:(hf + 1) * HT],
                                       start=(k == 0), stop=(k == nk - 1), skip_group_check=True)
                mm.then_inc(full, 1)

            with pe.Fori(0, 4) as i:
                for s in range(2):
                    w = wring[:, s * 1024:(s + 1) * 1024].rearrange("p (k n) -> p k n", k=KD)
                    through(w, mixT, KD, sv(V_OUT + s), (out_w[s], i * 16 + 16), v_free, i * 2 + (V_OUT + s - 1), v_full)
            n = A_SS2
            pe.wait_ge(a_free, n - 1)
            pe.wait_ge(sq2_written, 16)
            for hf in range(2):
                for k in range(KD):
                    mm = pe.matmul(sa(n)[:, hf, 0:HT], ones, sqx[:, k, hf * HT:(hf + 1) * HT], start=(k == 0), stop=(k == KD - 1))
            mm.then_inc(a_full, 1)
            pe.wait_ge(h2_done, 9)
            if PADA:
                pe.wait_ge(a_free, n + 1)
                pe.matmul(sa(n + 1)[0:1, 0, 0:1], ones[:, 0:1], ones[:, 0:1], start=True, stop=True).then_inc(a_full, 1)
            if PADV:
                pe.wait_ge(v_free, V_OUT + 8)
                pe.matmul(sv(V_OUT + 8)[0:1, 0, 0:1], ones[:, 0:1], ones[:, 0:1], start=True, stop=True).then_inc(v_full, 1)
            with pe.Fori(0, KF // 2) as i:
                for s in range(2):
                    for c, ring, free, full, base in ((0, sa(A_G + s), a_free, a_full, A_G), (1, sv(V_U + s), v_free, v_full, V_U)):
                        w = wring[:, s * 2048 + c * 1024:s * 2048 + (c + 1) * 1024].rearrange("p (k n) -> p k n", k=KD)
                        through(w, hT, KD, ring, (fin_w[s], i * 32 + 32), free, i * 2 + (base + s - 1), full)
            pe.wait_ge(v_free, V_U + KF)
            with pe.Fori(0, 4) as i:
                for s in range(2):
                    w = wring[:, s * 2816:(s + 1) * 2816].rearrange("p (k n) -> p k n", k=KF)
                    through(w, actT, KF, sv(V_DN + s), (fout_w[s], i * 16 + 16), v_free, i * 2 + (V_DN + s - 1), v_full)
            pe.wait_ge(x_new, 16)
            for t in range(5):
                n, w = A_Y + t, (128 if t < 4 else NB)
                pe.wait_ge(a_free, n - 1)
                out = sa(n).rearrange("p b n -> p (b n)")
                for k in range(KD):
                    mm = pe.transpose(out[0:w, k * 128:(k + 1) * 128], xT[:, k, t * 128:t * 128 + w], ident)
                mm.then_inc(a_full, 1)

        SQ, s = {}, 0
        for i in normed:
            SQ[i] = s
            s += U[i][1]
        widxT = rtmp_w = r1[0:8, 7 * T:8 * T]

        def act_program(act):
            A = nc.scalar.activation
            act.wait_ge(in_loaded, 16 * 21)
            A(csil, cin, ACT.Silu).then_inc(c_silu, 1)
            for j, n in enumerate(A_XT):
                act.wait_ge(a_full, n + 1)
                src = sa(n).rearrange("p b n -> p (b n)")
                if j < 4:
                    dst, src = xT[:, :, j * 128:(j + 1) * 128], src.rearrange("p (k n) -> p k n", k=KD)
                elif j == 4:
                    dst, src = xT[:, :, SEQ:T], src[:, 0:64].rearrange("p (k n) -> p k n", k=KD)
                elif j == 5:
                    dst, src = cT, src[:, 0:72].rearrange("p (k n) -> p k n", k=KD)
                else:
                    dst, src = gT[:], src[:, 0:N_GAIN]
                A(dst, src, ACT.Identity).then_inc(a_free, 1)
            act.wait_ge(a_free, A_XT[4] + 1)
            for k in range(KD):
                A(sqx[:, k, :], xT[:, k, :], ACT.Square).then_inc(sq_written, 1)
            act.wait_ge(a_full, A_MOD + 1)
            A(modT[:], sa(A_MOD)[:, 0, 0:432].rearrange("p (m c) -> p m c", m=48), ACT.Identity).then_inc(a_free, 1)
            act.wait_ge(eps_set, 1)
            act.wait_ge(a_full, A_SS + 1)
            A(halves(sd[:, 0, :]), sa(A_SS)[:, :, 0:HT], ACT.Sqrt, scale=1.0 / D, bias=epsc[:]).then_inc(a_free, 1)
            for k in range(KD):
                act.wait_ge(hT_scaled, k + 1)
                A(hT[:, k, 0:SEQ], hT[:, k, 0:SEQ], ACT.Identity, bias=modT[:, k, 0:1]).then_inc(hT_done, 1)
            act.wait_ge(zeroed, 2)
            for i in range(len(U) + 1):
                if i < len(U):
                    name, nt, rows = U[i]
                    k = kind(name)
                    j = int(name[-1]) if name[-1].isdigit() else 0
                    for t in range(nt):
                        n = A_proj[i][t]
                        act.wait_ge(a_full, n + 1)
                        src = sa(n)[0:rows, :, 0:HT]
                        if k in NORMED:
                            A(halves(sq[0:rows, (SQ[i] + t) % 4, :]), src, ACT.Square)
                            m = normed.index(i)
                            if k == "qlat":
                                dst = qlatT[:, t, :]
                            elif k == "kvlat":
                                dst = latT[:, t, :]
                            else:
                                if m >= 2:
                                    act.wait_ge(norm_done, m - 1)
                                dst = raw[0:rows, m % 2, :]
                            A(halves(dst), src, ACT.Identity).then_inc(a_free, 1)
                        elif k == "qi":
                            A(halves(qiz[0:64, 2 * j, :]), src[0:64], ACT.Identity)
                            A(halves(qiz[64:128, 2 * j + 1, :]), src[64:128], ACT.Identity).then_inc(a_free, 1)
                        else:
                            dst = {"v": vT[:], "kidx": kidxT[:], "widx": widxT}[k]
                            A(halves(dst), src, ACT.Identity).then_inc(a_free, 1)
                if i - 1 in A_norm:
                    name, nt, rows = U[i - 1]
                    m = normed.index(i - 1)
                    k = kind(name)
                    if m >= 2:
                        act.wait_ge(norm_done, m - 1)
                    act.wait_ge(a_full, A_norm[i - 1] + 1)
                    sc = {"qlat": 1.0 / QR, "kvlat": 1.0 / KVR, "q": 1.0 / HD, "k": 1.0 / HD}.get(k, 1.0)
                    A(halves(sd[0:rows, m % 2, :]), sa(A_norm[i - 1])[0:rows, :, 0:HT], ACT.Sqrt, scale=sc,
                      bias=epsc[0:rows]).then_inc(a_free, 1)
            for t in range(5):
                n = A_TOK + t
                w = 128 if t < 4 else NB
                act.wait_ge(a_full, n + 1)
                A(tok[0:w, t, 0:256], sa(n)[0:w, 0, 0:256], ACT.Identity)
                A(tok[0:w, t, 256:288], sa(n)[0:w, 0, 256 + 64:256 + 96], ACT.Identity)
                A(tok[0:w, t, 288:608], sa(n)[0:w, 1, 0:320], ACT.Identity).then_inc(a_free, 1)
            act.wait_ge(a_full, A_WT + 1)
            A(wtok[:, 0:4, :], sa(A_WT)[:, 0, 0:32].rearrange("p (t h) -> p t h", t=4), ACT.Identity, scale=IDX_SCALE)
            A(wtok[0:NB, 4, :], sa(A_WT)[0:NB, 0, 32:40], ACT.Identity, scale=IDX_SCALE).then_inc(a_free, 1)

            for j, (qt, h) in enumerate(IQ):
                n, W = A_IQ + j, (qt + 1) * 128
                act.wait_ge(a_full, n + 1)
                if j >= 2:
                    act.wait_ge(idx_acc, j - 1)
                A(rb[:, j % 2, 0:W], sa(n)[:, 0, 0:W], ACT.Relu).then_inc(a_free, 1)
            for t in range(4):
                n = A_VM + t
                act.wait_ge(a_full, n + 1)
                A(vm[:, t, :], sa(n)[:, 0, :], ACT.Identity).then_inc(a_free, 1)
            act.wait_ge(a_full, A_QS + 1)
            A(qs8.rearrange("b (x n) -> b x n", x=2), sa(A_QS)[0:NB, :, 0:4 * QK], ACT.Identity).then_inc(a_free, 1)
            act.wait_ge(v_full, V_KN + 1)
            act.wait_ge(v_free, V_KN + 1)
            A(pnsq, knew, ACT.Square).then_inc(new_sums, 1)
            for n in range(16):
                act.wait_ge(a_full, A_IP + n + 1)
                A(kiT[:, n % 2, :], sa(A_IP + n)[:, 0, :], ACT.Identity).then_inc(a_free, 1)
            NA = len(AT)
            for u in range(NA + 2):
                if u < NA:
                    g, qt, h = AT[u]
                    W = (qt + 1) * 128
                    act.wait_ge(stats_ready, u + 1)
                    if u >= 3:
                        act.wait_ge(a_full, A_PT + u - 2)
                    A(sP[:, u % 3, 0:W], sS[:, u % 3, 0:W], ACT.Exp, scale=(MLA_SCALE if g == 0 else 1.0),
                      bias=stat[:, u % 3, 1:2], accum_out=stat[:, u % 3, 2:3]).then_inc(exp_done, 1)
                if 1 <= u <= NA:
                    n, W = A_PT + u - 1, (AT[u - 1][1] + 1) * 128
                    act.wait_ge(a_full, n + 1)
                    if u - 1 >= 3:
                        act.wait_ge(pv_done, u - 3)
                    A(sPT[:, (u - 1) % 3, 0:W], sa(n)[:, 0, 0:W], ACT.Identity).then_inc(a_free, 1)
                if u >= 3 and u % 2 == 1:
                    g, qt, h = AT[u - 2]
                    pair = (u - 2) // 2
                    act.wait_ge(pv_done, u - 1)
                    A(mixT[:, 4 * g + h // 2, qt * 128:(qt + 1) * 128], psV[:, pair % 2, 1, 0:128], ACT.Identity).then_inc(o_free, 1)
            act_decode(act)
            act_tail(act)

        def act_decode(act):
            A = nc.scalar.activation

            def evacuate(b, par, j):
                act.wait_ge(a_full, at(b, NPG, A_LT + j + 1))
                A(lT[:, j % 2].rearrange("p k n -> p (k n)"), sa(A_LT + j)[:, 0, 0:256], ACT.Identity).then_inc(a_free, 1)

            def square(b, j):
                act.wait_ge(v_full, at(b, NPG, V_KX + j + 1))
                if not (isinstance(b, int) and b == 0 and j < 2):
                    act.wait_ge(page_sums, at(b, NPG, j - 1))
                A(sqk[:, j % 2, :], sv(V_KX + j)[:, 0, :], ACT.Square).then_inc(squared, 1)

            def roots(b, par):
                act.wait_ge(rstd_in, at(b, 1, 1))
                A(sums[par], sums[par], ACT.Sqrt, scale=1.0 / NOPE, bias=epsc[:]).then_inc(ss_ready, 1)

            def exps(b, par):
                act.wait_ge(shifted, at(b, 1, 1))
                A(pm[par], pm[par], ACT.Exp, scale=MLA_SCALE).then_inc(p_exp, 1)

            def take(b, par):
                act.wait_ge(lat_pv, at(b, 1, 1))
                dst = olb[:, b, :] if isinstance(b, int) else olb[:, bass.ds(at(b, 1, 0), 1), :].rearrange("p b r -> p (b r)")
                A(dst, psV[0:8, par, 1, 0:KVR], ACT.Identity).then_inc(lat_out, 1)

            def pages(b, par, prev):
                for j in range(NPG + 1):
                    if j < NPG:
                        evacuate(b, par, j)
                    if j >= 1:
                        square(b, j - 1)
                    if prev is not None and j == 3:
                        roots(prev, 1 - par)
                    if prev is not None and j == 9:
                        exps(prev, 1 - par)

            pages(0, 0, None)
            pages(1, 1, 0)
            take(0, 0)
            with act.Fori(1, 4) as i:
                pages((i, 0), 0, (i, -1))
                take((i, -1), 1)
                pages((i, 1), 1, (i, 0))
                take((i, 0), 0)
            roots(7, 1)
            exps(7, 1)
            take(7, 1)
            act.wait_ge(a_full, A_OL + 1)
            A(olT.rearrange("p k r -> p (k r)"), sa(A_OL)[:, 0, 0:128], ACT.Identity).then_inc(a_free, 1)
            for x in range(32):
                n = A_KD + x
                act.wait_ge(a_full, n + 1)
                A(kdT[:, x % 2, :], sa(n)[:, 0, :], ACT.Identity).then_inc(a_free, 1)
            act.wait_ge(s64_ready, 1)
            A(s64, s64, ACT.Exp, bias=small[0:64, 9:10], accum_out=small[0:64, 10:11]).then_inc(p64_exp, 1)
            for x in range(3):
                act.wait_ge(a_full, A_PD + x + 1)
                dst, rows = (ptd[:, x * 8:x * 8 + 8, :].rearrange("p j r -> p (j r)"), 128) if x < 2 else (ptd[0:NB, 16, :], NB)
                A(dst, sa(A_PD + x)[0:rows, 0, 0:(512 if x < 2 else 64)], ACT.Identity).then_inc(a_free, 1)

            def d_take(b, par):
                act.wait_ge(d_pv, at(b, 1, 1))
                dst = od[:, b, :] if isinstance(b, int) else od[:, bass.ds(at(b, 1, 0), 1), :].rearrange("p b n -> p (b n)")
                A(dst, psV[0:8, par, 1, 0:128], ACT.Identity).then_inc(d_out, 1)

            with act.Fori(0, 4) as i:
                for par in range(2):
                    d_take((i, par), par)
            act.wait_ge(a_full, A_OD + 1)
            A(odT.rearrange("p b h -> p (b h)"), sa(A_OD)[:, 0, 0:64], ACT.Identity).then_inc(a_free, 1)

        def act_tail(act):
            A = nc.scalar.activation
            act.wait_ge(o_free, len(AT) // 2)
            act.wait_ge(mix_s, 1)
            for k in range(KD):
                A(sqx[:, k, :], mixT[:, k, :], ACT.Square).then_inc(sq2_written, 1)
            for g in range(2):
                act.wait_ge(a_full, A_MIX + g + 1)
                A(halves(sd[:, g, :]), sa(A_MIX + g)[:, :, 0:HT], ACT.Sqrt, scale=1.0 / 512, bias=epsc[:]).then_inc(a_free, 1)
            act.wait_ge(x_new, 8)
            for k in range(KD):
                A(sqx[:, k, :], xT[:, k, :], ACT.Square).then_inc(sq2_written, 1)
            act.wait_ge(a_full, A_SS2 + 1)
            A(halves(sd[:, 0, :]), sa(A_SS2)[:, :, 0:HT], ACT.Sqrt, scale=1.0 / D, bias=epsc[:]).then_inc(a_free, 1)
            for k in range(KD):
                act.wait_ge(h2_scaled, k + 1)
                A(hT[:, k, 0:SEQ], hT[:, k, 0:SEQ], ACT.Identity, bias=modT[:, 24 + k, 0:1]).then_inc(h2_done, 1)
            if PADA:
                act.wait_ge(a_full, A_SS2 + 2)
                A(stat[0:1, 0, 0:1], sa(A_SS2 + 1)[0:1, 0, 0:1], ACT.Identity).then_inc(a_free, 1)
            with act.Fori(0, KF // 2) as i:
                for s in range(2):
                    act.wait_ge(a_full, i * 2 + (A_G + s + 1))
                    A(actT[:, bass.ds(i * 2 + s, 1), :].rearrange("p a (h t) -> p (a h) t", h=2), sa(A_G + s)[:, :, 0:HT],
                      ACT.Silu).then_inc(a_free, 1)
            for t in range(5):
                n, w = A_Y + t, (128 if t < 4 else NB)
                act.wait_ge(a_full, n + 1)
                if t >= 2:
                    act.wait_ge(y_stored[t % 2], 16 * (t // 2))
                A(yt[0:w, t % 2, :], sa(n)[0:w].rearrange("p b n -> p (b n)"), ACT.Identity).then_inc(a_free, 1)

        def dve_program(v):
            link = Link(v)

            v.memset(gin, 0.0)
            v.memset(epsc[:], EPS).then_inc(eps_set, 1)
            v.wait_ge(bada_loaded, 16)
            v.wait_ge(v_full, 1)

            def ada_rows(s, col, full):
                v.wait_ge(v_full, full)
                v.tensor_tensor(ada9[:, bass.ds(col, 256)], psV[0:9, s, 0, 0:256], bada9[:, bass.ds(col, 256)],
                                ALU.add).then_inc(v_free, 1)

            with v.Fori(0, 12) as i:
                for s in range(2):
                    ada_rows(s, i * 512 + s * 256, i * 2 + (s + 1))
            v.wait_ge(a_free, A_MOD + 1)
            for w, sc in ((0, 8), (1, 32)):
                link(v.scalar_tensor_tensor(amod[:, w], modT[:, sc:sc + 8, :], 1.0,
                                            gT[:, w * 8:w * 8 + 8].unsqueeze(2).broadcast_to([128, 8, 9]), ALU.add, ALU.mult))
            modulate(v, link, 0)
            v.wait_ge(zeroed, 2)
            for i in range(1, len(U) + 2):
                if i - 1 in A_norm:
                    name, nt, rows = U[i - 1]
                    k = kind(name)
                    j = int(name[-1]) if name[-1].isdigit() else 0
                    m = normed.index(i - 1)
                    v.wait_ge(a_free, A_norm[i - 1] + 1)
                    r = sd[0:rows, m % 2, :]
                    link(v.reciprocal(r, r))
                    for t in range(nt):
                        g = gT[0:rows, gain_col(name, t):gain_col(name, t) + 1]
                        if k == "q":
                            for p0, hh in ((0, j), (64, j + 4)):
                                ins = v.scalar_tensor_tensor(qz[p0:p0 + 64, hh, :], raw[p0:p0 + 64, m % 2, :], g[p0:p0 + 64],
                                                             r[p0:p0 + 64], ALU.mult, ALU.mult)
                        elif k == "kn":
                            ins = v.scalar_tensor_tensor(kcat[0:64, j, :], raw[0:64, m % 2, :], g, r, ALU.mult, ALU.mult)
                        else:
                            if k == "qlat":
                                src = dst = qlatT[:, t, :]
                            elif k == "kvlat":
                                src = dst = latT[:, t, :]
                            else:
                                src = raw[0:rows, m % 2, :]
                                dst = {"krope": krF[:], "k": kT[:], "qc": qcat[0:QK, j, :]}[k]
                            ins = v.scalar_tensor_tensor(dst, src, g, r, ALU.mult, ALU.mult)
                    ins.then_inc(norm_done, 1)
                if i - 2 in V_rot:
                    n = V_rot[i - 2]
                    dst = (krF[64:96, :] if U[i - 2][0] == "krope" else qcat[64:96, int(U[i - 2][0][-1]), :])
                    v.wait_ge(v_full, n + 1)
                    v.tensor_tensor(halves(rtmp[64:96, :]), sv(n)[64:96, :, 0:HT], halves(rope[64:96, 1, :]),
                                    ALU.mult).then_inc(v_free, 1)
                    v.wait_ge(norm_done, normed.index(i - 2) + 1)
                    link(v.tensor_tensor(dst, dst, rope[64:96, 0, :], ALU.mult))
                    v.wait_ge(v_free, n + 1)
                    v.tensor_tensor(dst, dst, rtmp[64:96, :], ALU.add).then_inc(rope_done, 1)
            v.wait_ge(rope_done, 1)
            v.tensor_copy(kcat[64:96, :, :], krF[64:96, :].unsqueeze(1).broadcast_to([32, 8, T])).then_inc(kr_spread, 1)

            for j, (qt, h) in enumerate(IQ):
                m0, m1 = MQ[qt]
                v.wait_ge(a_free, A_IQ + j + 1)
                if h > 0:
                    v.wait_ge(idx_acc, j)
                    v.scalar_tensor_tensor(msk[:, m0:m1], rb[:, j % 2, 0:m1 - m0], wtok[:, qt, h:h + 1], msk[:, m0:m1],
                                           ALU.mult, ALU.add).then_inc(idx_acc, 1)
                else:
                    v.tensor_scalar(msk[:, m0:m1], rb[:, j % 2, 0:m1 - m0], wtok[:, qt, h:h + 1], None, ALU.mult).then_inc(idx_acc, 1)
            v.wait_ge(idx_acc, len(IQ))
            for qt in range(1, 4):
                m1 = MQ[qt][1]
                link(v.tensor_tensor(msk[:, m1 - 128:m1], msk[:, m1 - 128:m1], cext[:, 384:512], ALU.add))
            v.wait_ge(v_full, V_BIAS + 1)
            v.tensor_copy(g8, sv(V_BIAS)[0:8, 0, 0:384]).then_inc(v_free, 1)
            for j in range(2):
                n = V_BIAS + 1 + j
                v.wait_ge(v_full, n + 1)
                v.tensor_copy(toep[:, j * 1024:(j + 1) * 1024], sv(n).rearrange("p b n -> p (b n)")).then_inc(v_free, 1)

            link(v.memset(w1, 0.0))
            v.memset(ptd[:, NPG, :], 0.0)
            v.wait_ge(norm_done, len(normed))
            v.tensor_scalar(qcat[0:64, :, SEQ:T], qcat[0:64, :, SEQ:T], gT[0:64, G_KN:G_KN + 1], None, ALU.mult).then_inc(qs_gained, 1)
            w1v = w1.rearrange("p (b x) -> p b x", x=144)
            for p0, c in ((0, 0), (64, 8)):
                for odd in range(2):
                    v.tensor_copy(w1v[p0:p0 + 64, :, c + odd:c + 8:2],
                                  qiz[odd * 64:odd * 64 + 64, odd:8:2, SEQ:T].rearrange("p h b -> p b h")).then_inc(w1_ready, 1)
            link(v.tensor_copy(qd[:].rearrange("p (b h) -> p b h", b=NB), qz[:, :, SEQ:T].rearrange("p h b -> p b h")))
            link(v.memset(qdz[:], 0.0))
            v.tensor_copy(qdz[:].rearrange("p (b x) -> p b x", x=72)[:, :, 0:8], qd[:].rearrange("p (b h) -> p b h", b=NB)).then_inc(w1_ready, 1)
            v.wait_ge(v_full, V_KN + 1)
            v.tensor_copy(knew, sv(V_KN)[0:NB, 0, :]).then_inc(v_free, 1)
            v.wait_ge(const_loaded, 80)
            v.wait_ge(v_full, V_WC + 1)
            v.tensor_tensor_reduce(small[:, 0:8], sv(V_WC)[:, 0, 0:8], sel[:, 64:72], 1.0, 0.0, ALU.mult, ALU.add,
                                   small[:, 8:9]).then_inc(v_free, 1)
            v.wait_ge(v_free, V_WC + 1)
            v.tensor_scalar(wz[:], sel[:, 0:64], small[:, 8:9], None, ALU.mult).then_inc(wz_ready, 1)
            v.tensor_tensor(irel[:, 0:64].rearrange("p (h b) -> p h b", h=H), qiz[:, :, SEQ:T],
                            kidxT[:, SEQ:T].unsqueeze(1).broadcast_to([128, H, NB]), ALU.mult).then_inc(pn_ready, 1)
            v.wait_ge(v_full, V_WC + 2)
            v.tensor_scalar(small[0:NB, 16:24], sv(V_WC + 1)[0:NB, 0, 0:8], 0.0, None, ALU.max).then_inc(v_free, 1)
            v.wait_ge(v_free, V_WC + 2)
            link(v.tensor_tensor_reduce(small[0:NB, 24:32], small[0:NB, 16:24], wtok[0:NB, 4, :], 1.0, 0.0, ALU.mult, ALU.add,
                                        small[0:NB, 32:33]))
            link(v.tensor_copy(sc8[:, PAST:PAST + 1], small[0:NB, 32:33]))
            v.wait_ge(new_sums, 1)
            link(v.tensor_reduce(ssnew[:], pnsq.rearrange("p (h d) -> p h d", h=H), AXX, ALU.add))
            link(v.tensor_copy(rb64[:].rearrange("p (b h) -> p b h", b=NB), rbias.unsqueeze(1).broadcast_to([NBUCK, NB, 8])))
            v.tensor_scalar(small[:, 40:41], small[:, 8:9], 0.0, None, ALU.mult).then_inc(pn_ready, 1)
            v.wait_ge(v_full, V_IS + 1)
            v.tensor_scalar(irel, sv(V_IS).rearrange("p b n -> p (b n)"), 0.0, None, ALU.max).then_inc(v_free, 1)
            v.wait_ge(v_free, V_IS + 1)
            v.tensor_scalar(small[:, 41:42], small[:, 8:9], 0.0, None, ALU.mult).then_inc(irel_ready, 1)
            v.wait_ge(v_full, V_ISW + 1)
            for g in range(2):
                for par in range(2):
                    dst = sc8[:, g * 1024:(g + 1) * 1024].rearrange("p (x two) -> p x two", two=2)[:, :, par]
                    ins = v.tensor_copy(dst, sv(V_ISW)[par * 32:par * 32 + NB, g, :])
            ins.then_inc(v_free, 1)
            v.wait_ge(v_free, V_ISW + 1)

            def top_rounds():
                for qt in range(1, 4):
                    m0, m1 = MQ[qt]
                    for r in range(TOPK_P // 8):
                        link(v.max(top8[:], msk[:, m0:m1]))
                        link(v.match_replace(msk[:, m0:m1], top8[:], msk[:, m0:m1], TAKEN))
                        yield
                    link(v.tensor_scalar(msk[:, m0:m1], msk[:, m0:m1], TAKEN / 2, NEG, ALU.is_gt, ALU.mult))
                for r in range(TOPK_S // 8):
                    link(v.max(top8[0:NB], sc8))
                    link(v.match_replace(sc8, top8[0:NB], sc8, TAKEN))
                    yield
                v.tensor_scalar(sc8, sc8, TAKEN / 2, NEG, ALU.is_gt, ALU.mult).then_inc(top_done, 1)

            rounds = top_rounds()
            v.wait_ge(qs_out, 16)
            NA = len(AT)
            for u in range(NA + 1):
                if u < NA:
                    g, qt, h = AT[u]
                    n, W, c = V_S + u, (qt + 1) * 128, u % 3
                    S = sS[:, c, 0:W]
                    v.wait_ge(v_full, n + 1)
                    if u >= 3:
                        v.wait_ge(exp_done, u - 2)
                    if g == 0:
                        v.tensor_tensor_reduce(S, sv(n)[:, 0, 0:W], cext[:, 512 - W:512], 1.0, TAKEN, ALU.add, ALU.max,
                                               stat[:, c, 0:1]).then_inc(v_free, 1)
                        v.wait_ge(v_free, n + 1)
                        v.tensor_scalar(stat[:, c, 1:2], stat[:, c, 0:1], -MLA_SCALE, None, ALU.mult).then_inc(stats_ready, 1)
                    else:
                        near = min(W, 256)
                        if W > near:
                            link(v.tensor_scalar(S[:, 0:W - near], sv(n)[:, 0, 0:W - near], DSA_SCALE, toepv[:, h, 0:1], ALU.mult, ALU.add))
                        v.scalar_tensor_tensor(S[:, W - near:W], sv(n)[:, 0, W - near:W], DSA_SCALE, toepv[:, h, 256 - near:256],
                                               ALU.mult, ALU.add).then_inc(v_free, 1)
                        v.wait_ge(v_free, n + 1)
                        mask = cext[:, 384:512] if qt == 0 else msk[:, MQ[qt][0]:MQ[qt][1]]
                        link(v.tensor_tensor_reduce(S, S, mask, 1.0, TAKEN, ALU.add, ALU.max, stat[:, c, 0:1]))
                        v.tensor_scalar(stat[:, c, 1:2], stat[:, c, 0:1], -1.0, None, ALU.mult).then_inc(stats_ready, 1)
                if u >= 1:
                    c, W = (u - 1) % 3, (AT[u - 1][1] + 1) * 128
                    v.wait_ge(exp_done, u)
                    link(v.reciprocal(stat[:, c, 3:4], stat[:, c, 2:3]))
                    v.tensor_scalar(sP[:, c, 0:W], sP[:, c, 0:W], stat[:, c, 3:4], None, ALU.mult).then_inc(p_ready, 1)
                for _ in range(2 if u < 31 else 1):
                    next(rounds, None)
            for _ in rounds:
                pass
            dve_decode(v, link)
            dve_tail(v, link)

        def dve_decode(v, link):
            link(v.memset(small[:, 42:43], 0.0))
            for x in range(3):
                n = V_BF + x
                v.wait_ge(v_full, n + 1)
                if x < 2:
                    v.tensor_copy(bm64[:, x * 1024:(x + 1) * 1024], sv(n)[0:64].rearrange("p b n -> p (b n)")).then_inc(v_free, 1)
                else:
                    v.tensor_copy(bm64[:, 2048:2049], sv(n)[0:64, 0, 0:1]).then_inc(v_free, 1)
            v.wait_ge(qbc_loaded, 16)
            for x in range(2):
                v.memset(sfull[x][:, NPG, :], NEG)
                ins = v.memset(sums[x][:, NPG, :], 1.0)
            ins.then_inc(neg_set, 1)
            v.wait_ge(neg_set, 1)

            def query(b):
                return qbc[:, b] if isinstance(b, int) else qbc[:, bass.ds(at(b, 1, 0), 1)].rearrange("p a h d -> p (a h) d")

            def dot(b, par, j):
                n = V_KX + j
                v.wait_ge(squared, at(b, NPG, j + 1))
                prj = pr[:, j % 2, :].rearrange("p (h d) -> p h d", h=H)
                v.tensor_tensor(prj, sv(n)[:, 0, :].rearrange("p (h d) -> p h d", h=H), query(b)[:, :, 0:NOPE], ALU.mult).then_inc(v_free, 1)
                v.wait_ge(v_free, at(b, NPG, n + 1))
                v.tensor_reduce(dots[par][:, j, :], prj, AXX, ALU.add)
                v.tensor_reduce(sums[par][:, j, :], sqk[:, j % 2, :].rearrange("p (h d) -> p h d", h=H), AXX, ALU.add).then_inc(page_sums, 1)

            def rope_part(b, par, c):
                v.wait_ge(rope_mul, at(b, 4, c + 1))
                v.tensor_reduce(drope[par][:, 4 * c:4 * c + 4, :], rp[:, c % 2], AXX, ALU.add).then_inc(rope_sum, 1)

            def new_row(b, par):
                q = query(b)
                t = small[0:NB, 0:1]
                big = newp
                link(v.tensor_tensor(big[:, :, 0:64], knew.rearrange("p (h d) -> p h d", h=H), q[0:NB, :, 0:64], ALU.mult))
                link(v.tensor_reduce(dots[par][0:NB, NPG, :], big[:, :, 0:64], AXX, ALU.add))
                link(v.tensor_tensor(big[:, :, 0:32], tok[0:NB, 4, KVR:ROW].unsqueeze(1).broadcast_to([NB, H, ROPE]), q[0:NB, :, 64:96], ALU.mult))
                link(v.tensor_reduce(drope[par][0:NB, NPG, :], big[:, :, 0:32], AXX, ALU.add))
                v.tensor_copy(sums[par][0:NB, NPG, :], ssnew[:]).then_inc(rstd_in, 1)

            def scores(b, par):
                v.wait_ge(ss_ready, at(b, 1, 1))
                link(v.reciprocal(sums[par], sums[par]))
                link(v.tensor_tensor(dots[par][:, 0:NPG], dots[par][:, 0:NPG], sums[par][:, 0:NPG], ALU.mult))
                link(v.tensor_tensor(dots[par][0:NB, NPG], dots[par][0:NB, NPG], sums[par][0:NB, NPG], ALU.mult))
                link(v.tensor_tensor(sfull[par][:, 0:NPG], dots[par][:, 0:NPG], drope[par][:, 0:NPG], ALU.add))
                link(v.tensor_tensor(sfull[par][0:NB, NPG], dots[par][0:NB, NPG], drope[par][0:NB, NPG], ALU.add))
                only = onlyc[0:NB, b:b + 1] if isinstance(b, int) else onlyc[0:NB, bass.ds(at(b, 1, 0), 1)]
                link(v.tensor_scalar(sfull[par][0:NB, NPG], sfull[par][0:NB, NPG], only, None, ALU.add))
                v.tensor_reduce(hstat[:, 0, :], sfull[par].rearrange("p j h -> p h j"), AXX, ALU.max).then_inc(smax, 1)

            def shift(b, par):
                v.wait_ge(gmax, at(b, 1, 1))
                v.tensor_tensor(pm[par], sfull[par], hstat[:, 1, :].unsqueeze(1).broadcast_to([128, NPG + 1, 8]), ALU.subtract).then_inc(shifted, 1)

            def row_sums(b, par):
                v.wait_ge(p_exp, at(b, 1, 1))
                v.tensor_reduce(hstat[:, 2, :], pm[par].rearrange("p j h -> p h j"), AXX, ALU.add).then_inc(psum_ready, 1)

            def normalise(b, par):
                v.wait_ge(gsum, at(b, 1, 1))
                link(v.reciprocal(hstat[:, 3, :], hstat[:, 3, :]))
                v.tensor_tensor(pm[par], pm[par], hstat[:, 3, :].unsqueeze(1).broadcast_to([128, NPG + 1, 8]), ALU.mult).then_inc(pm_ready, 1)

            def pages(b, par, prev):
                for j in range(NPG):
                    dot(b, par, j)
                    if j % 4 == 3:
                        rope_part(b, par, j // 4)
                    if prev is not None:
                        for at_j, step in ((4, scores), (8, shift), (10, row_sums), (13, normalise)):
                            if j == at_j:
                                step(prev, 1 - par)
                v.wait_ge(page_sums, at(b, NPG, NPG))
                new_row(b, par)

            pages(0, 0, None)
            pages(1, 1, 0)
            with v.Fori(1, 4) as i:
                LP = link.per_loop(i, 1, lambda: (pages((i, 0), 0, (i, -1)), pages((i, 1), 1, (i, 0))))
            link.after_loop()
            for step in (scores, shift, row_sums, normalise):
                step(7, 1)
            v.wait_ge(v_full, V_OV + 1)
            v.tensor_copy(mixT[:, 0:4, SEQ:T], sv(V_OV)[:, 0, 0:32].rearrange("p (k b) -> p k b", k=4)).then_inc(v_free, 1)

            v.wait_ge(mask_back, 16)
            link(v.tensor_tensor(bm64, bm64, s64, ALU.add))
            for c4 in range(4):
                n = V_SD + c4
                v.wait_ge(v_full, n + 1)
                v.scalar_tensor_tensor(s64[:, c4 * 512:(c4 + 1) * 512], sv(n)[0:64, 0, :], DSA_SCALE, bm64[:, c4 * 512:(c4 + 1) * 512],
                                       ALU.mult, ALU.add).then_inc(v_free, 1)
            v.wait_ge(v_full, V_SN + 1)
            v.tensor_tensor_reduce(small[0:64, 0:8], sv(V_SN)[0:64, 0, 0:8], sel[0:64, 72:80], 1.0, 0.0, ALU.mult, ALU.add,
                                   small[0:64, 8:9]).then_inc(v_free, 1)
            v.wait_ge(v_free, V_SN + 1)
            link(v.scalar_tensor_tensor(s64[:, PAST:PAST + 1], small[0:64, 8:9], DSA_SCALE, bm64[:, PAST:PAST + 1], ALU.mult, ALU.add))
            link(v.tensor_reduce(small[0:64, 11:12], s64, AXX, ALU.max))
            v.tensor_scalar(small[0:64, 9:10], small[0:64, 11:12], -1.0, None, ALU.mult).then_inc(s64_ready, 1)
            v.wait_ge(p64_exp, 1)
            link(v.reciprocal(small[0:64, 12:13], small[0:64, 10:11]))
            link(v.tensor_scalar(s64, s64, small[0:64, 12:13], None, ALU.mult))
            v.tensor_scalar(small[0:64, 0:8], sel[0:64, 72:80], s64[:, PAST:PAST + 1], None, ALU.mult).then_inc(p64_ready, 1)
            v.wait_ge(a_free, A_OD + 1)
            for c in range(2):
                for par in range(2):
                    ins = v.tensor_copy(mixT[par * 64:par * 64 + 64, 4 + 2 * c:6 + 2 * c, SEQ:T],
                                        odT[c * 64:c * 64 + 64, :, 4 * c + par:4 * c + 4:2].rearrange("p b h -> p h b"))
            ins.then_inc(mix_s, 1)

        def dve_tail(v, link):
            for g in range(2):
                v.wait_ge(a_free, A_MIX + g + 1)
                link(v.reciprocal(sd[:, g, :], sd[:, g, :]))
                for k in range(4 * g, 4 * g + 4):
                    v.scalar_tensor_tensor(mixT[:, k, :], mixT[:, k, :], gT[:, G_OUT + k:G_OUT + k + 1], sd[:, g, :],
                                           ALU.mult, ALU.mult).then_inc(mixed, 1)

            def add_gated(slot, m, gate, count, s):
                x = xT[:, bass.ds(m, 1), :].rearrange("p a t -> p (a t)")
                gt = modT[:, bass.ds(m + gate, 1), :].rearrange("p a c -> p (a c)")
                v.wait_ge(v_full, count)
                v.scalar_tensor_tensor(x[:, 0:HT], slot[:, 0, 0:HT], gt[:, 0:1], x[:, 0:HT], ALU.mult, ALU.add)
                v.scalar_tensor_tensor(x[:, HT:SEQ], slot[:, 1, 0:SEQ - HT], gt[:, 0:1], x[:, HT:SEQ], ALU.mult, ALU.add)
                v.tensor_tensor(gated[:, s, :], slot[:, 1, SEQ - HT:HT], gt[:, 1:9], ALU.mult).then_inc(v_free, 1)
                v.wait_ge(v_free, count)
                v.tensor_tensor(x[:, SEQ:T], x[:, SEQ:T], gated[:, s, :], ALU.add).then_inc(x_new, 1)

            with v.Fori(0, 4) as i:
                for s in range(2):
                    add_gated(sv(V_OUT + s), i * 2 + s, 16, i * 2 + (V_OUT + s + 1), s)
            v.wait_ge(a_free, A_SS2 + 1)
            modulate(v, link, 1)
            if PADV:
                v.wait_ge(v_full, V_OUT + 9)
                v.tensor_copy(stat[0:1, 0, 1:2], sv(V_OUT + 8)[0:1, 0, 0:1]).then_inc(v_free, 1)
            with v.Fori(0, KF // 2) as i:
                for s in range(2):
                    v.wait_ge(v_full, i * 2 + (V_U + s + 1))
                    v.wait_ge(a_free, i * 2 + (A_G + s + 1))
                    t = actT[:, bass.ds(i * 2 + s, 1), :].rearrange("p a (h t) -> p (a h) t", h=2)
                    v.tensor_tensor(t, t, sv(V_U + s)[:, :, 0:HT], ALU.mult).then_inc(v_free, 1)
            with v.Fori(0, 4) as i:
                for s in range(2):
                    add_gated(sv(V_DN + s), i * 2 + s, 40, i * 2 + (V_DN + s + 1), s)

        def modulate(v, link, w):
            v.wait_ge(a_free, (A_SS, A_SS2)[w] + 1)
            scaled, done = ((hT_scaled, hT_done), (h2_scaled, h2_done))[w]
            link(v.reciprocal(sd[:, 0, :], sd[:, 0, :]))
            for k in range(KD):
                v.scalar_tensor_tensor(hT[:, k, 0:SEQ], xT[:, k, 0:SEQ], amod[:, w, k, 0:1], sd[:, 0, 0:SEQ],
                                       ALU.mult, ALU.mult).then_inc(scaled, 1)
            hs = hT[:, :, SEQ:T]
            link(v.tensor_tensor(hs, xT[:, :, SEQ:T], amod[:, w, :, 1:9], ALU.mult))
            link(v.tensor_tensor(hs, hs, sd[:, 0, SEQ:T].unsqueeze(1).broadcast_to([128, 8, NB]), ALU.mult))
            v.tensor_tensor(hs, hs, modT[:, w * 24:w * 24 + 8, 1:9], ALU.add).then_inc(done, 1)

        def pool_program(g):
            g.memset(tok[:, 4, :], 0.0).then_inc(zeroed, 1)
            g.wait_ge(a_free, A_MOD + 1)
            g.wait_ge(a_full, A_XT[6] + 1)
            g.memset(qiz[:], 0.0)
            g.memset(qz, 0.0).then_inc(zeroed, 1)
            for t in range(5):
                g.wait_ge(a_free, A_TOK + t + 1)
                w = 128 if t < 4 else NB
                tt = slice(t * 128, t * 128 + w)
                if t < 4:
                    outs = (o["mla_p"][0, 0, tt, :], o["kv_p"][0, 0, tt].rearrange("t a c d -> t (a c d)"), o["idx_p"][0, 0, tt, :])
                else:
                    outs = (o["mla_s"][0, :, 0, :], o["kv_s"][0, :, 0].rearrange("t a c d -> t (a c d)"), o["idx_s"][0, :, 0, :])
                for (c0, c1), dst in zip(((0, 288), (288, 544), (544, 608)), outs):
                    g.dma_start(dst, tok[0:w, t, c0:c1]).then_inc(tokens_stored, 16)
            g.wait_ge(qbc_loaded, 16)

            def rope_pages(b, par, loads):
                q = qbc[:, b]
                g.wait_ge(mla_pages[par], loads)
                for c in range(4):
                    if b > 0 or c >= 2:
                        g.wait_ge(rope_sum, 4 * b + c - 1)
                    g.tensor_tensor(rp[:, c % 2], pgs[:, par, 4 * c:4 * c + 4, KVR:ROW].unsqueeze(2).broadcast_to([128, 4, H, ROPE]),
                                    q[:, :, NOPE:QK].unsqueeze(1).broadcast_to([128, 4, H, ROPE]), ALU.mult).then_inc(rope_mul, 1)

            def maxima(b):
                g.wait_ge(smax, b + 1)
                g.partition_all_reduce(hstat[:, 1, :], hstat[:, 0, :], 128, RMAX).then_inc(gmax, 1)
                g.wait_ge(psum_ready, b + 1)
                g.partition_all_reduce(hstat[:, 3, :], hstat[:, 2, :], 128, RADD).then_inc(gsum, 1)

            for b in range(NB):
                rope_pages(b, b % 2, 256 * (b // 2 + 1))
                if b >= 1:
                    maxima(b - 1)
            maxima(NB - 1)
            g.wait_ge(a_free, A_PD + 3)
            for par in range(2):
                g.tensor_copy(ptb[:, par], ptd[:, :, par * 8:par * 8 + 8]).then_inc(ptb_ready, 1)
            for b in range(2, NB):
                g.wait_ge(d_pv, b - 1)
                g.tensor_copy(ptb[:, b % 2], ptd[:, :, b * 8:b * 8 + 8]).then_inc(ptb_ready, 1)
            g.wait_ge(tokens_stored, 16 * 15)

        block = ctx.enter_context(nc.Block())
        block.sync(lambda e: sp_program(e))
        block.tensor(lambda e: pe_program(e))
        block.scalar(lambda e: act_program(e))
        block.vector(lambda e: dve_program(e))
        block.gpsimd(lambda e: pool_program(e))


_INS = ["x_prompt", "x_sample", "c_prompt", "c_sample", "cache_mla", "cache_kv", "cache_idx", "page_table",
        "rel_bias", "w_ada", "b_ada", "g_norm_mix", "g_norm_ffn", "w_in", "g_q_lat", "w_uq", "g_kv_lat", "w_ukv",
        "g_mla_q_nope", "g_mla_q_rope", "g_mla_k_nope", "g_mla_k_rope", "g_dsa_q", "g_dsa_k", "g_out", "w_out",
        "w_ffn_in", "w_ffn_out"]
_OUTS = [("y_p", (1, SEQ, D)), ("y_s", (NB, 1, D)),
         ("mla_p", (1, 1, SEQ, ROW)), ("kv_p", (1, 1, SEQ, 2, 2, HD)), ("idx_p", (1, 1, SEQ, IDX)),
         ("mla_s", (1, NB, 1, ROW)), ("kv_s", (1, NB, 1, 2, 2, HD)), ("idx_s", (1, NB, 1, IDX))]


def kernel(**inputs):
    import concourse.bacc as _bacc
    from concourse.bass_utils import run_bass_kernel_spmd as _run

    nc = _bacc.Bacc("TRN2", target_bir_lowering=False, num_devices=1)
    arrays = {name: np.ascontiguousarray(inputs[name]) for name in _INS}
    arrays.update(shape_constants())
    ins = {k: nc.dram_tensor(k, v.shape, mybir.dt.from_np(v.dtype), kind="ExternalInput").ap() for k, v in arrays.items()}
    outs = {k: nc.dram_tensor(k, shape, F32, kind="ExternalOutput").ap() for k, shape in _OUTS}
    build(nc, ins, outs)
    r = _run(nc, [arrays], core_ids=[0])
    return tuple(r.results[0][k] for k, _ in _OUTS)
```

```python
from contextlib import ExitStack

import numpy as np

import concourse.bass as bass
from concourse import mybir

F32 = mybir.dt.float32
F32R = mybir.dt.float32r
I32 = mybir.dt.int32
ALU = mybir.AluOpType
ACT = mybir.ActivationFunctionType
AXX = mybir.AxisListType.X
RMAX = bass.bass_isa.ReduceOp.max
RADD = bass.bass_isa.ReduceOp.add

D, SEQ, NB, PAST, PAGE = 1024, 512, 8, 2048, 128
NPG = PAST // PAGE
H, NOPE, ROPE, VD = 8, 64, 32, 64
QK = NOPE + ROPE
QR, KVR = 384, 256
ROW = KVR + ROPE
HD, IDX = 64, 64
TOPK_P, TOPK_S = min(256, SEQ // 4), min(256, (PAST + 1) // 4)
NBUCK, MAXD = 32, 128
DFF = 2816
EPS = 1e-6
T = SEQ + NB
HT = T // 2
KD = D // 128
KF = DFF // 128
MLA_SCALE = float(QK) ** -0.5
DSA_SCALE = float(HD) ** -0.5
IDX_SCALE = float(IDX * 8) ** -0.5
NEG = -1e30
TAKEN = -3e38
C_KV, C_KR, C_Q, C_K, C_V, C_QI, C_KI, C_WI = 384, 640, 672, 1184, 1312, 1440, 1952, 2016
PER_TURN = 22
G_MIX, G_FFN, G_OUT, G_QL, G_KVL, G_Q, G_KN, G_KR, G_DQ, G_DK, N_GAIN = 0, 8, 16, 24, 27, 29, 30, 30, 31, 32, 33


def shape_constants():
    f = np.float32
    mats = np.zeros((6, 128, 128), f)
    mats[0] = np.eye(128)
    mats[1] = np.eye(128)[::-1]
    mats[2] = 1.0
    mats[3, :64, :64] = mats[3, 64:, 64:] = 1.0
    mats[4, :64, :64] = 1.0 / NOPE
    mats[4, 64:96, 64:96] = 1.0 / ROPE
    half = ROPE // 2
    for j in range(half):
        mats[5, 64 + half + j, 64 + j] = -1.0
        mats[5, 64 + j, 64 + half + j] = 1.0
    pos = np.concatenate([np.arange(SEQ), np.full(NB, PAST)]).astype(f)
    freq = (f(10000.0) ** (-np.arange(half, dtype=f) / f(half))).astype(f)
    ang = pos[None, :] * freq[:, None]
    rope = np.zeros((QK, 2, T), f)
    for r in range(ROPE):
        rope[NOPE + r, 0] = np.cos(ang[r % half])
        rope[NOPE + r, 1] = np.sin(ang[r % half])
    def bucket(d):
        d = np.maximum(d, 0)
        lr = np.log((np.maximum(d, 16).astype(f) / f(16)).astype(f)) / f(np.log(MAXD / 16))
        large = np.minimum(16 + (lr * f(16)).astype(np.int32), NBUCK - 1)
        return np.where(d < 16, d, large)
    near = bucket(255 - np.arange(384))
    far = bucket(PAST - np.arange(PAST + 1))
    onehot = (np.concatenate([near, far])[None, :] == np.arange(NBUCK)[:, None]).astype(f)
    cext = np.zeros((128, 512), f)
    cext[:, 384:] = np.where(np.arange(128)[None, :] <= np.arange(128)[:, None], 0.0, NEG)
    only = np.where(np.arange(128)[:, None] == np.arange(NB)[None, :], 0.0, NEG).astype(f)
    rows = np.arange(128)
    sel = np.zeros((128, 192), f)
    sel[rows, ((rows // 8) % 2) * 32 + rows // 16] = 1.0
    sel[rows, 64 + rows % 8] = 1.0

    r64 = np.arange(64)
    sel[r64, 72 + r64 // 8] = 1.0
    sel[rows, 80] = rows % 8
    sel_b = (np.arange(NB)[:, None] == (rows // 16)[None, :]).astype(f)
    return {"k_sel": sel, "k_selb": sel_b, "k_mats": mats.transpose(1, 0, 2).copy(), "k_rope": rope, "k_onehot": onehot,
            "k_cext": cext, "k_only": only}


def units():
    u = [("qlat", 3, 128), ("v", 1, 128), ("kvlat", 2, 128), ("kidx", 1, 128), ("krope", 1, 96)]
    u += [(f"q{t}", 1, 128) for t in range(4)] + [("k", 1, 128)]
    u += [(f"qi{t}", 1, 128) for t in range(4)] + [("widx", 1, 8)]
    u += [(f"qc{h}", 1, QK) for h in range(H)] + [(f"kn{h}", 1, NOPE) for h in range(H)]
    return u


def kind(name):
    return name.rstrip("0123456789")


NORMED = {"qlat", "kvlat", "krope", "q", "k", "qc", "kn"}
ROPED = {"krope", "qc"}


def build(nc, a, o):
    U = units()
    stack = ExitStack()
    with stack as ctx:
        place = {}

        def sb(name, shape, dt=F32):
            place[name] = (nc.sbuf_base + 31) // 32 * 32
            return ctx.enter_context(nc.sbuf_tensor(name, shape, dt))

        def rounded(name, shape):
            return nc.alloc_sbuf_tensor_at(name + "_r", shape, F32R, offset=place[name])

        sems = {}

        def sem(name):
            if name not in sems:
                sems[name] = ctx.enter_context(nc.semaphore(name))
            return sems[name]

        xT = sb("xT", [128, KD, T])
        hT = sb("hT", [128, KD, T])
        wide = sb("wide", [128, 24, T])
        r1 = sb("r1", [128, 8320])
        qiz = sb("qiz", [128, 8, T])
        wring = sb("wring", [128, 5632])
        latT = sb("latT", [128, 2, T])
        kT = sb("kT", [128, T])
        vT = sb("vT", [128, T])
        kidxT = sb("kidxT", [128, T])
        krF = sb("krF", [QK, T])
        tok = sb("tok", [128, 5, 608])
        msk = sb("msk", [128, 1152])
        wukv = sb("wukv", [128, 2, H * 128])
        rope = sb("rope", [QK, 2, T])
        mats = sb("mats", [128, 6, 128])
        modT = sb("modT", [128, 48, 9])
        amod = sb("amod", [128, 2, 8, 9])
        gT = sb("gT", [128, N_GAIN])
        epsc = sb("epsc", [128, 1])
        cext = sb("cext", [128, 512])
        wtok = sb("wtok", [128, 5, 8])
        psA = ctx.enter_context(nc.psum_tensor("psA", [128, 2, 2, 512], F32))
        psV = ctx.enter_context(nc.psum_tensor("psV", [128, 2, 2, 512], F32))

        ident, flip, ones = mats[:, 0, :], mats[:, 1, :], mats[:, 2, :]
        block64, block96, rot96 = mats[:, 3, :], mats[0:QK, 4, 0:QK], mats[0:QK, 5, 0:QK]
        qcat, kcat, qz = wide[:, 0:8, :], wide[:, 8:16, :], wide[:, 16:24, :]
        wflat = wide[:].rearrange("p a t -> p (a t)")
        ada9, bada9 = wflat[0:9, 0:6144], wflat[0:9, 6144:12288]
        xtok = hT[:].rearrange("p a t -> p (a t)")[:, 0:4096].rearrange("p (t d) -> p t d", t=4)
        xs9 = qiz[:].rearrange("p a t -> p (a t)")
        xsam, cin, csil, gin = xs9[0:8, 0:1024], xs9[0:9, 1024:2048], xs9[0:9, 2048:3072], xs9[0:N_GAIN, 3072:3200]
        cT = r1[:, 8000:8072].rearrange("p (k c) -> p k c", k=8)
        sqx = r1[:, 0:KD * T].rearrange("p (k t) -> p k t", k=KD)
        sq = r1[:, 0:4 * T].rearrange("p (k t) -> p k t", k=4)
        raw = r1[:, 4 * T:6 * T].rearrange("p (k t) -> p k t", k=2)
        sd = r1[:, 8 * T:10 * T].rearrange("p (k t) -> p k t", k=2)
        wuq = r1[:, 10 * T:10 * T + 2304].rearrange("p (k n) -> p k n", k=3)

        qlatT = wflat[:, 8 * T:11 * T].rearrange("p (k t) -> p k t", k=3)
        rtmp = r1[:, 6 * T:7 * T]
        halves = lambda ap: ap.rearrange("p (h t) -> p h t", h=2)

        nA = 0
        A_XT = [nA + i for i in range(7)]; nA += 7
        A_MOD = nA; nA += 1
        A_SS = nA; nA += 1
        A_proj, A_norm, V_rot = {}, {}, {}
        nV = 24
        for i in range(len(U) + 2):
            if i < len(U):
                A_proj[i] = [nA + t for t in range(U[i][1])]
                nA += U[i][1]
            if 1 <= i <= len(U) and kind(U[i - 1][0]) in NORMED:
                A_norm[i - 1] = nA; nA += 1
            if i >= 2 and kind(U[i - 2][0]) in ROPED:
                V_rot[i - 2] = nV; nV += 1
        A_TOK = nA; nA += 5
        A_WT = nA; nA += 1
        IQ = [(qt, h) for qt in range(1, 4) for h in range(H)]
        A_IQ = nA; nA += len(IQ)
        V_BIAS = nV; nV += 3
        A_VM = nA; nA += 4
        A_QS = nA; nA += 1
        V_KN = nV; nV += 1
        V_WC = nV; nV += 2
        A_IP = nA; nA += 16
        V_IS = nV; nV += 1
        V_ISW = nV; nV += 1
        AT = [(g, qt, h) for g in range(2) for qt in range(4) for h in range(H)]
        A_PT, V_S = nA, nV
        nA += len(AT); nV += len(AT)
        V_BF = nV; nV += 3
        A_LT, V_KX = nA, nV
        nA += NB * NPG; nV += NB * NPG
        A_OL = nA; nA += 1
        V_OV = nV; nV += 1
        A_KD, V_SD = nA, nV
        nA += 4 * NB; nV += 2
        V_SN = nV; nV += 1
        A_PD = nA; nA += 3
        A_OD = nA; nA += 1
        A_MIX = nA; nA += 2
        V_OUT = nV; nV += 8
        A_SS2 = nA; nA += 1
        PADA, PADV = nA % 2, nV % 2
        nA += PADA; nV += PADV
        A_G, V_U = nA, nV
        nA += KF; nV += KF
        V_DN = nV; nV += 8
        A_Y = nA; nA += 5
        win_tiles = [(i, t) for i in range(15) for t in range(U[i][1])]

        rb = r1[:, 0:1024].rearrange("p (s n) -> p s n", s=2)
        vm = r1[:, 1024:3072].rearrange("p (t n) -> p t n", t=4)
        sS = r1[:, 3072:4608].rearrange("p (s n) -> p s n", s=3)
        sP = r1[:, 4608:6144].rearrange("p (s n) -> p s n", s=3)
        sPT = r1[:, 6144:7680].rearrange("p (s n) -> p s n", s=3)
        ohn, g8, rbias = r1[0:32, 3072:3456], r1[0:8, 3456:3840], r1[0:32, 3840:3848]
        stat = sb("stat", [128, 3, 4])
        gated = sb("gated", [128, 2, 8])
        top8 = sb("top8", [128, 8])
        trev, toep = wring[:, 0:2048], wring[:, 2050:4098]
        sc8 = wring[0:NB, 0:PAST + 1]
        ip = r1[:, 3848:5896].rearrange("p (s n) -> p s n", s=2)
        kiT = r1[:, 0:1024].rearrange("p (s n) -> p s n", s=2)
        irel = r1[:, 6144:7168]
        w1 = r1[:, 7168:8320]
        sel = sb("sel", [128, 192])
        selb = sb("selb", [NB, 128])
        ptab = sb("ptab", [128, NB], I32)
        rows_of = sb("rows_of", [128, NB], mybir.dt.uint32)
        wz = sb("wz", [128, 64])
        small = sb("small", [128, 64])
        rb64 = sb("rb64", [NBUCK, 64])
        qd = sb("qd", [128, 64])
        qdz = sb("qdz", [128, 576])
        ropeflat = rope[:].rearrange("p a t -> p (a t)")
        knew, pnsq = ropeflat[0:NB, 0:512], ropeflat[0:NB, 512:1024]
        ssnew = sb("ssnew", [NB, 8])
        qflat = qiz[:].rearrange("p a t -> p (a t)")
        bm64, s64, ohf = qflat[0:64, 0:2049], qflat[0:64, 2049:4098], qflat[0:32, 2049:4098]
        qs8 = r1[0:NB, 3072:3840]
        qbc = r1[:, 0:6144].rearrange("p (b h d) -> p b h d", b=NB, h=H)
        rp = r1[:, 6144:8192].rearrange("p (s j h d) -> p s j h d", s=2, j=4, h=H)
        pgs = wflat[:, 0:9216].rearrange("p (s j n) -> p s j n", s=2, j=NPG)
        lT = wflat[:, 9216:9728].rearrange("p (s k n) -> p s k n", s=2, k=2)
        pr = wflat[:, 9728:10752].rearrange("p (s n) -> p s n", s=2)
        sqk = wflat[:, 10752:11776].rearrange("p (s n) -> p s n", s=2)
        ol = wflat[0:8, 11776:12288]
        m8 = lambda x: msk[:, x * 136:(x + 1) * 136].rearrange("p (j h) -> p j h", h=8)
        dots, sums, sfull, pm = [m8(0), m8(1)], [m8(2), m8(3)], [m8(4), m8(5)], [m8(6), m8(7)]
        newp = krF[0:NB, 0:512].rearrange("p (h d) -> p h d", h=H)
        onlyc = sb("onlyc", [128, NB])
        drope = [vT[:, x * 136:(x + 1) * 136].rearrange("p (j h) -> p j h", h=8) for x in range(2)]
        hstat = sb("hstat", [128, 4, 8])
        kdT = wring[:, 3072:4096].rearrange("p (s n) -> p s n", s=2)
        ptd = wring[:, 4096:5184].rearrange("p (j r) -> p j r", j=17)
        ptb = wring[:, 5184:5456].rearrange("p (s j h) -> p s j h", s=2, j=17)
        olb = r1[0:8, 0:2048].rearrange("p (b r) -> p b r", b=NB)
        olT = wflat[:, 11776:11904].rearrange("p (k r) -> p k r", k=2)
        kvp = wflat[:, 0:8192].rearrange("p (s j n) -> p s j n", s=2, j=NPG)
        od = wflat[0:8, 8192:9216].rearrange("p (b n) -> p b n", b=NB)
        odT = wflat[:, 9216:9280].rearrange("p (b h) -> p b h", b=NB)
        q_rows = nc.dram_tensor("q_rows", [NB, 768], F32, kind="Internal").ap()
        mask_rows = nc.dram_tensor("mask_rows", [NB, PAST + 1], F32, kind="Internal").ap()
        toepv = toep.rearrange("p (h n) -> p h n", h=H)
        mixT = hT
        bias_rows = nc.dram_tensor("bias_rows", [8, 384], F32, kind="Internal").ap()
        MQ = {1: (0, 256), 2: (256, 640), 3: (640, 1152)}
        actT = wide[:, 0:KF, :]
        yt = hT[:].rearrange("p a t -> p (a t)")[:, 0:2048].rearrange("p (s n) -> p s n", s=2)
        SPLIT, NT = 4, 8 + 2 * KF
        r1_r, wring_r = rounded("r1", [128, 8320]), rounded("wring", [128, 5632])
        hT_r, qiz_r, wide_r = rounded("hT", [128, KD, T]), rounded("qiz", [128, 8, T]), rounded("wide", [128, 24, T])
        tok_r, wukv_r = rounded("tok", [128, 5 * 608]), rounded("wukv", [128, 2 * H * 128])
        latT_r, kT_r, vT_r = rounded("latT", [128, 2, T]), rounded("kT", [128, T]), rounded("vT", [128, T])
        wraw = [wring[:, s * 1024:(s + 1) * 1024] for s in range(SPLIT)]
        wlow = [wring_r[:, s * 1024:(s + 1) * 1024] for s in range(SPLIT)]
        whigh = [r1_r[:, 5200 + s * 1024:6224 + s * 1024] for s in range(3)] + [wring_r[:, 4096:5120]]
        WD = KF // 2 * 128
        draw = [wring[:, s * WD:(s + 1) * WD] for s in range(SPLIT)]
        dlow = [wring_r[:, s * WD:(s + 1) * WD] for s in range(SPLIT)]
        qizflat_r = qiz_r[:].rearrange("p a t -> p (a t)")
        dhigh = [qizflat_r[:, 0:WD], qizflat_r[:, WD:2 * WD], r1_r[:, 5200:5200 + WD], r1_r[:, 5200 + WD:5200 + 2 * WD]]
        xhigh, xlow = qiz_r, hT_r
        alow = wide_r
        ahigh = ([r1_r[:, k * T:(k + 1) * T] for k in range(8)] + [wide_r[:, 22 + k, :] for k in range(2)] +
                 [tok_r[:, k * T:(k + 1) * T] for k in range(5)] + [wukv_r[:, k * T:(k + 1) * T] for k in range(3)] +
                 [latT_r[:, k, :] for k in range(2)] + [kT_r[:], vT_r[:]])
        pieces = lambda w: w.rearrange("p (k n) -> p k n", n=128)

        sa = lambda n: psA[:, n % 2]
        sv = lambda n: psV[:, n % 2]
        a_full, a_free, v_full, v_free = sem("a_full"), sem("a_free"), sem("v_full"), sem("v_free")
        in_loaded, const_loaded, bada_loaded, wres_loaded = sem("in_loaded"), sem("const_loaded"), sem("bada_loaded"), sem("wres_loaded")
        ada_w = [sem(f"ada_w{s}") for s in range(2)]
        win_w = [sem(f"win_w{s}") for s in range(4)]
        c_silu, eps_set, amod_done, hT_scaled, hT_done = sem("c_silu"), sem("eps_set"), sem("amod_done"), sem("hT_scaled"), sem("hT_done")
        zeroed, norm_done, rope_done, dve_chain, act_chain = sem("zeroed"), sem("norm_done"), sem("rope_done"), sem("dve_chain"), sem("act_chain")
        kr_spread, tokens_stored = sem("kr_spread"), sem("tokens_stored")
        sq_written = sem("sq_written")
        idx_acc, bias_loaded, bias_out, trev_loaded, toep_done = sem("idx_acc"), sem("bias_loaded"), sem("bias_out"), sem("trev_loaded"), sem("toep_done")
        mask_done, stats_ready, exp_done, p_ready, pv_done, o_free = (sem(x) for x in ("mask_done", "stats_ready", "exp_done", "p_ready", "pv_done", "o_free"))
        mixed, sq2_written, x_new, h2_scaled, h2_done = (sem(x) for x in ("mixed", "sq2_written", "x_new", "h2_scaled", "h2_done"))
        y_stored = [sem(f"y_stored{s}") for s in range(2)]
        ptab_loaded, qs_gained, qs_out, qbc_loaded, w1_ready, irel_ready, wz_ready, pn_ready = (sem(x) for x in (
            "ptab_loaded", "qs_gained", "qs_out", "qbc_loaded", "w1_ready", "irel_ready", "wz_ready", "pn_ready"))
        far_loaded, mask_out, mask_back, top_done, bm_ready = (sem(x) for x in ("far_loaded", "mask_out", "mask_back", "top_done", "bm_ready"))
        idx_pages = [sem(f"idx_pages{x}") for x in range(2)]
        mla_pages = [sem(f"mla_pages{x}") for x in range(2)]
        kv_rows = [sem(f"kv_rows{x}") for x in range(2)]
        squared, page_sums, rope_mul, rope_sum, ss_ready, rstd_in = (sem(x) for x in ("squared", "page_sums", "rope_mul", "rope_sum", "ss_ready", "rstd_in"))
        smax, gmax, shifted, p_exp, psum_ready, gsum, pm_ready = (sem(x) for x in ("smax", "gmax", "shifted", "p_exp", "psum_ready", "gsum", "pm_ready"))
        lat_pv, lat_out, s64_ready, p64_exp, p64_ready, ptb_ready, d_pv, d_out = (sem(x) for x in (
            "lat_pv", "lat_out", "s64_ready", "p64_exp", "p64_ready", "ptb_ready", "d_pv", "d_out"))
        rows_ready = sem("rows_ready")
        mix_s, neg_set, new_sums = sem("mix_s"), sem("neg_set"), sem("new_sums")
        tail_w = [sem(f"tail_w{s}") for s in range(4)]
        down_w = [sem(f"down_w{s}") for s in range(4)]
        down_used, w_high, w_split, x_high, x_split, a_high, a_split = (sem(x) for x in ("down_used", "w_high", "w_split", "x_high", "x_split", "a_high", "a_split"))
        normed = [i for i in range(len(U)) if kind(U[i][0]) in NORMED]
        roped = [i for i in range(len(U)) if kind(U[i][0]) in ROPED]
        UI = {U[i][0]: i for i in range(len(U))}

        def gain_col(name, t):
            k = kind(name)
            c = {"qlat": G_QL + t, "kvlat": G_KVL + t, "krope": G_KR, "q": G_DQ, "k": G_DK, "qc": G_Q, "kn": G_KN}[k]
            return c

        def sp_program(sp):
            for t in range(4):
                sp.dma_start(xtok[:, t, :], a["x_prompt"][0, t * 128:(t + 1) * 128, :]).then_inc(in_loaded, 16)
            sp.dma_start(xsam, a["x_sample"][:, 0, :]).then_inc(in_loaded, 16)
            sp.dma_start(cin[0:1, :], a["c_prompt"]).then_inc(in_loaded, 16)
            sp.dma_start(cin[1:9, :], a["c_sample"]).then_inc(in_loaded, 16)
            sp.wait_ge(eps_set, 1)
            row = lambda name: a[name].rearrange("l (k n) -> (l k) n", n=128)
            for c, name, n in ((G_MIX, "g_norm_mix", 8), (G_FFN, "g_norm_ffn", 8), (G_OUT, "g_out", 8),
                               (G_QL, "g_q_lat", 3), (G_KVL, "g_kv_lat", 2)):
                sp.dma_start(gin[c:c + n, :], row(name)).then_inc(in_loaded, 16)
            for c, o0, name in ((G_Q, 0, "g_mla_q_nope"), (G_Q, 64, "g_mla_q_rope"), (G_KN, 0, "g_mla_k_nope"),
                                (G_KN, 64, "g_mla_k_rope"), (G_DQ, 0, "g_dsa_q"), (G_DQ, 64, "g_dsa_q"),
                                (G_DK, 0, "g_dsa_k"), (G_DK, 64, "g_dsa_k")):
                n = a[name].shape[1]
                sp.dma_start(gin[c:c + 1, o0:o0 + n], a[name]).then_inc(in_loaded, 16)
            sp.dma_start(mats[:], a["k_mats"]).then_inc(in_loaded, 16)
            sp.dma_start(bada9, a["b_ada"].broadcast_to([9, 6144])).then_inc(bada_loaded, 16)
            wada = a["w_ada"][0].rearrange("(k p) n -> p k n", p=128)
            aslot = lambda s: wring[:, s * 2048:(s + 1) * 2048].rearrange("p (k n) -> p k n", k=KD)
            for s in range(2):
                sp.dma_start(aslot(s), wada[:, :, s * 256:(s + 1) * 256]).then_inc(ada_w[s], 16)
            sp.dma_start(rope[:], a["k_rope"]).then_inc(const_loaded, 16)
            sp.dma_start(cext[:], a["k_cext"]).then_inc(const_loaded, 16)
            sp.dma_start(sel[:], a["k_sel"]).then_inc(const_loaded, 16)
            sp.dma_start(selb[:], a["k_selb"]).then_inc(const_loaded, 16)
            sp.dma_start(onlyc[:], a["k_only"]).then_inc(const_loaded, 16)
            for r in range(8):
                sp.dma_start(ptab[r:128:8, :], bass.AP(a["page_table"].tensor, 0, [[1, NPG], [NPG, NB]]),
                             allow_slow_non_contiguous=True).then_inc(ptab_loaded, 16)
            with sp.Fori(1, 12) as i:
                for s in range(2):
                    sp.wait_ge(v_full, i * 2 + (s - 1))
                    sp.dma_start(aslot(s), wada[:, :, bass.ds(i * 512 + s * 256, 256)]).then_inc(ada_w[s], 16)
            sp.wait_ge(a_full, A_SS + 1)
            sp.dma_start(wuq, a["w_uq"][0].rearrange("(k p) h d -> p k (h d)", p=128)).then_inc(wres_loaded, 16)
            sp.dma_start(wukv[:], a["w_ukv"][0].rearrange("(k p) h d -> p k (h d)", p=128)).then_inc(wres_loaded, 16)
            win = a["w_in"][0].rearrange("(k p) n -> p k n", p=128)
            sp.wait_ge(v_full, 24)
            for n, (i, t) in enumerate(win_tiles):
                if n >= 4:
                    pi, pt = win_tiles[n - 4]
                    sp.wait_ge(a_full, A_proj[pi][pt] + 1)
                dst = wring[:, (n % 4) * 1024:(n % 4 + 1) * 1024].rearrange("p (k n) -> p k n", k=KD)
                name = U[i][0]
                k = kind(name)
                j = int(name[-1]) if name[-1].isdigit() else 0
                if k == "q":
                    parts = [(0, C_Q + j * 64, 64), (64, C_Q + (j + 4) * 64, 64)]
                elif k == "kidx":
                    parts = [(0, C_KI, 64), (64, C_KI, 64)]
                else:
                    c = {"qlat": t * 128, "v": C_V, "kvlat": C_KV + t * 128, "krope": C_KR - 64, "k": C_K,
                         "qi": C_QI + j * 128, "widx": C_WI}[k]
                    parts = [(0, c, U[i][2])]
                for d0, c0, w in parts:
                    for kk in range(0, KD, 4):
                        sp.dma_start(dst[:, kk:kk + 4, d0:d0 + w], win[:, kk:kk + 4, c0:c0 + w]).then_inc(win_w[n % 4], 16)

            sp.wait_ge(norm_done, len(normed))
            sp.wait_ge(a_free, A_WT + 1)
            sp.dma_start(ohn, a["k_onehot"][:, 0:384]).then_inc(bias_loaded, 16)
            sp.dma_start(rbias, a["rel_bias"]).then_inc(bias_loaded, 16)
            sp.wait_ge(v_free, V_BIAS + 1)
            sp.dma_start(bias_rows, g8).then_inc(bias_out, 16)
            sp.wait_ge(bias_out, 16)
            sp.dma_start(trev.rearrange("p (h n) -> p h n", h=H),
                         bass.AP(bias_rows.tensor, 0, [[1, 128], [384, 8], [1, 256]])).then_inc(trev_loaded, 16)
            sp_decode(sp)
            self_sp_tail(sp)

        class Link:

            def __init__(self, v):
                self.v, self.n, self.turn = v, 0, None

            def __call__(self, ins):
                self.n += 1
                ins.then_inc(dve_chain, 1)
                self.v.wait_ge(dve_chain, self.n if self.turn is None else self.turn * PER_TURN + self.n)

            def per_loop(self, i, start, body):
                first = self.n
                self.turn, self.n = i, first - start * PER_TURN
                body()
                assert self.n - (first - start * PER_TURN) == PER_TURN, self.n - (first - start * PER_TURN)
                self.first = first

            def after_loop(self, turns=3):
                self.turn, self.n = None, self.first + turns * PER_TURN

        def at(b, k, c):
            if isinstance(b, tuple):
                return b[0] * (2 * k) + (b[1] * k + c)
            return b * k + c

        def sp_decode(sp):
            sp.wait_ge(a_free, A_QS + 1)
            sp.dma_start(q_rows, qs8).then_inc(qs_out, 16)
            sp.wait_ge(pn_ready, 1)
            sp.wait_ge(w1_ready, 5)
            sp.dma_start(ohf, a["k_onehot"][:, 384:384 + PAST + 1]).then_inc(far_loaded, 16)
            sp.wait_ge(qs_out, 16)
            sp.wait_ge(o_free, len(AT) // 2)
            sp.wait_ge(p_ready, len(AT))
            sp.dma_start(qbc.rearrange("p b h d -> p (b h d)"),
                         bass.AP(q_rows.tensor, 0, [[0, 128], [1, NB * 768]])).then_inc(qbc_loaded, 16)
            sp.wait_ge(top_done, 1)
            sp.dma_start(mask_rows, sc8).then_inc(mask_out, 16)
            sp.wait_ge(mask_out, 16)
            sp.wait_ge(v_free, V_BF + 3)
            sp.dma_start(s64, bass.AP(mask_rows.tensor, 0, [[PAST + 1, NB], [0, 8], [1, PAST + 1]])).then_inc(mask_back, 16)

        def self_sp_tail(sp):
            wo = a["w_out"][0].rearrange("(k p) n -> p k n", p=128)
            wf = a["w_ffn_in"][0].rearrange("(k p) n -> p k n", p=128)
            wd = a["w_ffn_out"][0].rearrange("(k p) n -> p k n", p=128)

            def load(s, src, col):
                sp.dma_start(pieces(wraw[s]), src[:, :, bass.ds(col, 128)]).then_inc(tail_w[s], 16)

            sp.wait_ge(p_ready, len(AT))
            for s in range(3):
                load(s, wo, s * 128)
            sp.wait_ge(v_full, V_SD + 2)
            load(3, wo, 3 * 128)
            for n in range(4, 8):
                sp.wait_ge(v_full, V_OUT + n - 3)
                load(n % 4, wo, n * 128)
            for n in range(4):
                sp.wait_ge(v_full, V_OUT + n + 5)
                load(n, wf, (n % 2) * DFF + n // 2 * 128)
            with sp.Fori(1, KF // 2) as i:
                for s in range(4):
                    if s % 2 == 0:
                        sp.wait_ge(a_full, i * 2 + (A_G + s // 2 - 1))
                    else:
                        sp.wait_ge(v_full, i * 2 + (V_U + s // 2 - 1))
                    load(s, wf, i * 256 + ((s % 2) * DFF + s // 2 * 128))

            def load_down(s, m, half):
                sp.dma_start(pieces(draw[s]), wd[:, half * (KF // 2):(half + 1) * (KF // 2), bass.ds(m, 128)]).then_inc(down_w[s], 16)

            for s, full in enumerate((KF - 1, KF, KF, KF)):
                sp.wait_ge(v_full, V_U + full)
                load_down(s, s // 2 * 128, s % 2)
            with sp.Fori(1, 4) as i:
                for s in range(4):
                    if s % 2 == 0:
                        sp.wait_ge(down_used, i * 2 + (s // 2 - 1))
                    else:
                        sp.wait_ge(v_full, i * 2 + (V_DN + s // 2 - 1))
                    load_down(s, i * 256 + s // 2 * 128, s % 2)
            for t in range(5):
                w = 128 if t < 4 else NB
                sp.wait_ge(a_free, A_Y + t + 1)
                dst = o["y_p"][0, t * 128:(t + 1) * 128, :] if t < 4 else o["y_s"][:, 0, :]
                sp.dma_start(dst, yt[0:w, t % 2, :]).then_inc(y_stored[t % 2], 16)
            sp.wait_ge(y_stored[0], 48)
            sp.wait_ge(y_stored[1], 32)

        def win_count(n):
            c = 0
            for m in range(n % 4, n + 1, 4):
                k = kind(U[win_tiles[m][0]][0])
                c += 4 if k in ("q", "kidx") else 2
            return 16 * c

        def pe_program(pe):
            def sumsq(job, src, need, count):
                if job >= 2:
                    pe.wait_ge(a_free, job - 1)
                pe.wait_ge(need, count)
                for hf in range(2):
                    for k in range(KD):
                        mm = pe.matmul(sa(job)[:, hf, 0:HT], ones, src[:, k, hf * HT:(hf + 1) * HT],
                                       start=(k == 0), stop=(k == KD - 1))
                mm.then_inc(a_full, 1)

            pe.wait_ge(in_loaded, 16 * 21)
            for j, n in enumerate(A_XT):
                if n >= 2:
                    pe.wait_ge(a_free, n - 1)
                out = sa(n).rearrange("p b n -> p (b n)")
                if j < 4:
                    for k in range(KD):
                        mm = pe.transpose(out[:, k * 128:(k + 1) * 128], xtok[:, j, k * 128:(k + 1) * 128], ident)
                elif j == 4:
                    for k in range(KD):
                        mm = pe.transpose(out[:, k * 8:k * 8 + 8], xsam[:, k * 128:(k + 1) * 128], ident[0:8, 0:8])
                elif j == 5:
                    pe.wait_ge(c_silu, 1)
                    for k in range(KD):
                        mm = pe.transpose(out[:, k * 9:k * 9 + 9], csil[:, k * 128:(k + 1) * 128], ident[0:9, 0:9])
                else:
                    mm = pe.transpose(out[:, 0:N_GAIN], gin, ident[0:N_GAIN, 0:N_GAIN])
                mm.then_inc(a_full, 1)
            pe.wait_ge(a_free, A_XT[5] + 1)

            def ada_chunk(s, loads, n=None):
                pe.wait_ge(ada_w[s], loads)
                if n is not None:
                    pe.wait_ge(v_free, n)
                w = wring[:, s * 2048:(s + 1) * 2048].rearrange("p (k n) -> p k n", k=KD)
                for k in range(KD):
                    mm = pe.matmul(psV[0:9, s, 0, 0:256], cT[:, k, :], w[:, k, :], start=(k == 0), stop=(k == KD - 1))
                mm.then_inc(v_full, 1)

            ada_chunk(0, 16)
            ada_chunk(1, 16)
            with pe.Fori(1, 12) as i:
                for s in range(2):
                    ada_chunk(s, i * 16 + 16, i * 2 + (s - 1))
            pe.wait_ge(a_free, A_MOD - 1)
            pe.wait_ge(v_free, 24)
            for m in range(48):
                mm = pe.transpose(sa(A_MOD)[:, 0, m * 9:m * 9 + 9], ada9[:, m * 128:(m + 1) * 128], ident[0:9, 0:9])
            mm.then_inc(a_full, 1)
            sumsq(A_SS, sqx, sq_written, 8)

            pe.wait_ge(hT_done, 9)
            wn = 0
            for i in range(len(U) + 2):
                if i < len(U):
                    name, nt, rows = U[i]
                    k = kind(name)
                    j = int(name[-1]) if name[-1].isdigit() else 0
                    for t in range(nt):
                        n = A_proj[i][t]
                        pe.wait_ge(a_free, n - 1)
                        if i < 15:
                            pe.wait_ge(win_w[wn % 4], win_count(wn))
                            w = wring[:, (wn % 4) * 1024:(wn % 4 + 1) * 1024].rearrange("p (k n) -> p k n", k=KD)
                            wn += 1
                            src, nk = hT, KD
                            lhs = lambda kk: w[:, kk, 0:rows]
                        elif k == "qc":
                            pe.wait_ge(wres_loaded, 32)
                            pe.wait_ge(norm_done, normed.index(UI["qlat"]) + 1)
                            src, nk = qlatT, 3
                            lhs = lambda kk: wuq[:, kk, j * QK:(j + 1) * QK]
                        else:
                            pe.wait_ge(norm_done, normed.index(UI["kvlat"]) + 1)
                            src, nk = latT, 2
                            lhs = lambda kk: wukv[:, kk, j * 128:j * 128 + 64]
                        for kk in range(nk):
                            for hf in range(2):
                                mm = pe.matmul(sa(n)[0:rows, hf, 0:HT], lhs(kk), src[:, kk, hf * HT:(hf + 1) * HT],
                                               start=(kk == 0), stop=(kk == nk - 1), skip_group_check=True)
                        mm.then_inc(a_full, 1)
                if i - 1 in A_norm:
                    name, nt, rows = U[i - 1]
                    k = kind(name)
                    n = A_norm[i - 1]
                    pe.wait_ge(a_free, max(n - 1, A_proj[i - 1][-1] + 1))
                    blk = {"qlat": ones, "kvlat": ones, "krope": block96, "qc": block96, "q": block64, "k": block64,
                           "kn": block96[0:64, 0:64]}[k]
                    for hf in range(2):
                        for t in range(nt):
                            s = SQ[i - 1] + t
                            mm = pe.matmul(sa(n)[0:rows, hf, 0:HT], blk, sq[0:rows, s % 4, hf * HT:(hf + 1) * HT],
                                           start=(t == 0), stop=(t == nt - 1))
                    mm.then_inc(a_full, 1)
                if i - 2 in V_rot:
                    n = V_rot[i - 2]
                    pe.wait_ge(v_free, n - 1)
                    pe.wait_ge(norm_done, normed.index(i - 2) + 1)
                    src = krF[:] if U[i - 2][0] == "krope" else qcat[0:QK, int(U[i - 2][0][-1]), :]
                    for hf in range(2):
                        mm = pe.matmul(sv(n)[0:QK, hf, 0:HT], rot96, src[:, hf * HT:(hf + 1) * HT], start=True, stop=True)
                    mm.then_inc(v_full, 1)
            pe.wait_ge(rope_done, 1)
            pe.wait_ge(norm_done, len(normed))
            for t in range(5):
                n = A_TOK + t
                pe.wait_ge(a_free, n - 1)
                c, w = t * 128, (128 if t < 4 else NB)
                for k in range(2):
                    pe.transpose(sa(n)[0:w, 0, k * 128:(k + 1) * 128], latT[:, k, c:c + w], ident)
                pe.transpose(sa(n)[0:w, 0, 256:256 + QK], krF[:, c:c + w], ident[0:QK, 0:QK])
                for j, src in enumerate((kT, vT, kidxT)):
                    mm = pe.transpose(sa(n)[0:w, 1, j * 128:(j + 1) * 128], src[:, c:c + w], ident)
                mm.then_inc(a_full, 1)
            n = A_WT
            pe.wait_ge(a_free, n - 1)
            for t in range(5):
                w = 128 if t < 4 else NB
                mm = pe.transpose(sa(n)[0:w, 0, t * 8:t * 8 + 8], widxT[:, t * 128:t * 128 + w], ident[0:8, 0:8])
            mm.then_inc(a_full, 1)

            for j, (qt, h) in enumerate(IQ):
                n = A_IQ + j
                pe.wait_ge(a_free, n - 1)
                mm = pe.matmul(sa(n)[:, 0, 0:(qt + 1) * 128], qiz[:, h, qt * 128:(qt + 1) * 128],
                               kidxT[:, 0:(qt + 1) * 128], start=True, stop=True)
                mm.then_inc(a_full, 1)
            pe.wait_ge(bias_loaded, 32)
            pe.wait_ge(v_free, V_BIAS - 1)
            pe.matmul(sv(V_BIAS)[0:8, 0, 0:384], rbias, ohn, start=True, stop=True).then_inc(v_full, 1)
            for t in range(4):
                n = A_VM + t
                pe.wait_ge(a_free, n - 1)
                for k in range(2):
                    mm = pe.matmul(sa(n)[:, 0, :], latT[:, k, t * 128:(t + 1) * 128],
                                   wukv[:, k, :].rearrange("p (h d) -> p h d", h=H)[:, :, 64:128], start=(k == 0), stop=(k == 1))
                mm.then_inc(a_full, 1)
            pe.wait_ge(trev_loaded, 16)
            for j in range(2):
                n = V_BIAS + 1 + j
                pe.wait_ge(v_free, n - 1)
                for b in range(2):
                    c = j * 1024 + b * 512
                    mm = pe.matmul(sv(n)[:, b, :], flip, trev[:, c:c + 512], start=True, stop=True)
                mm.then_inc(v_full, 1)
            pe.wait_ge(kr_spread, 1)
            pe.wait_ge(rope_done, len(roped))
            n = A_QS
            pe.wait_ge(a_free, n - 1)
            pe.wait_ge(qs_gained, 1)
            for h in range(H):
                mm = pe.transpose(sa(n)[0:NB, h // 4, (h % 4) * QK:(h % 4 + 1) * QK], qcat[0:QK, h, SEQ:T], ident[0:QK, 0:QK])
            mm.then_inc(a_full, 1)
            pe.wait_ge(v_free, V_KN - 1)
            for k in range(2):
                mm = pe.matmul(sv(V_KN)[0:NB, 0, :], latT[:, k, SEQ:T],
                               wukv[:, k, :].rearrange("p (h d) -> p h d", h=H)[:, :, 0:64], start=(k == 0), stop=(k == 1))
            mm.then_inc(v_full, 1)
            pe.wait_ge(const_loaded, 80)
            pe.wait_ge(v_free, V_WC - 1)
            pe.matmul(sv(V_WC)[:, 0, 0:8], selb[:], wtok[0:NB, 4, :], start=True, stop=True).then_inc(v_full, 1)
            pe.wait_ge(v_free, V_WC)
            pe.wait_ge(pn_ready, 1)
            for h in range(H):
                mm = pe.matmul(sv(V_WC + 1)[0:NB, 0, h:h + 1], irel[:, h * 8:h * 8 + 8], ones[:, 0:1], start=True, stop=True,
                               skip_group_check=True)
            mm.then_inc(v_full, 1)
            pe.wait_ge(w1_ready, 5)

            def idx_product(n):
                b, g = divmod(n, 2)
                pe.wait_ge(a_free, A_IP + n + 1)
                return pe.matmul(sv(V_IS)[:, g, :], w1[:, b * 128:(b + 1) * 128], kiT[:, n % 2, :], start=(b == 0), stop=(b == 7),
                                 skip_group_check=True)

            for x in range(17):
                if x < 16:
                    b, g = divmod(x, 2)
                    pe.wait_ge(idx_pages[b % 2], 16 * (b // 2 + 1))
                    pe.wait_ge(a_free, A_IP + x - 1)
                    for y in range(4):
                        c = g * 512 + y * 128
                        mm = pe.transpose(sa(A_IP + x)[:, 0, y * 128:(y + 1) * 128], ip[:, b % 2, c:c + 128], ident)
                    mm.then_inc(a_full, 1)
                if x == 1:
                    pe.wait_ge(v_free, V_IS - 1)
                if x >= 1:
                    mm = idx_product(x - 1)
            mm.then_inc(v_full, 1)
            pe.wait_ge(irel_ready, 1)
            pe.wait_ge(wz_ready, 1)
            pe.wait_ge(v_free, V_ISW - 1)
            for g in range(2):
                mm = pe.matmul(sv(V_ISW)[0:64, g, :], wz[:], irel[:, g * 512:(g + 1) * 512], start=True, stop=True)
            mm.then_inc(v_full, 1)
            NA = len(AT)
            for u in range(NA + 2):
                if u < NA:
                    g, qt, h = AT[u]
                    n, qs, W = V_S + u, slice(qt * 128, (qt + 1) * 128), (qt + 1) * 128
                    pe.wait_ge(v_free, n - 1)
                    lhs, rhs = (qcat[0:QK, h, qs], kcat[0:QK, h, 0:W]) if g == 0 else (qz[:, h, qs], kT[:, 0:W])
                    pe.matmul(sv(n)[:, 0, 0:W], lhs, rhs, start=True, stop=True).then_inc(v_full, 1)
                if 1 <= u <= NA:
                    g, qt, h = AT[u - 1]
                    n = A_PT + u - 1
                    pe.wait_ge(a_free, n - 1)
                    pe.wait_ge(p_ready, u)
                    for kt in range(qt + 1):
                        mm = pe.transpose(sa(n)[:, 0, kt * 128:(kt + 1) * 128], sP[:, (u - 1) % 3, kt * 128:(kt + 1) * 128], ident)
                    mm.then_inc(a_full, 1)
                if u >= 2:
                    g, qt, h = AT[u - 2]
                    pair, p0 = (u - 2) // 2, (h % 2) * 64
                    pe.wait_ge(a_free, A_PT + u - 1)
                    if pair >= 2 and h % 2 == 0:
                        pe.wait_ge(o_free, pair - 1)
                    for kt in range(qt + 1):
                        vv = vm[:, kt, h * 64:(h + 1) * 64] if g == 0 else tok[:, kt, 416 + (h // 4) * 64:480 + (h // 4) * 64]
                        mm = pe.matmul(psV[p0:p0 + 64, pair % 2, 1, 0:128], vv, sPT[:, (u - 2) % 3, kt * 128:(kt + 1) * 128],
                                       start=(kt == 0), stop=(kt == qt), skip_group_check=True)
                    mm.then_inc(pv_done, 1)
            pe_decode(pe)
            pe_tail(pe)

        def pe_decode(pe):
            pe.wait_ge(far_loaded, 16)
            pe.wait_ge(pn_ready, 2)
            pe.wait_ge(o_free, len(AT) // 2)
            for x in range(3):
                n = V_BF + x
                pe.wait_ge(v_free, n - 1)
                for b in range(2):
                    c = (x * 2 + b) * 512
                    if c < PAST + 1:
                        w = min(512, PAST + 1 - c)
                        mm = pe.matmul(sv(n)[0:64, b, 0:w], rb64[:], ohf[:, c:c + w], start=True, stop=True)
                mm.then_inc(v_full, 1)

            def turn(b, par, j):
                n = A_LT + j
                pe.wait_ge(a_free, at(b, NPG, n - 1))
                for k in range(2):
                    mm = pe.transpose(sa(n)[:, 0, k * 128:(k + 1) * 128], pgs[:, par, j, k * 128:(k + 1) * 128], ident)
                mm.then_inc(a_full, 1)

            def expand(b, j):
                n = V_KX + j
                pe.wait_ge(a_free, at(b, NPG, A_LT + j + 1))
                pe.wait_ge(v_free, at(b, NPG, n - 1))
                for k in range(2):
                    mm = pe.matmul(sv(n)[:, 0, :], lT[:, j % 2, k, :], wukv[:, k, :].rearrange("p (h d) -> p h d", h=H)[:, :, 0:64],
                                   start=(k == 0), stop=(k == 1), skip_group_check=True)
                mm.then_inc(v_full, 1)

            def pages(b, par, loads, prev=None):
                pe.wait_ge(mla_pages[par], loads)
                for j in range(NPG + 1):
                    if j < NPG:
                        turn(b, par, j)
                    if j >= 1:
                        expand(b, j - 1)
                    if j == 11 and prev is not None:
                        weigh(prev, 1 - par)

            def weigh(b, par):
                pe.wait_ge(pm_ready, at(b, 1, 1))
                pe.wait_ge(lat_out, at(b, 1, -1)) if not (isinstance(b, int) and b < 2) else None
                for j in range(NPG + 1):
                    rows = pgs[:, par, j, 0:KVR] if j < NPG else tok[:, 4, 0:KVR]
                    mm = pe.matmul(psV[0:8, par, 1, 0:KVR], pm[par][:, j, :], rows, start=(j == 0), stop=(j == NPG), skip_group_check=True)
                mm.then_inc(lat_pv, 1)

            pages(0, 0, 16)
            pages(1, 1, 16, 0)
            with pe.Fori(1, 4) as i:
                pages((i, 0), 0, i * 16 + 16, (i, -1))
                pages((i, 1), 1, i * 16 + 16, (i, 0))
            weigh(7, 1)
            n = A_OL
            pe.wait_ge(a_free, n - 1)
            pe.wait_ge(lat_out, NB)
            for k in range(2):
                for b in range(NB):
                    c = k * 64 + b * 8
                    mm = pe.transpose(sa(n)[:, 0, c:c + 8], olb[:, b, k * 128:(k + 1) * 128], ident[0:8, 0:8])
            mm.then_inc(a_full, 1)
            pe.wait_ge(a_free, n + 1)
            pe.wait_ge(v_free, V_OV - 1)
            for h in range(H):
                for k in range(2):
                    mm = pe.matmul(sv(V_OV)[(h % 2) * 64:(h % 2) * 64 + 64, 0, (h // 2) * 8:(h // 2) * 8 + 8],
                                   wukv[:, k, h * 128 + 64:(h + 1) * 128], olT[:, k, :].rearrange("p (b h) -> p h b", b=NB)[:, h, :],
                                   start=(k == 0), stop=(k == 1), skip_group_check=True)
            mm.then_inc(v_full, 1)

            def k_turn(b, c4):
                n = A_KD + b * 4 + c4
                pe.wait_ge(kv_rows[b % 2], 16 * (b // 2 + 1))
                pe.wait_ge(a_free, n - 1)
                for x in range(4):
                    mm = pe.transpose(sa(n)[:, 0, x * 128:(x + 1) * 128], kvp[:, b % 2, c4 * 4 + x, 0:128], ident)
                mm.then_inc(a_full, 1)

            def k_product(b, c4):
                n = V_SD + c4 // 2
                if b == 0 and c4 % 2 == 0:
                    pe.wait_ge(v_free, n - 1)
                pe.wait_ge(a_free, A_KD + b * 4 + c4 + 1)
                mm = pe.matmul(sv(n)[0:64, c4 % 2, :], qdz[:, b * 64:(b + 1) * 64], kdT[:, c4 % 2, :], start=(b == 0), stop=(b == 7),
                               skip_group_check=True)
                if b == 7 and c4 % 2 == 1:
                    mm.then_inc(v_full, 1)

            pe.wait_ge(lat_out, NB)
            for x in range(33):
                if x < 32:
                    k_turn(*divmod(x, 4))
                if x >= 1:
                    k_product(*divmod(x - 1, 4))
            pe.wait_ge(v_free, V_SN - 1)
            pe.matmul(sv(V_SN)[0:64, 0, 0:8], qd[:], kT[:, SEQ:T], start=True, stop=True).then_inc(v_full, 1)
            pe.wait_ge(p64_ready, 1)
            for x in range(3):
                n = A_PD + x
                pe.wait_ge(a_free, n - 1)
                if x < 2:
                    for j in range(8):
                        mm = pe.transpose(sa(n)[:, 0, j * 64:(j + 1) * 64], s64[:, (x * 8 + j) * 128:(x * 8 + j + 1) * 128], ident[0:64, 0:64])
                else:
                    mm = pe.transpose(sa(n)[0:NB, 0, 0:64], small[0:64, 0:8], ident[0:64, 0:64])
                mm.then_inc(a_full, 1)

            def d_weigh(b, par, loads):
                pe.wait_ge(kv_rows[par], loads)
                pe.wait_ge(ptb_ready, at(b, 1, 1))
                pe.wait_ge(d_out, at(b, 1, -1)) if not (isinstance(b, int) and b < 2) else None
                for j in range(NPG):
                    pe.matmul(psV[0:8, par, 1, 0:128], ptb[:, par, j, :], kvp[:, par, j, 128:256], start=(j == 0), stop=False, skip_group_check=True)
                pe.matmul(psV[0:8, par, 1, 0:128], ptb[0:NB, par, NPG, :], tok[0:NB, 4, 416:544], start=False, stop=True,
                          skip_group_check=True).then_inc(d_pv, 1)

            d_weigh(0, 0, 80)
            d_weigh(1, 1, 80)
            with pe.Fori(1, 4) as i:
                for par in range(2):
                    d_weigh((i, par), par, i * 16 + 80)
            n = A_OD
            pe.wait_ge(a_free, n - 1)
            pe.wait_ge(d_out, NB)
            for b in range(NB):
                mm = pe.transpose(sa(n)[:, 0, b * 8:b * 8 + 8], od[:, b, :], ident[0:8, 0:8])
            mm.then_inc(a_full, 1)

        def pe_tail(pe):
            pe.wait_ge(sq2_written, 8)
            for g in range(2):
                n = A_MIX + g
                pe.wait_ge(a_free, n - 1)
                for hf in range(2):
                    for k in range(4):
                        mm = pe.matmul(sa(n)[:, hf, 0:HT], ones, sqx[:, 4 * g + k, hf * HT:(hf + 1) * HT], start=(k == 0), stop=(k == 3))
                mm.then_inc(a_full, 1)
            pe.wait_ge(mixed, 8)

            def passes(low, high, src, out, k0=0, nk=KD, last=KD, need=None):
                for k in range(nk):
                    if need is not None:
                        pe.wait_ge(need, k0 + k + 1)
                    xh, xl = src(k0 + k)
                    for w, x in ((high, xh), (high, xl), (low, xh)):
                        for hf in range(2):
                            mm = pe.matmul(out[:, hf, 0:HT], w[:, k, :], x[:, hf * HT:(hf + 1) * HT],
                                           start=(k0 + k == 0 and x is xh and w is high), stop=(k0 + k == last - 1 and w is low),
                                           skip_group_check=True)
                return mm

            proj = lambda k: (xhigh[:, k, :], xlow[:, k, :])
            pe.wait_ge(x_split, 2)
            with pe.Fori(0, 2) as i:
                for s in range(4):
                    pe.wait_ge(w_split, i * 4 + (s + 1))
                    pe.wait_ge(v_free, i * 4 + (V_OUT + s - 1))
                    passes(pieces(wlow[s]), pieces(whigh[s]), proj, sv(V_OUT + s)).then_inc(v_full, 1)
            n = A_SS2
            pe.wait_ge(a_free, n - 1)
            pe.wait_ge(sq2_written, 16)
            for hf in range(2):
                for k in range(KD):
                    mm = pe.matmul(sa(n)[:, hf, 0:HT], ones, sqx[:, k, hf * HT:(hf + 1) * HT], start=(k == 0), stop=(k == KD - 1))
            mm.then_inc(a_full, 1)
            pe.wait_ge(h2_done, 9)
            if PADA:
                pe.wait_ge(a_free, n + 1)
                pe.matmul(sa(n + 1)[0:1, 0, 0:1], ones[:, 0:1], ones[:, 0:1], start=True, stop=True).then_inc(a_full, 1)
            if PADV:
                pe.wait_ge(v_free, V_OUT + 8)
                pe.matmul(sv(V_OUT + 8)[0:1, 0, 0:1], ones[:, 0:1], ones[:, 0:1], start=True, stop=True).then_inc(v_full, 1)
            pe.wait_ge(x_split, 4)
            with pe.Fori(0, KF // 2) as i:
                for s in range(4):
                    ring, free, full, base = ((sa(A_G + s // 2), a_free, a_full, A_G), (sv(V_U + s // 2), v_free, v_full, V_U))[s % 2]
                    pe.wait_ge(w_split, i * 4 + (8 + s + 1))
                    pe.wait_ge(free, i * 2 + (base + s // 2 - 1))
                    passes(pieces(wlow[s]), pieces(whigh[s]), proj, ring).then_inc(full, 1)
            down = lambda k: (ahigh[k], alow[:, k, :])

            def down_turn(i, need=None):
                for s in range(4):
                    m, half = divmod(s, 2)
                    pe.wait_ge(w_split, i * 4 + (NT + s + 1))
                    if half == 0:
                        pe.wait_ge(v_free, i * 2 + (V_DN + m - 1))
                    passes(pieces(dlow[s]), pieces(dhigh[s]), down, sv(V_DN + m), half * (KF // 2), KF // 2, KF,
                           need if m == 0 else None).then_inc((down_used, v_full)[half], 1)

            down_turn(0, a_split)
            with pe.Fori(1, 4) as i:
                down_turn(i)
            pe.wait_ge(x_new, 16)
            for t in range(5):
                n, w = A_Y + t, (128 if t < 4 else NB)
                pe.wait_ge(a_free, n - 1)
                out = sa(n).rearrange("p b n -> p (b n)")
                for k in range(KD):
                    mm = pe.transpose(out[0:w, k * 128:(k + 1) * 128], xT[:, k, t * 128:t * 128 + w], ident)
                mm.then_inc(a_full, 1)

        SQ, s = {}, 0
        for i in normed:
            SQ[i] = s
            s += U[i][1]
        widxT = rtmp_w = r1[0:8, 7 * T:8 * T]

        def act_program(act):
            A = nc.scalar.activation
            act.wait_ge(in_loaded, 16 * 21)
            A(csil, cin, ACT.Silu).then_inc(c_silu, 1)
            for j, n in enumerate(A_XT):
                act.wait_ge(a_full, n + 1)
                src = sa(n).rearrange("p b n -> p (b n)")
                if j < 4:
                    dst, src = xT[:, :, j * 128:(j + 1) * 128], src.rearrange("p (k n) -> p k n", k=KD)
                elif j == 4:
                    dst, src = xT[:, :, SEQ:T], src[:, 0:64].rearrange("p (k n) -> p k n", k=KD)
                elif j == 5:
                    dst, src = cT, src[:, 0:72].rearrange("p (k n) -> p k n", k=KD)
                else:
                    dst, src = gT[:], src[:, 0:N_GAIN]
                A(dst, src, ACT.Identity).then_inc(a_free, 1)
            act.wait_ge(a_free, A_XT[4] + 1)
            for k in range(KD):
                A(sqx[:, k, :], xT[:, k, :], ACT.Square).then_inc(sq_written, 1)
            act.wait_ge(a_full, A_MOD + 1)
            A(modT[:], sa(A_MOD)[:, 0, 0:432].rearrange("p (m c) -> p m c", m=48), ACT.Identity).then_inc(a_free, 1)
            act.wait_ge(eps_set, 1)
            act.wait_ge(a_full, A_SS + 1)
            A(halves(sd[:, 0, :]), sa(A_SS)[:, :, 0:HT], ACT.Sqrt, scale=1.0 / D, bias=epsc[:]).then_inc(a_free, 1)
            for k in range(KD):
                act.wait_ge(hT_scaled, k + 1)
                A(hT[:, k, 0:SEQ], hT[:, k, 0:SEQ], ACT.Identity, bias=modT[:, k, 0:1]).then_inc(hT_done, 1)
            act.wait_ge(zeroed, 2)
            for i in range(len(U) + 1):
                if i < len(U):
                    name, nt, rows = U[i]
                    k = kind(name)
                    j = int(name[-1]) if name[-1].isdigit() else 0
                    for t in range(nt):
                        n = A_proj[i][t]
                        act.wait_ge(a_full, n + 1)
                        src = sa(n)[0:rows, :, 0:HT]
                        if k in NORMED:
                            A(halves(sq[0:rows, (SQ[i] + t) % 4, :]), src, ACT.Square)
                            m = normed.index(i)
                            if k == "qlat":
                                dst = qlatT[:, t, :]
                            elif k == "kvlat":
                                dst = latT[:, t, :]
                            else:
                                if m >= 2:
                                    act.wait_ge(norm_done, m - 1)
                                dst = raw[0:rows, m % 2, :]
                            A(halves(dst), src, ACT.Identity).then_inc(a_free, 1)
                        elif k == "qi":
                            A(halves(qiz[0:64, 2 * j, :]), src[0:64], ACT.Identity)
                            A(halves(qiz[64:128, 2 * j + 1, :]), src[64:128], ACT.Identity).then_inc(a_free, 1)
                        else:
                            dst = {"v": vT[:], "kidx": kidxT[:], "widx": widxT}[k]
                            A(halves(dst), src, ACT.Identity).then_inc(a_free, 1)
                if i - 1 in A_norm:
                    name, nt, rows = U[i - 1]
                    m = normed.index(i - 1)
                    k = kind(name)
                    if m >= 2:
                        act.wait_ge(norm_done, m - 1)
                    act.wait_ge(a_full, A_norm[i - 1] + 1)
                    sc = {"qlat": 1.0 / QR, "kvlat": 1.0 / KVR, "q": 1.0 / HD, "k": 1.0 / HD}.get(k, 1.0)
                    A(halves(sd[0:rows, m % 2, :]), sa(A_norm[i - 1])[0:rows, :, 0:HT], ACT.Sqrt, scale=sc,
                      bias=epsc[0:rows]).then_inc(a_free, 1)
            for t in range(5):
                n = A_TOK + t
                w = 128 if t < 4 else NB
                act.wait_ge(a_full, n + 1)
                A(tok[0:w, t, 0:256], sa(n)[0:w, 0, 0:256], ACT.Identity)
                A(tok[0:w, t, 256:288], sa(n)[0:w, 0, 256 + 64:256 + 96], ACT.Identity)
                A(tok[0:w, t, 288:608], sa(n)[0:w, 1, 0:320], ACT.Identity).then_inc(a_free, 1)
            act.wait_ge(a_full, A_WT + 1)
            A(wtok[:, 0:4, :], sa(A_WT)[:, 0, 0:32].rearrange("p (t h) -> p t h", t=4), ACT.Identity, scale=IDX_SCALE)
            A(wtok[0:NB, 4, :], sa(A_WT)[0:NB, 0, 32:40], ACT.Identity, scale=IDX_SCALE).then_inc(a_free, 1)

            for j, (qt, h) in enumerate(IQ):
                n, W = A_IQ + j, (qt + 1) * 128
                act.wait_ge(a_full, n + 1)
                if j >= 2:
                    act.wait_ge(idx_acc, j - 1)
                A(rb[:, j % 2, 0:W], sa(n)[:, 0, 0:W], ACT.Relu).then_inc(a_free, 1)
            for t in range(4):
                n = A_VM + t
                act.wait_ge(a_full, n + 1)
                A(vm[:, t, :], sa(n)[:, 0, :], ACT.Identity).then_inc(a_free, 1)
            act.wait_ge(a_full, A_QS + 1)
            A(qs8.rearrange("b (x n) -> b x n", x=2), sa(A_QS)[0:NB, :, 0:4 * QK], ACT.Identity).then_inc(a_free, 1)
            act.wait_ge(v_full, V_KN + 1)
            act.wait_ge(v_free, V_KN + 1)
            A(pnsq, knew, ACT.Square).then_inc(new_sums, 1)
            act.wait_ge(idx_acc, len(IQ))
            for n in range(16):
                act.wait_ge(a_full, A_IP + n + 1)
                A(kiT[:, n % 2, :], sa(A_IP + n)[:, 0, :], ACT.Identity).then_inc(a_free, 1)
            NA = len(AT)
            for u in range(NA + 2):
                if u < NA:
                    g, qt, h = AT[u]
                    W = (qt + 1) * 128
                    act.wait_ge(stats_ready, u + 1)
                    if u >= 3:
                        act.wait_ge(a_full, A_PT + u - 2)
                    A(sP[:, u % 3, 0:W], sS[:, u % 3, 0:W], ACT.Exp, scale=(MLA_SCALE if g == 0 else 1.0),
                      bias=stat[:, u % 3, 1:2], accum_out=stat[:, u % 3, 2:3]).then_inc(exp_done, 1)
                if 1 <= u <= NA:
                    n, W = A_PT + u - 1, (AT[u - 1][1] + 1) * 128
                    act.wait_ge(a_full, n + 1)
                    if u - 1 >= 3:
                        act.wait_ge(pv_done, u - 3)
                    A(sPT[:, (u - 1) % 3, 0:W], sa(n)[:, 0, 0:W], ACT.Identity).then_inc(a_free, 1)
                if u >= 3 and u % 2 == 1:
                    g, qt, h = AT[u - 2]
                    pair = (u - 2) // 2
                    act.wait_ge(pv_done, u - 1)
                    A(mixT[:, 4 * g + h // 2, qt * 128:(qt + 1) * 128], psV[:, pair % 2, 1, 0:128], ACT.Identity).then_inc(o_free, 1)
            act_decode(act)
            act_tail(act)

        def act_decode(act):
            A = nc.scalar.activation

            def evacuate(b, par, j):
                act.wait_ge(a_full, at(b, NPG, A_LT + j + 1))
                A(lT[:, j % 2].rearrange("p k n -> p (k n)"), sa(A_LT + j)[:, 0, 0:256], ACT.Identity).then_inc(a_free, 1)

            def square(b, j):
                act.wait_ge(v_full, at(b, NPG, V_KX + j + 1))
                if not (isinstance(b, int) and b == 0 and j < 2):
                    act.wait_ge(page_sums, at(b, NPG, j - 1))
                A(sqk[:, j % 2, :], sv(V_KX + j)[:, 0, :], ACT.Square).then_inc(squared, 1)

            def roots(b, par):
                act.wait_ge(rstd_in, at(b, 1, 1))
                A(sums[par], sums[par], ACT.Sqrt, scale=1.0 / NOPE, bias=epsc[:]).then_inc(ss_ready, 1)

            def exps(b, par):
                act.wait_ge(shifted, at(b, 1, 1))
                A(pm[par], pm[par], ACT.Exp, scale=MLA_SCALE).then_inc(p_exp, 1)

            def take(b, par):
                act.wait_ge(lat_pv, at(b, 1, 1))
                dst = olb[:, b, :] if isinstance(b, int) else olb[:, bass.ds(at(b, 1, 0), 1), :].rearrange("p b r -> p (b r)")
                A(dst, psV[0:8, par, 1, 0:KVR], ACT.Identity).then_inc(lat_out, 1)

            def pages(b, par, prev):
                for j in range(NPG + 1):
                    if j < NPG:
                        evacuate(b, par, j)
                    if j >= 1:
                        square(b, j - 1)
                    if prev is not None and j == 1:
                        roots(prev, 1 - par)
                    if prev is not None and j == 5:
                        exps(prev, 1 - par)
                    if prev is not None and j == 13:
                        take(prev, 1 - par)

            pages(0, 0, None)
            pages(1, 1, 0)
            with act.Fori(1, 4) as i:
                pages((i, 0), 0, (i, -1))
                pages((i, 1), 1, (i, 0))
            roots(7, 1)
            exps(7, 1)
            take(7, 1)
            act.wait_ge(a_full, A_OL + 1)
            A(olT.rearrange("p k r -> p (k r)"), sa(A_OL)[:, 0, 0:128], ACT.Identity).then_inc(a_free, 1)
            for x in range(32):
                n = A_KD + x
                act.wait_ge(a_full, n + 1)
                A(kdT[:, x % 2, :], sa(n)[:, 0, :], ACT.Identity).then_inc(a_free, 1)
            act.wait_ge(s64_ready, 1)
            A(s64, s64, ACT.Exp, bias=small[0:64, 9:10], accum_out=small[0:64, 10:11]).then_inc(p64_exp, 1)
            for x in range(3):
                act.wait_ge(a_full, A_PD + x + 1)
                dst, rows = (ptd[:, x * 8:x * 8 + 8, :].rearrange("p j r -> p (j r)"), 128) if x < 2 else (ptd[0:NB, 16, :], NB)
                A(dst, sa(A_PD + x)[0:rows, 0, 0:(512 if x < 2 else 64)], ACT.Identity).then_inc(a_free, 1)

            def d_take(b, par):
                act.wait_ge(d_pv, at(b, 1, 1))
                dst = od[:, b, :] if isinstance(b, int) else od[:, bass.ds(at(b, 1, 0), 1), :].rearrange("p b n -> p (b n)")
                A(dst, psV[0:8, par, 1, 0:128], ACT.Identity).then_inc(d_out, 1)

            with act.Fori(0, 4) as i:
                for par in range(2):
                    d_take((i, par), par)
            act.wait_ge(a_full, A_OD + 1)
            A(odT.rearrange("p b h -> p (b h)"), sa(A_OD)[:, 0, 0:64], ACT.Identity).then_inc(a_free, 1)

        def act_tail(act):
            A = nc.scalar.activation
            act.wait_ge(o_free, len(AT) // 2)
            act.wait_ge(mix_s, 1)
            for k in range(KD):
                A(sqx[:, k, :], mixT[:, k, :], ACT.Square).then_inc(sq2_written, 1)
            for g in range(2):
                act.wait_ge(a_full, A_MIX + g + 1)
                A(halves(sd[:, g, :]), sa(A_MIX + g)[:, :, 0:HT], ACT.Sqrt, scale=1.0 / 512, bias=epsc[:]).then_inc(a_free, 1)
            act.wait_ge(x_new, 8)
            for k in range(KD):
                A(sqx[:, k, :], xT[:, k, :], ACT.Square).then_inc(sq2_written, 1)
            act.wait_ge(a_full, A_SS2 + 1)
            A(halves(sd[:, 0, :]), sa(A_SS2)[:, :, 0:HT], ACT.Sqrt, scale=1.0 / D, bias=epsc[:]).then_inc(a_free, 1)
            for k in range(KD):
                act.wait_ge(h2_scaled, k + 1)
                A(hT[:, k, 0:SEQ], hT[:, k, 0:SEQ], ACT.Identity, bias=modT[:, 24 + k, 0:1]).then_inc(h2_done, 1)
            if PADA:
                act.wait_ge(a_full, A_SS2 + 2)
                A(stat[0:1, 0, 0:1], sa(A_SS2 + 1)[0:1, 0, 0:1], ACT.Identity).then_inc(a_free, 1)
            with act.Fori(0, KF // 2) as i:
                for s in range(2):
                    act.wait_ge(a_full, i * 2 + (A_G + s + 1))
                    A(actT[:, bass.ds(i * 2 + s, 1), :].rearrange("p a (h t) -> p (a h) t", h=2), sa(A_G + s)[:, :, 0:HT],
                      ACT.Silu).then_inc(a_free, 1)
            for t in range(5):
                n, w = A_Y + t, (128 if t < 4 else NB)
                act.wait_ge(a_full, n + 1)
                if t >= 2:
                    act.wait_ge(y_stored[t % 2], 16 * (t // 2))
                A(yt[0:w, t % 2, :], sa(n)[0:w].rearrange("p b n -> p (b n)"), ACT.Identity).then_inc(a_free, 1)

        def dve_program(v):
            link = Link(v)

            v.memset(gin, 0.0)
            v.memset(epsc[:], EPS).then_inc(eps_set, 1)
            v.wait_ge(bada_loaded, 16)
            v.wait_ge(v_full, 1)

            def ada_rows(s, col, full):
                v.wait_ge(v_full, full)
                v.tensor_tensor(ada9[:, bass.ds(col, 256)], psV[0:9, s, 0, 0:256], bada9[:, bass.ds(col, 256)],
                                ALU.add).then_inc(v_free, 1)

            with v.Fori(0, 12) as i:
                for s in range(2):
                    ada_rows(s, i * 512 + s * 256, i * 2 + (s + 1))
            v.wait_ge(a_free, A_MOD + 1)
            for w, sc in ((0, 8), (1, 32)):
                link(v.scalar_tensor_tensor(amod[:, w], modT[:, sc:sc + 8, :], 1.0,
                                            gT[:, w * 8:w * 8 + 8].unsqueeze(2).broadcast_to([128, 8, 9]), ALU.add, ALU.mult))
            modulate(v, link, 0)
            v.wait_ge(zeroed, 2)
            for i in range(1, len(U) + 2):
                if i - 1 in A_norm:
                    name, nt, rows = U[i - 1]
                    k = kind(name)
                    j = int(name[-1]) if name[-1].isdigit() else 0
                    m = normed.index(i - 1)
                    v.wait_ge(a_free, A_norm[i - 1] + 1)
                    r = sd[0:rows, m % 2, :]
                    link(v.reciprocal(r, r))
                    for t in range(nt):
                        g = gT[0:rows, gain_col(name, t):gain_col(name, t) + 1]
                        if k == "q":
                            for p0, hh in ((0, j), (64, j + 4)):
                                ins = v.scalar_tensor_tensor(qz[p0:p0 + 64, hh, :], raw[p0:p0 + 64, m % 2, :], g[p0:p0 + 64],
                                                             r[p0:p0 + 64], ALU.mult, ALU.mult)
                        elif k == "kn":
                            ins = v.scalar_tensor_tensor(kcat[0:64, j, :], raw[0:64, m % 2, :], g, r, ALU.mult, ALU.mult)
                        else:
                            if k == "qlat":
                                src = dst = qlatT[:, t, :]
                            elif k == "kvlat":
                                src = dst = latT[:, t, :]
                            else:
                                src = raw[0:rows, m % 2, :]
                                dst = {"krope": krF[:], "k": kT[:], "qc": qcat[0:QK, j, :]}[k]
                            ins = v.scalar_tensor_tensor(dst, src, g, r, ALU.mult, ALU.mult)
                    ins.then_inc(norm_done, 1)
                if i - 2 in V_rot:
                    n = V_rot[i - 2]
                    dst = (krF[64:96, :] if U[i - 2][0] == "krope" else qcat[64:96, int(U[i - 2][0][-1]), :])
                    v.wait_ge(v_full, n + 1)
                    v.tensor_tensor(halves(rtmp[64:96, :]), sv(n)[64:96, :, 0:HT], halves(rope[64:96, 1, :]),
                                    ALU.mult).then_inc(v_free, 1)
                    v.wait_ge(norm_done, normed.index(i - 2) + 1)
                    link(v.tensor_tensor(dst, dst, rope[64:96, 0, :], ALU.mult))
                    v.wait_ge(v_free, n + 1)
                    v.tensor_tensor(dst, dst, rtmp[64:96, :], ALU.add).then_inc(rope_done, 1)
            v.wait_ge(rope_done, 1)
            v.tensor_copy(kcat[64:96, :, :], krF[64:96, :].unsqueeze(1).broadcast_to([32, 8, T])).then_inc(kr_spread, 1)

            for j, (qt, h) in enumerate(IQ):
                m0, m1 = MQ[qt]
                v.wait_ge(a_free, A_IQ + j + 1)
                if h > 0:
                    v.wait_ge(idx_acc, j)
                    v.scalar_tensor_tensor(msk[:, m0:m1], rb[:, j % 2, 0:m1 - m0], wtok[:, qt, h:h + 1], msk[:, m0:m1],
                                           ALU.mult, ALU.add).then_inc(idx_acc, 1)
                else:
                    v.tensor_scalar(msk[:, m0:m1], rb[:, j % 2, 0:m1 - m0], wtok[:, qt, h:h + 1], None, ALU.mult).then_inc(idx_acc, 1)
            v.wait_ge(idx_acc, len(IQ))
            for qt in range(1, 4):
                m1 = MQ[qt][1]
                link(v.tensor_tensor(msk[:, m1 - 128:m1], msk[:, m1 - 128:m1], cext[:, 384:512], ALU.add))
            v.wait_ge(v_full, V_BIAS + 1)
            v.tensor_copy(g8, sv(V_BIAS)[0:8, 0, 0:384]).then_inc(v_free, 1)
            for j in range(2):
                n = V_BIAS + 1 + j
                v.wait_ge(v_full, n + 1)
                v.tensor_copy(toep[:, j * 1024:(j + 1) * 1024], sv(n).rearrange("p b n -> p (b n)")).then_inc(v_free, 1)

            v.wait_ge(ptab_loaded, 128)
            v.tensor_scalar(rows_of[:], ptab[:], 8.0, sel[:, 80:81], ALU.mult, ALU.add).then_inc(rows_ready, 1)
            link(v.memset(w1, 0.0))
            v.memset(ptd[:, NPG, :], 0.0)
            v.wait_ge(norm_done, len(normed))
            v.tensor_scalar(qcat[0:64, :, SEQ:T], qcat[0:64, :, SEQ:T], gT[0:64, G_KN:G_KN + 1], None, ALU.mult).then_inc(qs_gained, 1)
            w1v = w1.rearrange("p (b x) -> p b x", x=144)
            for p0, c in ((0, 0), (64, 8)):
                for odd in range(2):
                    v.tensor_copy(w1v[p0:p0 + 64, :, c + odd:c + 8:2],
                                  qiz[odd * 64:odd * 64 + 64, odd:8:2, SEQ:T].rearrange("p h b -> p b h")).then_inc(w1_ready, 1)
            link(v.tensor_copy(qd[:].rearrange("p (b h) -> p b h", b=NB), qz[:, :, SEQ:T].rearrange("p h b -> p b h")))
            link(v.memset(qdz[:], 0.0))
            v.tensor_copy(qdz[:].rearrange("p (b x) -> p b x", x=72)[:, :, 0:8], qd[:].rearrange("p (b h) -> p b h", b=NB)).then_inc(w1_ready, 1)
            v.wait_ge(v_full, V_KN + 1)
            v.tensor_copy(knew, sv(V_KN)[0:NB, 0, :]).then_inc(v_free, 1)
            v.wait_ge(const_loaded, 80)
            v.wait_ge(v_full, V_WC + 1)
            v.tensor_tensor_reduce(small[:, 0:8], sv(V_WC)[:, 0, 0:8], sel[:, 64:72], 1.0, 0.0, ALU.mult, ALU.add,
                                   small[:, 8:9]).then_inc(v_free, 1)
            v.wait_ge(v_free, V_WC + 1)
            v.tensor_scalar(wz[:], sel[:, 0:64], small[:, 8:9], None, ALU.mult).then_inc(wz_ready, 1)
            v.tensor_tensor(irel[:, 0:64].rearrange("p (h b) -> p h b", h=H), qiz[:, :, SEQ:T],
                            kidxT[:, SEQ:T].unsqueeze(1).broadcast_to([128, H, NB]), ALU.mult).then_inc(pn_ready, 1)
            v.wait_ge(v_full, V_WC + 2)
            v.tensor_scalar(small[0:NB, 16:24], sv(V_WC + 1)[0:NB, 0, 0:8], 0.0, None, ALU.max).then_inc(v_free, 1)
            v.wait_ge(v_free, V_WC + 2)
            link(v.tensor_tensor_reduce(small[0:NB, 24:32], small[0:NB, 16:24], wtok[0:NB, 4, :], 1.0, 0.0, ALU.mult, ALU.add,
                                        small[0:NB, 32:33]))
            link(v.tensor_copy(sc8[:, PAST:PAST + 1], small[0:NB, 32:33]))
            v.wait_ge(new_sums, 1)
            link(v.tensor_reduce(ssnew[:], pnsq.rearrange("p (h d) -> p h d", h=H), AXX, ALU.add))
            link(v.tensor_copy(rb64[:].rearrange("p (b h) -> p b h", b=NB), rbias.unsqueeze(1).broadcast_to([NBUCK, NB, 8])))
            v.tensor_scalar(small[:, 40:41], small[:, 8:9], 0.0, None, ALU.mult).then_inc(pn_ready, 1)
            v.wait_ge(v_full, V_IS + 1)
            v.tensor_scalar(irel, sv(V_IS).rearrange("p b n -> p (b n)"), 0.0, None, ALU.max).then_inc(v_free, 1)
            v.wait_ge(v_free, V_IS + 1)
            v.tensor_scalar(small[:, 41:42], small[:, 8:9], 0.0, None, ALU.mult).then_inc(irel_ready, 1)
            v.wait_ge(v_full, V_ISW + 1)
            for g in range(2):
                for par in range(2):
                    dst = sc8[:, 0:PAST].rearrange("r (p x two) -> r x p two", x=8, two=2)[:, 4 * g:4 * g + 4, :, par]
                    ins = v.tensor_copy(dst, sv(V_ISW)[par * 32:par * 32 + NB, g, :].rearrange("r (x p) -> r x p", x=4))
            ins.then_inc(v_free, 1)
            v.wait_ge(v_free, V_ISW + 1)

            def top_rounds():
                for qt in range(1, 4):
                    m0, m1 = MQ[qt]
                    for r in range(TOPK_P // 8):
                        link(v.max(top8[:], msk[:, m0:m1]))
                        link(v.match_replace(msk[:, m0:m1], top8[:], msk[:, m0:m1], TAKEN))
                        yield
                    link(v.tensor_scalar(msk[:, m0:m1], msk[:, m0:m1], TAKEN / 2, NEG, ALU.is_gt, ALU.mult))
                for r in range(TOPK_S // 8):
                    link(v.max(top8[0:NB], sc8))
                    link(v.match_replace(sc8, top8[0:NB], sc8, TAKEN))
                    yield
                v.tensor_scalar(sc8, sc8, TAKEN / 2, NEG, ALU.is_gt, ALU.mult).then_inc(top_done, 1)

            rounds = top_rounds()
            v.wait_ge(qs_out, 16)
            NA = len(AT)
            for u in range(NA + 1):
                if u < NA:
                    g, qt, h = AT[u]
                    n, W, c = V_S + u, (qt + 1) * 128, u % 3
                    S = sS[:, c, 0:W]
                    v.wait_ge(v_full, n + 1)
                    if u >= 3:
                        v.wait_ge(exp_done, u - 2)
                    if g == 0:
                        v.tensor_tensor_reduce(S, sv(n)[:, 0, 0:W], cext[:, 512 - W:512], 1.0, TAKEN, ALU.add, ALU.max,
                                               stat[:, c, 0:1]).then_inc(v_free, 1)
                        v.wait_ge(v_free, n + 1)
                        v.tensor_scalar(stat[:, c, 1:2], stat[:, c, 0:1], -MLA_SCALE, None, ALU.mult).then_inc(stats_ready, 1)
                    else:
                        near = min(W, 256)
                        if W > near:
                            link(v.tensor_scalar(S[:, 0:W - near], sv(n)[:, 0, 0:W - near], DSA_SCALE, toepv[:, h, 0:1], ALU.mult, ALU.add))
                        v.scalar_tensor_tensor(S[:, W - near:W], sv(n)[:, 0, W - near:W], DSA_SCALE, toepv[:, h, 256 - near:256],
                                               ALU.mult, ALU.add).then_inc(v_free, 1)
                        v.wait_ge(v_free, n + 1)
                        mask = cext[:, 384:512] if qt == 0 else msk[:, MQ[qt][0]:MQ[qt][1]]
                        link(v.tensor_tensor_reduce(S, S, mask, 1.0, TAKEN, ALU.add, ALU.max, stat[:, c, 0:1]))
                        v.tensor_scalar(stat[:, c, 1:2], stat[:, c, 0:1], -1.0, None, ALU.mult).then_inc(stats_ready, 1)
                if u >= 1:
                    c, W = (u - 1) % 3, (AT[u - 1][1] + 1) * 128
                    v.wait_ge(exp_done, u)
                    link(v.reciprocal(stat[:, c, 3:4], stat[:, c, 2:3]))
                    v.tensor_scalar(sP[:, c, 0:W], sP[:, c, 0:W], stat[:, c, 3:4], None, ALU.mult).then_inc(p_ready, 1)
                for _ in range(2 if u < 31 else 1):
                    next(rounds, None)
            for _ in rounds:
                pass
            dve_decode(v, link)
            dve_tail(v, link)

        def dve_decode(v, link):
            link(v.memset(small[:, 42:43], 0.0))
            for x in range(3):
                n = V_BF + x
                v.wait_ge(v_full, n + 1)
                if x < 2:
                    v.tensor_copy(bm64[:, x * 1024:(x + 1) * 1024], sv(n)[0:64].rearrange("p b n -> p (b n)")).then_inc(v_free, 1)
                else:
                    v.tensor_copy(bm64[:, 2048:2049], sv(n)[0:64, 0, 0:1]).then_inc(v_free, 1)
            v.wait_ge(qbc_loaded, 16)
            for x in range(2):
                v.memset(sfull[x][:, NPG, :], NEG)
                ins = v.memset(sums[x][:, NPG, :], 1.0)
            ins.then_inc(neg_set, 1)
            v.wait_ge(neg_set, 1)

            def query(b):
                return qbc[:, b] if isinstance(b, int) else qbc[:, bass.ds(at(b, 1, 0), 1)].rearrange("p a h d -> p (a h) d")

            def dot(b, par, j):
                n = V_KX + j
                v.wait_ge(squared, at(b, NPG, j + 1))
                prj = pr[:, j % 2, :].rearrange("p (h d) -> p h d", h=H)
                v.tensor_tensor(prj, sv(n)[:, 0, :].rearrange("p (h d) -> p h d", h=H), query(b)[:, :, 0:NOPE], ALU.mult).then_inc(v_free, 1)
                v.wait_ge(v_free, at(b, NPG, n + 1))
                v.tensor_reduce(dots[par][:, j, :], prj, AXX, ALU.add)
                v.tensor_reduce(sums[par][:, j, :], sqk[:, j % 2, :].rearrange("p (h d) -> p h d", h=H), AXX, ALU.add).then_inc(page_sums, 1)

            def rope_part(b, par, c):
                v.wait_ge(rope_mul, at(b, 4, c + 1))
                v.tensor_reduce(drope[par][:, 4 * c:4 * c + 4, :], rp[:, c % 2], AXX, ALU.add).then_inc(rope_sum, 1)

            def new_row(b, par):
                q = query(b)
                t = small[0:NB, 0:1]
                big = newp
                link(v.tensor_tensor(big[:, :, 0:64], knew.rearrange("p (h d) -> p h d", h=H), q[0:NB, :, 0:64], ALU.mult))
                link(v.tensor_reduce(dots[par][0:NB, NPG, :], big[:, :, 0:64], AXX, ALU.add))
                link(v.tensor_tensor(big[:, :, 0:32], tok[0:NB, 4, KVR:ROW].unsqueeze(1).broadcast_to([NB, H, ROPE]), q[0:NB, :, 64:96], ALU.mult))
                link(v.tensor_reduce(drope[par][0:NB, NPG, :], big[:, :, 0:32], AXX, ALU.add))
                v.tensor_copy(sums[par][0:NB, NPG, :], ssnew[:]).then_inc(rstd_in, 1)

            def scores(b, par):
                v.wait_ge(ss_ready, at(b, 1, 1))
                link(v.reciprocal(sums[par], sums[par]))
                link(v.tensor_tensor(dots[par][:, 0:NPG], dots[par][:, 0:NPG], sums[par][:, 0:NPG], ALU.mult))
                link(v.tensor_tensor(dots[par][0:NB, NPG], dots[par][0:NB, NPG], sums[par][0:NB, NPG], ALU.mult))
                link(v.tensor_tensor(sfull[par][:, 0:NPG], dots[par][:, 0:NPG], drope[par][:, 0:NPG], ALU.add))
                link(v.tensor_tensor(sfull[par][0:NB, NPG], dots[par][0:NB, NPG], drope[par][0:NB, NPG], ALU.add))
                only = onlyc[0:NB, b:b + 1] if isinstance(b, int) else onlyc[0:NB, bass.ds(at(b, 1, 0), 1)]
                link(v.tensor_scalar(sfull[par][0:NB, NPG], sfull[par][0:NB, NPG], only, None, ALU.add))
                v.tensor_reduce(hstat[:, 0, :], sfull[par].rearrange("p j h -> p h j"), AXX, ALU.max).then_inc(smax, 1)

            def shift(b, par):
                v.wait_ge(gmax, at(b, 1, 1))
                v.tensor_tensor(pm[par], sfull[par], hstat[:, 1, :].unsqueeze(1).broadcast_to([128, NPG + 1, 8]), ALU.subtract).then_inc(shifted, 1)

            def row_sums(b, par):
                v.wait_ge(p_exp, at(b, 1, 1))
                v.tensor_reduce(hstat[:, 2, :], pm[par].rearrange("p j h -> p h j"), AXX, ALU.add).then_inc(psum_ready, 1)

            def normalise(b, par):
                v.wait_ge(gsum, at(b, 1, 1))
                link(v.reciprocal(hstat[:, 3, :], hstat[:, 3, :]))
                v.tensor_tensor(pm[par], pm[par], hstat[:, 3, :].unsqueeze(1).broadcast_to([128, NPG + 1, 8]), ALU.mult).then_inc(pm_ready, 1)

            def pages(b, par, prev):
                for j in range(NPG):
                    dot(b, par, j)
                    if j % 4 == 3:
                        rope_part(b, par, j // 4)
                    if prev is not None:
                        for at_j, step in ((1, scores), (4, shift), (6, row_sums), (9, normalise)):
                            if j == at_j:
                                step(prev, 1 - par)
                v.wait_ge(page_sums, at(b, NPG, NPG))
                new_row(b, par)

            pages(0, 0, None)
            pages(1, 1, 0)
            with v.Fori(1, 4) as i:
                LP = link.per_loop(i, 1, lambda: (pages((i, 0), 0, (i, -1)), pages((i, 1), 1, (i, 0))))
            link.after_loop()
            for step in (scores, shift, row_sums, normalise):
                step(7, 1)
            v.wait_ge(v_full, V_OV + 1)
            v.tensor_copy(mixT[:, 0:4, SEQ:T], sv(V_OV)[:, 0, 0:32].rearrange("p (k b) -> p k b", k=4)).then_inc(v_free, 1)

            v.wait_ge(mask_back, 16)
            link(v.tensor_tensor(bm64, bm64, s64, ALU.add))
            by_slot = bm64[:, 0:PAST].rearrange("r (p j) -> r j p", j=NPG)
            for x in range(2):
                n = V_SD + x
                v.wait_ge(v_full, n + 1)
                for g in range(2):
                    c4 = 2 * x + g
                    ins = v.scalar_tensor_tensor(s64[:, c4 * 512:(c4 + 1) * 512].rearrange("r (j p) -> r j p", j=4),
                                                 sv(n)[0:64, g, :].rearrange("r (j p) -> r j p", j=4), DSA_SCALE,
                                                 by_slot[:, 4 * c4:4 * c4 + 4, :], ALU.mult, ALU.add)
                ins.then_inc(v_free, 1)
            v.wait_ge(v_full, V_SN + 1)
            v.tensor_tensor_reduce(small[0:64, 0:8], sv(V_SN)[0:64, 0, 0:8], sel[0:64, 72:80], 1.0, 0.0, ALU.mult, ALU.add,
                                   small[0:64, 8:9]).then_inc(v_free, 1)
            v.wait_ge(v_free, V_SN + 1)
            link(v.scalar_tensor_tensor(s64[:, PAST:PAST + 1], small[0:64, 8:9], DSA_SCALE, bm64[:, PAST:PAST + 1], ALU.mult, ALU.add))
            link(v.tensor_reduce(small[0:64, 11:12], s64, AXX, ALU.max))
            v.tensor_scalar(small[0:64, 9:10], small[0:64, 11:12], -1.0, None, ALU.mult).then_inc(s64_ready, 1)
            v.wait_ge(p64_exp, 1)
            link(v.reciprocal(small[0:64, 12:13], small[0:64, 10:11]))
            link(v.tensor_scalar(s64, s64, small[0:64, 12:13], None, ALU.mult))
            v.tensor_scalar(small[0:64, 0:8], sel[0:64, 72:80], s64[:, PAST:PAST + 1], None, ALU.mult).then_inc(p64_ready, 1)
            split_tile(v, 0, 0)
            split_tile(v, 0, 1)
            v.wait_ge(a_free, A_OD + 1)
            for c in range(2):
                for par in range(2):
                    ins = v.tensor_copy(mixT[par * 64:par * 64 + 64, 4 + 2 * c:6 + 2 * c, SEQ:T],
                                        odT[c * 64:c * 64 + 64, :, 4 * c + par:4 * c + 4:2].rearrange("p b h -> p h b"))
            ins.then_inc(mix_s, 1)

        def split(v, raw, low, high, need, count, n):
            v.wait_ge(need, count)
            v.tensor_copy(high, raw).then_inc(w_high, 1)
            v.wait_ge(w_high, n + 1)
            v.tensor_tensor(low, raw, high.bitcast(F32), ALU.subtract).then_inc(w_split, 1)

        def split_tile(v, i, s):
            split(v, wraw[s], wlow[s], whigh[s], tail_w[s], i * 16 + 16, i * 4 + s)

        def split_down(v, i, s):
            split(v, draw[s], dlow[s], dhigh[s], down_w[s], i * 16 + 16, i * 4 + (NT + s))

        def split_input(v, n, k):
            v.tensor_copy(xhigh[:, k:k + 4, :], hT[:, k:k + 4, :]).then_inc(x_high, 1)
            v.wait_ge(x_high, n + 1)
            v.tensor_tensor(xlow[:, k:k + 4, :], hT[:, k:k + 4, :], xhigh[:, k:k + 4, :].bitcast(F32), ALU.subtract).then_inc(x_split, 1)

        def dve_tail(v, link):
            for g in range(2):
                v.wait_ge(a_free, A_MIX + g + 1)
                link(v.reciprocal(sd[:, g, :], sd[:, g, :]))
                for k in range(4 * g, 4 * g + 4):
                    v.scalar_tensor_tensor(mixT[:, k, :], mixT[:, k, :], gT[:, G_OUT + k:G_OUT + k + 1], sd[:, g, :],
                                           ALU.mult, ALU.mult).then_inc(mixed, 1)
                v.wait_ge(mixed, 4 * g + 4)
                split_input(v, g, 4 * g)

            def add_gated(slot, m, gate, count, s):
                x = xT[:, bass.ds(m, 1), :].rearrange("p a t -> p (a t)")
                gt = modT[:, bass.ds(m + gate, 1), :].rearrange("p a c -> p (a c)")
                v.wait_ge(v_full, count)
                v.scalar_tensor_tensor(x[:, 0:HT], slot[:, 0, 0:HT], gt[:, 0:1], x[:, 0:HT], ALU.mult, ALU.add)
                v.scalar_tensor_tensor(x[:, HT:SEQ], slot[:, 1, 0:SEQ - HT], gt[:, 0:1], x[:, HT:SEQ], ALU.mult, ALU.add)
                v.tensor_tensor(gated[:, s, :], slot[:, 1, SEQ - HT:HT], gt[:, 1:9], ALU.mult).then_inc(v_free, 1)
                v.wait_ge(v_free, count)
                v.tensor_tensor(x[:, SEQ:T], x[:, SEQ:T], gated[:, s, :], ALU.add).then_inc(x_new, 1)

            with v.Fori(0, 2) as i:
                for s in range(4):
                    split_tile(v, i + (s + 2) // 4, (s + 2) % 4)
                    add_gated(sv(V_OUT + s), i * 4 + s, 16, i * 4 + (V_OUT + s + 1), s % 2)
            v.wait_ge(a_free, A_SS2 + 1)
            modulate(v, link, 1)
            v.wait_ge(h2_done, 9)
            for g in range(2):
                split_input(v, 2 + g, 4 * g)
            if PADV:
                v.wait_ge(v_full, V_OUT + 9)
                v.tensor_copy(stat[0:1, 0, 1:2], sv(V_OUT + 8)[0:1, 0, 0:1]).then_inc(v_free, 1)

            def gate_turn(i, ahead):
                for s in range(2):
                    if s == 0 or ahead:
                        for c in range(2):
                            split_tile(v, i + (2 + (s + 1) // 2), (s + 1) % 2 * 2 + c)
                    v.wait_ge(v_full, i * 2 + (V_U + s + 1))
                    v.wait_ge(a_free, i * 2 + (A_G + s + 1))
                    t = actT[:, bass.ds(i * 2 + s, 1), :].rearrange("p a (h t) -> p (a h) t", h=2)
                    v.tensor_tensor(t, t, sv(V_U + s)[:, :, 0:HT], ALU.mult).then_inc(v_free, 1)

            with v.Fori(0, KF // 2 - 1) as i:
                gate_turn(i, True)
            gate_turn(KF // 2 - 1, False)
            v.wait_ge(v_free, V_U + KF)
            v.wait_ge(tokens_stored, 16 * 15)
            split_down(v, 0, 0)
            for k in range(KF):
                v.tensor_copy(ahigh[k], actT[:, k, :]).then_inc(a_high, 1)
                v.wait_ge(a_high, k + 1)
                v.tensor_tensor(alow[:, k, :], actT[:, k, :], ahigh[k].bitcast(F32), ALU.subtract).then_inc(a_split, 1)
                if k == KF // 2 - 1:
                    split_down(v, 0, 1)

            def down_turn(i, ahead):
                for s in range(4):
                    if s < 2 or ahead:
                        split_down(v, i + (s + 2) // 4, (s + 2) % 4)
                    if s % 2 == 1:
                        add_gated(sv(V_DN + s // 2), i * 2 + s // 2, 40, i * 2 + (V_DN + s // 2 + 1), s // 2)

            with v.Fori(0, 3) as i:
                down_turn(i, True)
            down_turn(3, False)

        def modulate(v, link, w):
            v.wait_ge(a_free, (A_SS, A_SS2)[w] + 1)
            scaled, done = ((hT_scaled, hT_done), (h2_scaled, h2_done))[w]
            link(v.reciprocal(sd[:, 0, :], sd[:, 0, :]))
            for k in range(KD):
                v.scalar_tensor_tensor(hT[:, k, 0:SEQ], xT[:, k, 0:SEQ], amod[:, w, k, 0:1], sd[:, 0, 0:SEQ],
                                       ALU.mult, ALU.mult).then_inc(scaled, 1)
            hs = hT[:, :, SEQ:T]
            link(v.tensor_tensor(hs, xT[:, :, SEQ:T], amod[:, w, :, 1:9], ALU.mult))
            link(v.tensor_tensor(hs, hs, sd[:, 0, SEQ:T].unsqueeze(1).broadcast_to([128, 8, NB]), ALU.mult))
            v.tensor_tensor(hs, hs, modT[:, w * 24:w * 24 + 8, 1:9], ALU.add).then_inc(done, 1)

        def pool_program(g):
            g.memset(tok[:, 4, :], 0.0).then_inc(zeroed, 1)
            g.wait_ge(a_free, A_MOD + 1)
            g.wait_ge(a_full, A_XT[6] + 1)
            g.memset(qiz[:], 0.0)
            g.memset(qz, 0.0).then_inc(zeroed, 1)
            for t in range(5):
                g.wait_ge(a_free, A_TOK + t + 1)
                w = 128 if t < 4 else NB
                tt = slice(t * 128, t * 128 + w)
                if t < 4:
                    outs = (o["mla_p"][0, 0, tt, :], o["kv_p"][0, 0, tt].rearrange("t a c d -> t (a c d)"), o["idx_p"][0, 0, tt, :])
                else:
                    outs = (o["mla_s"][0, :, 0, :], o["kv_s"][0, :, 0].rearrange("t a c d -> t (a c d)"), o["idx_s"][0, :, 0, :])
                for (c0, c1), dst in zip(((0, 288), (288, 544), (544, 608)), outs):
                    g.dma_start(dst, tok[0:w, t, c0:c1]).then_inc(tokens_stored, 16)
            def fetch(dst, name, width, b, done):
                n = a[name].shape[1]
                src = bass.AP(a[name].tensor, 0, [[16 * width, n * 8], [1, 16 * width]])
                g.indirect_dma_start(out=dst, out_offset=None, in_=src,
                                     in_offset=bass.IndirectOffsetOnAxis(ap=rows_of[:, b:b + 1], axis=0)).then_inc(done, 16)

            g.wait_ge(rows_ready, 1)
            g.wait_ge(v_free, V_BIAS + 1)
            for b in range(NB):
                if b >= 2:
                    g.wait_ge(a_full, A_IP + 2 * b - 2)
                fetch(ip[:, b % 2, :], "cache_idx", IDX, b, idx_pages[b % 2])
            g.wait_ge(a_full, A_PT + len(AT))
            g.wait_ge(pv_done, len(AT))
            mla_rows = lambda b: fetch(pgs[:, b % 2].rearrange("p j n -> p (j n)"), "cache_mla", ROW, b, mla_pages[b % 2])
            kv_pair = lambda b, c: fetch(kvp[:, b % 2].rearrange("p j n -> p (j n)"), "cache_kv", 256, b, kv_rows[b % 2])
            mla_rows(0)
            mla_rows(1)
            g.wait_ge(qbc_loaded, 16)

            def rope_pages(b, par, loads, c):
                q = qbc[:, b]
                g.wait_ge(mla_pages[par], loads)
                if b > 0 or c >= 2:
                    g.wait_ge(rope_sum, 4 * b + c - 1)
                g.tensor_tensor(rp[:, c % 2], pgs[:, par, 4 * c:4 * c + 4, KVR:ROW].unsqueeze(2).broadcast_to([128, 4, H, ROPE]),
                                q[:, :, NOPE:QK].unsqueeze(1).broadcast_to([128, 4, H, ROPE]), ALU.mult).then_inc(rope_mul, 1)

            def head_max(b):
                g.wait_ge(smax, b + 1)
                g.partition_all_reduce(hstat[:, 1, :], hstat[:, 0, :], 128, RMAX).then_inc(gmax, 1)

            def head_sum(b):
                g.wait_ge(psum_ready, b + 1)
                g.partition_all_reduce(hstat[:, 3, :], hstat[:, 2, :], 128, RADD).then_inc(gsum, 1)

            for b in range(NB):
                rope_pages(b, b % 2, 16 * (b // 2 + 1), 0)
                if b >= 1:
                    head_max(b - 1)
                rope_pages(b, b % 2, 16 * (b // 2 + 1), 1)
                if b >= 1:
                    head_sum(b - 1)
                rope_pages(b, b % 2, 16 * (b // 2 + 1), 2)
                rope_pages(b, b % 2, 16 * (b // 2 + 1), 3)
                if 1 <= b < NB - 1:
                    g.wait_ge(lat_pv, b)
                    mla_rows(b + 1)
            head_max(NB - 1)
            head_sum(NB - 1)
            g.wait_ge(lat_pv, NB)
            for b in range(NB):
                if b >= 2:
                    g.wait_ge(a_full, A_KD + 4 * b - 4)
                kv_pair(b, 0)
            for b in range(2):
                g.wait_ge(a_full, A_KD + 4 * (NB - 2 + b) + 4)
                kv_pair(b, 1)
            g.wait_ge(a_free, A_PD + 3)
            for b in range(NB):
                if b >= 2:
                    g.wait_ge(d_pv, b - 1)
                    kv_pair(b, 1)
                g.tensor_copy(ptb[:, b % 2], ptd[:, :, b * 8:b * 8 + 8]).then_inc(ptb_ready, 1)
            g.wait_ge(tokens_stored, 16 * 15)

        block = ctx.enter_context(nc.Block())
        block.sync(lambda e: sp_program(e))
        block.tensor(lambda e: pe_program(e))
        block.scalar(lambda e: act_program(e))
        block.vector(lambda e: dve_program(e))
        block.gpsimd(lambda e: pool_program(e))


_INS = ["x_prompt", "x_sample", "c_prompt", "c_sample", "cache_mla", "cache_kv", "cache_idx", "page_table",
        "rel_bias", "w_ada", "b_ada", "g_norm_mix", "g_norm_ffn", "w_in", "g_q_lat", "w_uq", "g_kv_lat", "w_ukv",
        "g_mla_q_nope", "g_mla_q_rope", "g_mla_k_nope", "g_mla_k_rope", "g_dsa_q", "g_dsa_k", "g_out", "w_out",
        "w_ffn_in", "w_ffn_out"]
_OUTS = [("y_p", (1, SEQ, D)), ("y_s", (NB, 1, D)),
         ("mla_p", (1, 1, SEQ, ROW)), ("kv_p", (1, 1, SEQ, 2, 2, HD)), ("idx_p", (1, 1, SEQ, IDX)),
         ("mla_s", (1, NB, 1, ROW)), ("kv_s", (1, NB, 1, 2, 2, HD)), ("idx_s", (1, NB, 1, IDX))]


def kernel(**inputs):
    import concourse.bacc as _bacc
    from concourse.bass_utils import run_bass_kernel_spmd as _run

    nc = _bacc.Bacc("TRN2", target_bir_lowering=False, num_devices=1)
    arrays = {name: np.ascontiguousarray(inputs[name]) for name in _INS}
    arrays.update(shape_constants())
    ins = {k: nc.dram_tensor(k, v.shape, mybir.dt.from_np(v.dtype), kind="ExternalInput").ap() for k, v in arrays.items()}
    outs = {k: nc.dram_tensor(k, shape, F32, kind="ExternalOutput").ap() for k, shape in _OUTS}
    build(nc, ins, outs)
    r = _run(nc, [arrays], core_ids=[0])
    return tuple(r.results[0][k] for k, _ in _OUTS)
```

```python
from contextlib import ExitStack

import numpy as np

import concourse.bass as bass
from concourse import mybir

F32 = mybir.dt.float32
F32R = mybir.dt.float32r
I32 = mybir.dt.int32
ALU = mybir.AluOpType
ACT = mybir.ActivationFunctionType
AXX = mybir.AxisListType.X
RMAX = bass.bass_isa.ReduceOp.max
RADD = bass.bass_isa.ReduceOp.add

D, SEQ, NB, PAST, PAGE = 1024, 512, 8, 2048, 128
NPG = PAST // PAGE
H, NOPE, ROPE, VD = 8, 64, 32, 64
QK = NOPE + ROPE
QR, KVR = 384, 256
ROW = KVR + ROPE
HD, IDX = 64, 64
TOPK_P, TOPK_S = min(256, SEQ // 4), min(256, (PAST + 1) // 4)
NBUCK, MAXD = 32, 128
DFF = 2816
EPS = 1e-6
T = SEQ + NB
HT = T // 2
KD = D // 128
KF = DFF // 128
MLA_SCALE = float(QK) ** -0.5
DSA_SCALE = float(HD) ** -0.5
IDX_SCALE = float(IDX * 8) ** -0.5
NEG = -1e30
TAKEN = -3e38
C_KV, C_KR, C_Q, C_K, C_V, C_QI, C_KI, C_WI = 384, 640, 672, 1184, 1312, 1440, 1952, 2016
PER_TURN = 22
G_MIX, G_FFN, G_OUT, G_QL, G_KVL, G_Q, G_KN, G_KR, G_DQ, G_DK, N_GAIN = 0, 8, 16, 24, 27, 29, 30, 30, 31, 32, 33


def shape_constants():
    f = np.float32
    mats = np.zeros((6, 128, 128), f)
    mats[0] = np.eye(128)
    mats[1] = np.eye(128)[::-1]
    mats[2] = 1.0
    mats[3, :64, :64] = mats[3, 64:, 64:] = 1.0
    mats[4, :64, :64] = 1.0 / NOPE
    mats[4, 64:96, 64:96] = 1.0 / ROPE
    half = ROPE // 2
    for j in range(half):
        mats[5, 64 + half + j, 64 + j] = -1.0
        mats[5, 64 + j, 64 + half + j] = 1.0
    pos = np.concatenate([np.arange(SEQ), np.full(NB, PAST)]).astype(f)
    freq = (f(10000.0) ** (-np.arange(half, dtype=f) / f(half))).astype(f)
    ang = pos[None, :] * freq[:, None]
    rope = np.zeros((QK, 2, T), f)
    for r in range(ROPE):
        rope[NOPE + r, 0] = np.cos(ang[r % half])
        rope[NOPE + r, 1] = np.sin(ang[r % half])
    def bucket(d):
        d = np.maximum(d, 0)
        lr = np.log((np.maximum(d, 16).astype(f) / f(16)).astype(f)) / f(np.log(MAXD / 16))
        large = np.minimum(16 + (lr * f(16)).astype(np.int32), NBUCK - 1)
        return np.where(d < 16, d, large)
    near = bucket(255 - np.arange(384))
    far = bucket(PAST - np.arange(PAST + 1))
    onehot = (np.concatenate([near, far])[None, :] == np.arange(NBUCK)[:, None]).astype(f)
    cext = np.zeros((128, 512), f)
    cext[:, 384:] = np.where(np.arange(128)[None, :] <= np.arange(128)[:, None], 0.0, NEG)
    only = np.where(np.arange(128)[:, None] == np.arange(NB)[None, :], 0.0, NEG).astype(f)
    rows = np.arange(128)
    sel = np.zeros((128, 192), f)
    sel[rows, ((rows // 8) % 2) * 32 + rows // 16] = 1.0
    sel[rows, 64 + rows % 8] = 1.0

    r64 = np.arange(64)
    sel[r64, 72 + r64 // 8] = 1.0
    sel[rows, 80] = rows % 8
    sel_b = (np.arange(NB)[:, None] == (rows // 16)[None, :]).astype(f)
    return {"k_sel": sel, "k_selb": sel_b, "k_mats": mats.transpose(1, 0, 2).copy(), "k_rope": rope, "k_onehot": onehot,
            "k_cext": cext, "k_only": only}


def units():
    u = [("qlat", 3, 128), ("v", 1, 128), ("kvlat", 2, 128), ("kidx", 1, 128), ("krope", 1, 96)]
    u += [(f"q{t}", 1, 128) for t in range(4)] + [("k", 1, 128)]
    u += [(f"qi{t}", 1, 128) for t in range(4)] + [("widx", 1, 8)]
    u += [(f"qc{h}", 1, QK) for h in range(H)] + [(f"kn{h}", 1, NOPE) for h in range(H)]
    return u


def kind(name):
    return name.rstrip("0123456789")


NORMED = {"qlat", "kvlat", "krope", "q", "k", "qc", "kn"}
ROPED = {"krope", "qc"}


def build(nc, a, o):
    U = units()
    stack = ExitStack()
    with stack as ctx:
        place = {}

        def sb(name, shape, dt=F32):
            place[name] = (nc.sbuf_base + 31) // 32 * 32
            return ctx.enter_context(nc.sbuf_tensor(name, shape, dt))

        def rounded(name, shape):
            return nc.alloc_sbuf_tensor_at(name + "_r", shape, F32R, offset=place[name])

        sems = {}

        def sem(name):
            if name not in sems:
                sems[name] = ctx.enter_context(nc.semaphore(name))
            return sems[name]

        xT = sb("xT", [128, KD, T])
        hT = sb("hT", [128, KD, T])
        wide = sb("wide", [128, 24, T])
        r1 = sb("r1", [128, 8320])
        qiz = sb("qiz", [128, 8, T])
        wring = sb("wring", [128, 5632])
        latT = sb("latT", [128, 2, T])
        kT = sb("kT", [128, T])
        vT = sb("vT", [128, T])
        kidxT = sb("kidxT", [128, T])
        krF = sb("krF", [QK, T])
        tok = sb("tok", [128, 5, 608])
        msk = sb("msk", [128, 1152])
        wukv = sb("wukv", [128, 2, H * 128])
        rope = sb("rope", [QK, 2, T])
        mats = sb("mats", [128, 6, 128])
        modT = sb("modT", [128, 48, 9])
        amod = sb("amod", [128, 2, 8, 9])
        gT = sb("gT", [128, N_GAIN])
        epsc = sb("epsc", [128, 1])
        cext = sb("cext", [128, 512])
        wtok = sb("wtok", [128, 5, 8])
        psA = ctx.enter_context(nc.psum_tensor("psA", [128, 2, 2, 512], F32))
        psV = ctx.enter_context(nc.psum_tensor("psV", [128, 2, 2, 512], F32))

        ident, flip, ones = mats[:, 0, :], mats[:, 1, :], mats[:, 2, :]
        block64, block96, rot96 = mats[:, 3, :], mats[0:QK, 4, 0:QK], mats[0:QK, 5, 0:QK]
        qcat, kcat, qz = wide[:, 0:8, :], wide[:, 8:16, :], wide[:, 16:24, :]
        wflat = wide[:].rearrange("p a t -> p (a t)")
        ada9, bada9 = wflat[0:9, 0:6144], wflat[0:9, 6144:12288]
        xtok = hT[:].rearrange("p a t -> p (a t)")[:, 0:4096].rearrange("p (t d) -> p t d", t=4)
        xs9 = qiz[:].rearrange("p a t -> p (a t)")
        xsam, cin, csil, gin = xs9[0:8, 0:1024], xs9[0:9, 1024:2048], xs9[0:9, 2048:3072], xs9[0:N_GAIN, 3072:3200]
        cT = r1[:, 8000:8072].rearrange("p (k c) -> p k c", k=8)
        sqx = r1[:, 0:KD * T].rearrange("p (k t) -> p k t", k=KD)
        sq = r1[:, 0:4 * T].rearrange("p (k t) -> p k t", k=4)
        raw = r1[:, 4 * T:6 * T].rearrange("p (k t) -> p k t", k=2)
        sd = r1[:, 8 * T:10 * T].rearrange("p (k t) -> p k t", k=2)
        wuq = r1[:, 10 * T:10 * T + 2304].rearrange("p (k n) -> p k n", k=3)
        qlatT = wflat[:, 8 * T:11 * T].rearrange("p (k t) -> p k t", k=3)
        rtmp = r1[:, 6 * T:7 * T]
        halves = lambda ap: ap.rearrange("p (h t) -> p h t", h=2)

        nA = 0
        A_XT = [nA + i for i in range(7)]; nA += 7
        A_MOD = nA; nA += 1
        A_SS = nA; nA += 1
        A_proj, A_norm, V_rot = {}, {}, {}
        nV = 24
        for i in range(len(U) + 2):
            if i < len(U):
                A_proj[i] = [nA + t for t in range(U[i][1])]
                nA += U[i][1]
            if 1 <= i <= len(U) and kind(U[i - 1][0]) in NORMED:
                A_norm[i - 1] = nA; nA += 1
            if i >= 2 and kind(U[i - 2][0]) in ROPED:
                V_rot[i - 2] = nV; nV += 1
        A_TOK = nA; nA += 5
        A_WT = nA; nA += 1
        IQ = [(qt, h) for qt in range(1, 4) for h in range(H)]
        A_IQ = nA; nA += len(IQ)
        V_BIAS = nV; nV += 3
        A_VM = nA; nA += 4
        A_QS = nA; nA += 1
        V_KN = nV; nV += 1
        V_WC = nV; nV += 2
        A_IP = nA; nA += 16
        V_IS = nV; nV += 1
        V_ISW = nV; nV += 1
        AT = [(g, qt, h) for g in range(2) for qt in range(4) for h in range(H)]
        A_PT, V_S = nA, nV
        nA += len(AT); nV += len(AT)
        A_LT, V_KX = nA, nV
        nA += NB * NPG; nV += NB * NPG
        A_OL = nA; nA += 1
        V_OV = nV; nV += 1
        V_BF = nV; nV += 3
        A_KD, V_SD = nA, nV
        nA += 4 * NB; nV += 2
        V_SN = nV; nV += 1
        A_PD = nA; nA += 3
        A_OD = nA; nA += 1
        A_MIX = nA; nA += 2
        V_OUT = nV; nV += 8
        A_SS2 = nA; nA += 1
        PADA, PADV = nA % 2, nV % 2
        nA += PADA; nV += PADV
        A_G, V_U = nA, nV
        nA += KF; nV += KF
        V_DN = nV; nV += 8
        A_Y = nA; nA += 5
        win_tiles = [(i, t) for i in range(15) for t in range(U[i][1])]

        rb = r1[:, 0:1024].rearrange("p (s n) -> p s n", s=2)
        vm = r1[:, 1024:3072].rearrange("p (t n) -> p t n", t=4)
        sS = r1[:, 3072:4608].rearrange("p (s n) -> p s n", s=3)
        sP = r1[:, 4608:6144].rearrange("p (s n) -> p s n", s=3)
        sPT = r1[:, 6144:7680].rearrange("p (s n) -> p s n", s=3)
        ohn, g8, rbias = r1[0:32, 3072:3456], r1[0:8, 3456:3840], r1[0:32, 3840:3848]
        stat = sb("stat", [128, 3, 4])
        gated = sb("gated", [128, 2, 8])
        top8 = sb("top8", [128, 8])
        trev, toep = wring[:, 0:2048], wring[:, 2050:4098]
        by_sample = lambda x: wring[:, x * 136:(x + 1) * 136].rearrange("p (b s) -> p b s", b=NB)
        sct, key_i, key_hi, key_lo, above, equal, before = (by_sample(x) for x in range(7))
        as_int = lambda w: w.bitcast(I32)
        thr, cand, step_up, counts, room = (wring[:, 952 + 8 * x:960 + 8 * x] for x in range(5))
        ends = wring[:, 992:1008]
        earlier = wring[:, 1008:1136]
        totals = psA[:, 0, 1, :]
        ip = r1[:, 3848:5896].rearrange("p (s n) -> p s n", s=2)
        kiT = r1[:, 0:1024].rearrange("p (s n) -> p s n", s=2)
        irel = r1[:, 6144:7168]
        w1 = r1[:, 7168:8320]
        sel = sb("sel", [128, 192])
        selb = sb("selb", [NB, 128])
        ptab = sb("ptab", [128, NB], I32)
        rows_of = sb("rows_of", [128, NB], mybir.dt.uint32)
        wz = sb("wz", [128, 64])
        small = sb("small", [128, 64])
        rb64 = sb("rb64", [NBUCK, 64])
        qd = sb("qd", [128, 64])
        qdz = sb("qdz", [128, 576])
        ropeflat = rope[:].rearrange("p a t -> p (a t)")
        knew, pnsq = ropeflat[0:NB, 0:512], ropeflat[0:NB, 512:1024]
        ssnew = sb("ssnew", [NB, 8])
        qflat = qiz[:].rearrange("p a t -> p (a t)")
        bm64, s64, ohf = r1[0:64, 0:2049], r1[0:64, 2049:4098], r1[0:32, 2049:4098]
        qs8 = r1[0:NB, 3072:3840]
        qbc = r1[:, 0:6144].rearrange("p (b h d) -> p b h d", b=NB, h=H)
        rp = r1[:, 6144:8192].rearrange("p (s j h d) -> p s j h d", s=2, j=4, h=H)
        pgs = wflat[:, 0:9216].rearrange("p (s j n) -> p s j n", s=2, j=NPG)
        lT = wflat[:, 9216:9728].rearrange("p (s k n) -> p s k n", s=2, k=2)
        kx = [psV[:, V_KX % 2, 0, :], psV[:, (V_KX + 1) % 2, 0, :], psA[:, 0, 1, :], psA[:, 1, 1, :]]
        heads = lambda w: w.rearrange("p (h d) -> p h d", h=H)
        pr = [heads(w) for w in (wflat[:, 9728:10240], wflat[:, 10240:10752], wring[:, 3072:3584], wring[:, 3584:4096])]
        sqk = [heads(w) for w in (wflat[:, 10752:11264], wflat[:, 11264:11776], wring[:, 4096:4608], wring[:, 4608:5120])]
        m8 = lambda x: msk[:, x * 136:(x + 1) * 136].rearrange("p (j h) -> p j h", h=8)
        dots, sums, sfull, pm = [m8(0), m8(1)], [m8(2), m8(3)], [m8(4), m8(5)], [m8(6), m8(7)]
        newp = krF[0:NB, 0:512].rearrange("p (h d) -> p h d", h=H)
        onlyc = sb("onlyc", [128, NB])
        drope = [vT[:, x * 136:(x + 1) * 136].rearrange("p (j h) -> p j h", h=8) for x in range(2)]
        hstat = sb("hstat", [128, 4, 8])
        kdT = wring[:, 3072:4096].rearrange("p (s n) -> p s n", s=2)
        ptd = wring[:, 4096:5184].rearrange("p (j r) -> p j r", j=17)
        ptb = wring[:, 5184:5456].rearrange("p (s j h) -> p s j h", s=2, j=17)
        olb = r1[0:8, 0:2048].rearrange("p (b r) -> p b r", b=NB)
        olT = wflat[:, 11776:11904].rearrange("p (k r) -> p k r", k=2)
        kvp = [w.rearrange("p (j n) -> p j n", j=NPG) for w in (qflat[:, 0:4096], wflat[:, 0:4096], wflat[:, 4608:8704])]
        V_ORDER = (6, 7, 5, 0, 1, 2, 3, 4)
        V_LOADS = [16 * n for n in (3, 3, 2, 4, 4, 3, 5, 5)]
        od = wflat[0:8, 9728:10752].rearrange("p (b n) -> p b n", b=NB)
        odT = wflat[:, 10752:10816].rearrange("p (b h) -> p b h", b=NB)
        q_rows = nc.dram_tensor("q_rows", [NB, 768], F32, kind="Internal").ap()
        mask_rows = nc.dram_tensor("mask_rows", [NB, PAST + 1], F32, kind="Internal").ap()
        toepv = toep.rearrange("p (h n) -> p h n", h=H)
        mixT = hT
        bias_rows = nc.dram_tensor("bias_rows", [8, 384], F32, kind="Internal").ap()
        MQ = {1: (0, 256), 2: (256, 640), 3: (640, 1152)}
        actT = wide[:, 0:KF, :]
        yt = hT[:].rearrange("p a t -> p (a t)")[:, 0:2048].rearrange("p (s n) -> p s n", s=2)
        SPLIT, NT = 4, 8 + 2 * KF
        r1_r, wring_r = rounded("r1", [128, 8320]), rounded("wring", [128, 5632])
        hT_r, qiz_r, wide_r = rounded("hT", [128, KD, T]), rounded("qiz", [128, 8, T]), rounded("wide", [128, 24, T])
        tok_r, wukv_r = rounded("tok", [128, 5 * 608]), rounded("wukv", [128, 2 * H * 128])
        latT_r, kT_r, vT_r = rounded("latT", [128, 2, T]), rounded("kT", [128, T]), rounded("vT", [128, T])
        wraw = [wring[:, s * 1024:(s + 1) * 1024] for s in range(SPLIT)]
        wlow = [wring_r[:, s * 1024:(s + 1) * 1024] for s in range(SPLIT)]
        whigh = [r1_r[:, 5200 + s * 1024:6224 + s * 1024] for s in range(3)] + [wring_r[:, 4096:5120]]
        WD = KF // 2 * 128
        draw = [wring[:, s * WD:(s + 1) * WD] for s in range(SPLIT)]
        dlow = [wring_r[:, s * WD:(s + 1) * WD] for s in range(SPLIT)]
        qizflat_r = qiz_r[:].rearrange("p a t -> p (a t)")
        dhigh = [qizflat_r[:, 0:WD], qizflat_r[:, WD:2 * WD], r1_r[:, 5200:5200 + WD], r1_r[:, 5200 + WD:5200 + 2 * WD]]
        xhigh, xlow = qiz_r, hT_r
        alow = wide_r
        ahigh = ([r1_r[:, k * T:(k + 1) * T] for k in range(8)] + [wide_r[:, 22 + k, :] for k in range(2)] +
                 [tok_r[:, k * T:(k + 1) * T] for k in range(5)] + [wukv_r[:, k * T:(k + 1) * T] for k in range(3)] +
                 [latT_r[:, k, :] for k in range(2)] + [kT_r[:], vT_r[:]])
        pieces = lambda w: w.rearrange("p (k n) -> p k n", n=128)

        sa = lambda n: psA[:, n % 2]
        sv = lambda n: psV[:, n % 2]
        a_full, a_free, v_full, v_free = sem("a_full"), sem("a_free"), sem("v_full"), sem("v_free")
        in_loaded, const_loaded, bada_loaded, wres_loaded = sem("in_loaded"), sem("const_loaded"), sem("bada_loaded"), sem("wres_loaded")
        ada_w = [sem(f"ada_w{s}") for s in range(4)]
        aslot = lambda s: (wring[:, 0:2048], wring[:, 2048:4096], r1[:, 5200:7248],
                           tok[:].rearrange("p a n -> p (a n)")[:, 0:2048])[s].rearrange("p (k n) -> p k n", k=KD)
        win_w = [sem(f"win_w{s}") for s in range(4)]
        c_silu, eps_set, amod_done, hT_scaled, hT_done = sem("c_silu"), sem("eps_set"), sem("amod_done"), sem("hT_scaled"), sem("hT_done")
        zeroed, norm_done, rope_done, dve_chain, act_chain = sem("zeroed"), sem("norm_done"), sem("rope_done"), sem("dve_chain"), sem("act_chain")
        kr_spread, tokens_stored = sem("kr_spread"), sem("tokens_stored")
        sq_written = sem("sq_written")
        idx_acc, bias_loaded, bias_out, trev_loaded, toep_done = sem("idx_acc"), sem("bias_loaded"), sem("bias_out"), sem("trev_loaded"), sem("toep_done")
        mask_done, stats_ready, exp_done, p_ready, pv_done, o_free = (sem(x) for x in ("mask_done", "stats_ready", "exp_done", "p_ready", "pv_done", "o_free"))
        mixed, sq2_written, x_new, h2_scaled, h2_done = (sem(x) for x in ("mixed", "sq2_written", "x_new", "h2_scaled", "h2_done"))
        y_stored = [sem(f"y_stored{s}") for s in range(2)]
        ptab_loaded, qs_gained, qs_out, qbc_loaded, w1_ready, irel_ready, wz_ready, pn_ready = (sem(x) for x in (
            "ptab_loaded", "qs_gained", "qs_out", "qbc_loaded", "w1_ready", "irel_ready", "wz_ready", "pn_ready"))
        far_loaded, mask_out, mask_back, top_done, bm_ready = (sem(x) for x in ("far_loaded", "mask_out", "mask_back", "top_done", "bm_ready"))
        idx_pages = [sem(f"idx_pages{x}") for x in range(2)]
        mla_pages = [sem(f"mla_pages{x}") for x in range(2)]
        kv_rows = [sem(f"kv_rows{x}") for x in range(3)]
        squared, page_sums, rope_mul, rope_sum, ss_ready = (sem(x) for x in ("squared", "page_sums", "rope_mul", "rope_sum", "ss_ready"))
        smax, gmax, shifted, p_exp, psum_ready, gsum, pm_ready = (sem(x) for x in ("smax", "gmax", "shifted", "p_exp", "psum_ready", "gsum", "pm_ready"))
        lat_pv, lat_out, s64_ready, p64_exp, p64_ready, ptb_ready, d_pv, d_out = (sem(x) for x in (
            "lat_pv", "lat_out", "s64_ready", "p64_exp", "p64_ready", "ptb_ready", "d_pv", "d_out"))
        rows_ready, halved = sem("rows_ready"), sem("halved")
        new_score, new_in, cnt_ready, cnt_total = (sem(x) for x in ("new_score", "new_in", "cnt_ready", "cnt_total"))
        qbc_rest, totals_read = sem("qbc_rest"), sem("totals_read")
        STEPS = 32
        mix_s, neg_set, new_sums = sem("mix_s"), sem("neg_set"), sem("new_sums")
        tail_w = [sem(f"tail_w{s}") for s in range(4)]
        down_w = [sem(f"down_w{s}") for s in range(4)]
        down_used, w_high, w_split, x_high, x_split, a_high, a_split = (sem(x) for x in ("down_used", "w_high", "w_split", "x_high", "x_split", "a_high", "a_split"))
        normed = [i for i in range(len(U)) if kind(U[i][0]) in NORMED]
        roped = [i for i in range(len(U)) if kind(U[i][0]) in ROPED]
        UI = {U[i][0]: i for i in range(len(U))}

        def gain_col(name, t):
            k = kind(name)
            c = {"qlat": G_QL + t, "kvlat": G_KVL + t, "krope": G_KR, "q": G_DQ, "k": G_DK, "qc": G_Q, "kn": G_KN}[k]
            return c

        def sp_program(sp):
            for t in range(4):
                sp.dma_start(xtok[:, t, :], a["x_prompt"][0, t * 128:(t + 1) * 128, :]).then_inc(in_loaded, 16)
            sp.dma_start(xsam, a["x_sample"][:, 0, :]).then_inc(in_loaded, 16)
            sp.dma_start(cin[0:1, :], a["c_prompt"]).then_inc(in_loaded, 16)
            sp.dma_start(cin[1:9, :], a["c_sample"]).then_inc(in_loaded, 16)
            sp.wait_ge(eps_set, 1)
            row = lambda name: a[name].rearrange("l (k n) -> (l k) n", n=128)
            for c, name, n in ((G_MIX, "g_norm_mix", 8), (G_FFN, "g_norm_ffn", 8), (G_OUT, "g_out", 8),
                               (G_QL, "g_q_lat", 3), (G_KVL, "g_kv_lat", 2)):
                sp.dma_start(gin[c:c + n, :], row(name)).then_inc(in_loaded, 16)
            for c, o0, name in ((G_Q, 0, "g_mla_q_nope"), (G_Q, 64, "g_mla_q_rope"), (G_KN, 0, "g_mla_k_nope"),
                                (G_KN, 64, "g_mla_k_rope"), (G_DQ, 0, "g_dsa_q"), (G_DQ, 64, "g_dsa_q"),
                                (G_DK, 0, "g_dsa_k"), (G_DK, 64, "g_dsa_k")):
                n = a[name].shape[1]
                sp.dma_start(gin[c:c + 1, o0:o0 + n], a[name]).then_inc(in_loaded, 16)
            sp.dma_start(mats[:], a["k_mats"]).then_inc(in_loaded, 16)
            sp.dma_start(bada9, a["b_ada"].broadcast_to([9, 6144])).then_inc(bada_loaded, 16)
            wada = a["w_ada"][0].rearrange("(k p) n -> p k n", p=128)
            for s in range(4):
                sp.dma_start(aslot(s), wada[:, :, s * 256:(s + 1) * 256]).then_inc(ada_w[s], 16)
            sp.dma_start(rope[:], a["k_rope"]).then_inc(const_loaded, 16)
            sp.dma_start(cext[:], a["k_cext"]).then_inc(const_loaded, 16)
            sp.dma_start(sel[:], a["k_sel"]).then_inc(const_loaded, 16)
            sp.dma_start(selb[:], a["k_selb"]).then_inc(const_loaded, 16)
            sp.dma_start(onlyc[:], a["k_only"]).then_inc(const_loaded, 16)
            for r in range(8):
                sp.dma_start(ptab[r:128:8, :], bass.AP(a["page_table"].tensor, 0, [[1, NPG], [NPG, NB]]),
                             allow_slow_non_contiguous=True).then_inc(ptab_loaded, 16)
            with sp.Fori(1, 6) as i:
                for s in range(4):
                    sp.wait_ge(v_full, i * 4 + (s - 3))
                    sp.dma_start(aslot(s), wada[:, :, bass.ds(i * 1024 + s * 256, 256)]).then_inc(ada_w[s], 16)
            sp.wait_ge(a_full, A_SS + 1)
            sp.dma_start(wuq, a["w_uq"][0].rearrange("(k p) h d -> p k (h d)", p=128)).then_inc(wres_loaded, 16)
            sp.dma_start(wukv[:], a["w_ukv"][0].rearrange("(k p) h d -> p k (h d)", p=128)).then_inc(wres_loaded, 16)
            win = a["w_in"][0].rearrange("(k p) n -> p k n", p=128)
            sp.wait_ge(v_full, 24)
            for n, (i, t) in enumerate(win_tiles):
                if n >= 4:
                    pi, pt = win_tiles[n - 4]
                    sp.wait_ge(a_full, A_proj[pi][pt] + 1)
                dst = wring[:, (n % 4) * 1024:(n % 4 + 1) * 1024].rearrange("p (k n) -> p k n", k=KD)
                name = U[i][0]
                k = kind(name)
                j = int(name[-1]) if name[-1].isdigit() else 0
                if k == "q":
                    parts = [(0, C_Q + j * 64, 64), (64, C_Q + (j + 4) * 64, 64)]
                elif k == "kidx":
                    parts = [(0, C_KI, 64), (64, C_KI, 64)]
                else:
                    c = {"qlat": t * 128, "v": C_V, "kvlat": C_KV + t * 128, "krope": C_KR - 64, "k": C_K,
                         "qi": C_QI + j * 128, "widx": C_WI}[k]
                    parts = [(0, c, U[i][2])]
                for d0, c0, w in parts:
                    for kk in range(0, KD, 4):
                        sp.dma_start(dst[:, kk:kk + 4, d0:d0 + w], win[:, kk:kk + 4, c0:c0 + w]).then_inc(win_w[n % 4], 16)

            sp.wait_ge(norm_done, len(normed))
            sp.wait_ge(a_free, A_WT + 1)
            sp.dma_start(ohn, a["k_onehot"][:, 0:384]).then_inc(bias_loaded, 16)
            sp.dma_start(rbias, a["rel_bias"]).then_inc(bias_loaded, 16)
            sp.wait_ge(v_free, V_BIAS + 1)
            sp.dma_start(bias_rows, g8).then_inc(bias_out, 16)
            sp.wait_ge(bias_out, 16)
            sp.dma_start(trev.rearrange("p (h n) -> p h n", h=H),
                         bass.AP(bias_rows.tensor, 0, [[1, 128], [384, 8], [1, 256]])).then_inc(trev_loaded, 16)
            sp_decode(sp)
            sp_tail(sp)

        class Link:

            def __init__(self, v):
                self.v, self.n, self.turn = v, 0, None

            def __call__(self, ins):
                self.n += 1
                ins.then_inc(dve_chain, 1)
                self.v.wait_ge(dve_chain, self.n if self.turn is None else self.turn * PER_TURN + self.n)

            def per_loop(self, i, start, body):
                first = self.n
                self.turn, self.n = i, first - start * PER_TURN
                body()
                assert self.n - (first - start * PER_TURN) == PER_TURN, self.n - (first - start * PER_TURN)
                self.first = first

            def after_loop(self, turns=3):
                self.turn, self.n = None, self.first + turns * PER_TURN

        def at(b, k, c):
            if isinstance(b, tuple):
                return b[0] * (2 * k) + (b[1] * k + c)
            return b * k + c

        def sp_decode(sp):
            sp.wait_ge(a_free, A_QS + 1)
            sp.dma_start(q_rows, qs8).then_inc(qs_out, 16)
            sp.wait_ge(new_score, 1)
            sp.dma_start(sct[127:128, :, NPG:NPG + 1], small[0:NB, 32:33], allow_slow_non_contiguous=True).then_inc(new_in, 16)
            sp.wait_ge(pn_ready, 1)
            sp.wait_ge(qs_out, 16)
            for half, (turned, loaded) in enumerate(((len(AT) // 2, qbc_loaded), (len(AT), qbc_rest))):
                sp.wait_ge(p_ready, turned)
                sp.wait_ge(pv_done, turned)
                sp.wait_ge(a_full, A_PT + turned)
                sp.dma_start(qbc[:, 4 * half:4 * half + 4].rearrange("p b h d -> p (b h d)"),
                             bass.AP(q_rows.tensor, half * 4 * 768, [[0, 128], [1, 4 * 768]])).then_inc(loaded, 16)
            sp.wait_ge(top_done, 1)
            sp.dma_start(mask_rows[:, 0:PAST].rearrange("b (p s) -> p b s", s=NPG), sct[:, :, 0:NPG]).then_inc(mask_out, 16)
            sp.dma_start(mask_rows[:, PAST:PAST + 1].rearrange("b (p s) -> p b s", s=1), sct[127:128, :, NPG:NPG + 1],
                         allow_slow_non_contiguous=True).then_inc(mask_out, 16)
            sp.wait_ge(mask_out, 32)
            sp.wait_ge(lat_pv, NB)
            sp.dma_start(ohf, a["k_onehot"][:, 384:384 + PAST + 1]).then_inc(far_loaded, 16)
            sp.wait_ge(v_free, V_BF + 3)
            sp.dma_start(s64, bass.AP(mask_rows.tensor, 0, [[PAST + 1, NB], [0, 8], [1, PAST + 1]])).then_inc(mask_back, 16)

        def sp_tail(sp):
            wo = a["w_out"][0].rearrange("(k p) n -> p k n", p=128)
            wf = a["w_ffn_in"][0].rearrange("(k p) n -> p k n", p=128)
            wd = a["w_ffn_out"][0].rearrange("(k p) n -> p k n", p=128)

            def load(s, src, col):
                sp.dma_start(pieces(wraw[s]), src[:, :, bass.ds(col, 128)]).then_inc(tail_w[s], 16)

            sp.wait_ge(p_ready, len(AT))
            for s in range(3):
                load(s, wo, s * 128)
            sp.wait_ge(v_full, V_SD + 2)
            load(3, wo, 3 * 128)
            for n in range(4, 8):
                sp.wait_ge(v_full, V_OUT + n - 3)
                load(n % 4, wo, n * 128)
            for n in range(4):
                sp.wait_ge(v_full, V_OUT + n + 5)
                load(n, wf, (n % 2) * DFF + n // 2 * 128)
            with sp.Fori(1, KF // 2) as i:
                for s in range(4):
                    if s % 2 == 0:
                        sp.wait_ge(a_full, i * 2 + (A_G + s // 2 - 1))
                    else:
                        sp.wait_ge(v_full, i * 2 + (V_U + s // 2 - 1))
                    load(s, wf, i * 256 + ((s % 2) * DFF + s // 2 * 128))

            def load_down(s, m, half):
                sp.dma_start(pieces(draw[s]), wd[:, half * (KF // 2):(half + 1) * (KF // 2), bass.ds(m, 128)]).then_inc(down_w[s], 16)

            for s, full in enumerate((KF - 1, KF, KF, KF)):
                sp.wait_ge(v_full, V_U + full)
                load_down(s, s // 2 * 128, s % 2)
            with sp.Fori(1, 4) as i:
                for s in range(4):
                    if s % 2 == 0:
                        sp.wait_ge(down_used, i * 2 + (s // 2 - 1))
                    else:
                        sp.wait_ge(v_full, i * 2 + (V_DN + s // 2 - 1))
                    load_down(s, i * 256 + s // 2 * 128, s % 2)
            for t in range(5):
                w = 128 if t < 4 else NB
                sp.wait_ge(a_free, A_Y + t + 1)
                dst = o["y_p"][0, t * 128:(t + 1) * 128, :] if t < 4 else o["y_s"][:, 0, :]
                sp.dma_start(dst, yt[0:w, t % 2, :]).then_inc(y_stored[t % 2], 16)
            sp.wait_ge(y_stored[0], 48)
            sp.wait_ge(y_stored[1], 32)

        def win_count(n):
            c = 0
            for m in range(n % 4, n + 1, 4):
                k = kind(U[win_tiles[m][0]][0])
                c += 4 if k in ("q", "kidx") else 2
            return 16 * c

        def pe_program(pe):
            def sumsq(job, src, need, count):
                if job >= 2:
                    pe.wait_ge(a_free, job - 1)
                pe.wait_ge(need, count)
                for hf in range(2):
                    for k in range(KD):
                        mm = pe.matmul(sa(job)[:, hf, 0:HT], ones, src[:, k, hf * HT:(hf + 1) * HT],
                                       start=(k == 0), stop=(k == KD - 1))
                mm.then_inc(a_full, 1)

            pe.wait_ge(in_loaded, 16 * 21)
            for j, n in enumerate(A_XT):
                if n >= 2:
                    pe.wait_ge(a_free, n - 1)
                out = sa(n).rearrange("p b n -> p (b n)")
                if j < 4:
                    for k in range(KD):
                        mm = pe.transpose(out[:, k * 128:(k + 1) * 128], xtok[:, j, k * 128:(k + 1) * 128], ident)
                elif j == 4:
                    for k in range(KD):
                        mm = pe.transpose(out[:, k * 8:k * 8 + 8], xsam[:, k * 128:(k + 1) * 128], ident[0:8, 0:8])
                elif j == 5:
                    pe.wait_ge(c_silu, 1)
                    for k in range(KD):
                        mm = pe.transpose(out[:, k * 9:k * 9 + 9], csil[:, k * 128:(k + 1) * 128], ident[0:9, 0:9])
                else:
                    mm = pe.transpose(out[:, 0:N_GAIN], gin, ident[0:N_GAIN, 0:N_GAIN])
                mm.then_inc(a_full, 1)
            pe.wait_ge(a_free, A_XT[5] + 1)

            def ada_chunk(s, loads, n=None):
                pe.wait_ge(ada_w[s], loads)
                if n is not None:
                    pe.wait_ge(v_free, n)
                w = aslot(s)
                for k in range(KD):
                    mm = pe.matmul(psV[0:9, s % 2, 0, 0:256], cT[:, k, :], w[:, k, :], start=(k == 0), stop=(k == KD - 1))
                mm.then_inc(v_full, 1)

            for s in range(4):
                ada_chunk(s, 16, s - 1 if s >= 2 else None)
            with pe.Fori(1, 6) as i:
                for s in range(4):
                    ada_chunk(s, i * 16 + 16, i * 4 + (s - 1))
            pe.wait_ge(a_free, A_MOD - 1)
            pe.wait_ge(v_free, 24)
            for m in range(48):
                mm = pe.transpose(sa(A_MOD)[:, 0, m * 9:m * 9 + 9], ada9[:, m * 128:(m + 1) * 128], ident[0:9, 0:9])
            mm.then_inc(a_full, 1)
            sumsq(A_SS, sqx, sq_written, 8)

            wn = 0
            for i in range(len(U) + 2):
                if i < len(U):
                    name, nt, rows = U[i]
                    k = kind(name)
                    j = int(name[-1]) if name[-1].isdigit() else 0
                    for t in range(nt):
                        n = A_proj[i][t]
                        pe.wait_ge(a_free, n - 1)
                        if i < 15:
                            pe.wait_ge(win_w[wn % 4], win_count(wn))
                            w = wring[:, (wn % 4) * 1024:(wn % 4 + 1) * 1024].rearrange("p (k n) -> p k n", k=KD)
                            wn += 1
                            src, nk = hT, KD
                            lhs = lambda kk: w[:, kk, 0:rows]
                        elif k == "qc":
                            pe.wait_ge(wres_loaded, 32)
                            pe.wait_ge(norm_done, normed.index(UI["qlat"]) + 1)
                            src, nk = qlatT, 3
                            lhs = lambda kk: wuq[:, kk, j * QK:(j + 1) * QK]
                        else:
                            pe.wait_ge(norm_done, normed.index(UI["kvlat"]) + 1)
                            src, nk = latT, 2
                            lhs = lambda kk: wukv[:, kk, j * 128:j * 128 + 64]
                        for kk in range(nk):
                            if i == 0 and t == 0:
                                pe.wait_ge(hT_done, kk + 2)
                            for hf in range(2):
                                mm = pe.matmul(sa(n)[0:rows, hf, 0:HT], lhs(kk), src[:, kk, hf * HT:(hf + 1) * HT],
                                               start=(kk == 0), stop=(kk == nk - 1), skip_group_check=True)
                        mm.then_inc(a_full, 1)
                if i - 1 in A_norm:
                    name, nt, rows = U[i - 1]
                    k = kind(name)
                    n = A_norm[i - 1]
                    pe.wait_ge(a_free, max(n - 1, A_proj[i - 1][-1] + 1))
                    blk = {"qlat": ones, "kvlat": ones, "krope": block96, "qc": block96, "q": block64, "k": block64,
                           "kn": block96[0:64, 0:64]}[k]
                    for hf in range(2):
                        for t in range(nt):
                            s = SQ[i - 1] + t
                            mm = pe.matmul(sa(n)[0:rows, hf, 0:HT], blk, sq[0:rows, s % 4, hf * HT:(hf + 1) * HT],
                                           start=(t == 0), stop=(t == nt - 1))
                    mm.then_inc(a_full, 1)
                if i - 2 in V_rot:
                    n = V_rot[i - 2]
                    pe.wait_ge(v_free, n - 1)
                    pe.wait_ge(norm_done, normed.index(i - 2) + 1)
                    src = krF[:] if U[i - 2][0] == "krope" else qcat[0:QK, int(U[i - 2][0][-1]), :]
                    for hf in range(2):
                        mm = pe.matmul(sv(n)[0:QK, hf, 0:HT], rot96, src[:, hf * HT:(hf + 1) * HT], start=True, stop=True)
                    mm.then_inc(v_full, 1)
            pe.wait_ge(rope_done, 1)
            pe.wait_ge(norm_done, len(normed))
            for t in range(5):
                n = A_TOK + t
                pe.wait_ge(a_free, n - 1)
                c, w = t * 128, (128 if t < 4 else NB)
                for k in range(2):
                    pe.transpose(sa(n)[0:w, 0, k * 128:(k + 1) * 128], latT[:, k, c:c + w], ident)
                pe.transpose(sa(n)[0:w, 0, 256:256 + QK], krF[:, c:c + w], ident[0:QK, 0:QK])
                for j, src in enumerate((kT, vT, kidxT)):
                    mm = pe.transpose(sa(n)[0:w, 1, j * 128:(j + 1) * 128], src[:, c:c + w], ident)
                mm.then_inc(a_full, 1)
            n = A_WT
            pe.wait_ge(a_free, n - 1)
            for t in range(5):
                w = 128 if t < 4 else NB
                mm = pe.transpose(sa(n)[0:w, 0, t * 8:t * 8 + 8], widxT[:, t * 128:t * 128 + w], ident[0:8, 0:8])
            mm.then_inc(a_full, 1)

            for j, (qt, h) in enumerate(IQ):
                n = A_IQ + j
                pe.wait_ge(a_free, n - 1)
                mm = pe.matmul(sa(n)[:, 0, 0:(qt + 1) * 128], qiz[:, h, qt * 128:(qt + 1) * 128],
                               kidxT[:, 0:(qt + 1) * 128], start=True, stop=True)
                mm.then_inc(a_full, 1)
            pe.wait_ge(bias_loaded, 32)
            pe.wait_ge(v_free, V_BIAS - 1)
            pe.matmul(sv(V_BIAS)[0:8, 0, 0:384], rbias, ohn, start=True, stop=True).then_inc(v_full, 1)
            for t in range(4):
                n = A_VM + t
                pe.wait_ge(a_free, n - 1)
                for k in range(2):
                    mm = pe.matmul(sa(n)[:, 0, :], latT[:, k, t * 128:(t + 1) * 128],
                                   wukv[:, k, :].rearrange("p (h d) -> p h d", h=H)[:, :, 64:128], start=(k == 0), stop=(k == 1))
                mm.then_inc(a_full, 1)
            pe.wait_ge(trev_loaded, 16)
            for j in range(2):
                n = V_BIAS + 1 + j
                pe.wait_ge(v_free, n - 1)
                for b in range(2):
                    c = j * 1024 + b * 512
                    mm = pe.matmul(sv(n)[:, b, :], flip, trev[:, c:c + 512], start=True, stop=True)
                mm.then_inc(v_full, 1)
            pe.wait_ge(kr_spread, 1)
            pe.wait_ge(rope_done, len(roped))
            n = A_QS
            pe.wait_ge(a_free, n - 1)
            pe.wait_ge(qs_gained, 1)
            for h in range(H):
                mm = pe.transpose(sa(n)[0:NB, h // 4, (h % 4) * QK:(h % 4 + 1) * QK], qcat[0:QK, h, SEQ:T], ident[0:QK, 0:QK])
            mm.then_inc(a_full, 1)
            pe.wait_ge(v_free, V_KN - 1)
            for k in range(2):
                mm = pe.matmul(sv(V_KN)[0:NB, 0, :], latT[:, k, SEQ:T],
                               wukv[:, k, :].rearrange("p (h d) -> p h d", h=H)[:, :, 0:64], start=(k == 0), stop=(k == 1))
            mm.then_inc(v_full, 1)
            pe.wait_ge(const_loaded, 80)
            pe.wait_ge(v_free, V_WC - 1)
            pe.matmul(sv(V_WC)[:, 0, 0:8], selb[:], wtok[0:NB, 4, :], start=True, stop=True).then_inc(v_full, 1)
            pe.wait_ge(v_free, V_WC)
            pe.wait_ge(pn_ready, 1)
            for h in range(H):
                mm = pe.matmul(sv(V_WC + 1)[0:NB, 0, h:h + 1], irel[:, h * 8:h * 8 + 8], ones[:, 0:1], start=True, stop=True,
                               skip_group_check=True)
            mm.then_inc(v_full, 1)
            pe.wait_ge(w1_ready, 5)

            def idx_product(n):
                b, g = divmod(n, 2)
                pe.wait_ge(a_free, A_IP + n + 1)
                return pe.matmul(sv(V_IS)[:, g, :], w1[:, b * 128:(b + 1) * 128], kiT[:, n % 2, :], start=(b == 0), stop=(b == 7),
                                 skip_group_check=True)

            for x in range(17):
                if x < 16:
                    b, g = divmod(x, 2)
                    pe.wait_ge(idx_pages[b % 2], 16 * (b // 2 + 1))
                    pe.wait_ge(a_free, A_IP + x - 1)
                    for y in range(4):
                        c = g * 512 + y * 128
                        mm = pe.transpose(sa(A_IP + x)[:, 0, y * 128:(y + 1) * 128], ip[:, b % 2, c:c + 128], ident)
                    mm.then_inc(a_full, 1)
                if x == 1:
                    pe.wait_ge(v_free, V_IS - 1)
                if x >= 1:
                    mm = idx_product(x - 1)
            mm.then_inc(v_full, 1)
            pe.wait_ge(irel_ready, 1)
            pe.wait_ge(wz_ready, 1)
            pe.wait_ge(v_free, V_ISW - 1)
            for x in range(8):
                mm = pe.matmul(sv(V_ISW)[:, 0, x * 16:(x + 1) * 16], irel[:, x * 128:(x + 1) * 128],
                               wz[:].rearrange("p (two b) -> p b two", two=2)[:, 0:NB, :], start=True, stop=True, skip_group_check=True)
            mm.then_inc(v_full, 1)
            NA = len(AT)
            for u in range(-1, NA + 2):
                if u + 1 < NA:
                    g, qt, h = AT[u + 1]
                    n, qs, W = V_S + u + 1, slice(qt * 128, (qt + 1) * 128), (qt + 1) * 128
                    pe.wait_ge(v_free, n - 1)
                    lhs, rhs = (qcat[0:QK, h, qs], kcat[0:QK, h, 0:W]) if g == 0 else (qz[:, h, qs], kT[:, 0:W])
                    pe.matmul(sv(n)[:, 0, 0:W], lhs, rhs, start=True, stop=True).then_inc(v_full, 1)
                if u % 2 == 1 and 0 < u < NA:
                    pe.wait_ge(cnt_ready, u // 2 + 1)
                    pe.matmul(totals[:, 0:8], ones, counts, start=True, stop=True, skip_group_check=True).then_inc(cnt_total, 1)
                if 1 <= u <= NA:
                    g, qt, h = AT[u - 1]
                    n = A_PT + u - 1
                    pe.wait_ge(a_free, n - 1)
                    pe.wait_ge(p_ready, u)
                    for kt in range(qt + 1):
                        mm = pe.transpose(sa(n)[:, 0, kt * 128:(kt + 1) * 128], sP[:, (u - 1) % 3, kt * 128:(kt + 1) * 128], ident)
                    mm.then_inc(a_full, 1)
                if u >= 2:
                    g, qt, h = AT[u - 2]
                    pair, p0 = (u - 2) // 2, (h % 2) * 64
                    pe.wait_ge(a_free, A_PT + u - 1)
                    if pair >= 2 and h % 2 == 0:
                        pe.wait_ge(o_free, pair - 1)
                    for kt in range(qt + 1):
                        vv = vm[:, kt, h * 64:(h + 1) * 64] if g == 0 else tok[:, kt, 416 + (h // 4) * 64:480 + (h // 4) * 64]
                        mm = pe.matmul(psV[p0:p0 + 64, pair % 2, 1, 0:128], vv, sPT[:, (u - 2) % 3, kt * 128:(kt + 1) * 128],
                                       start=(kt == 0), stop=(kt == qt), skip_group_check=True)
                    mm.then_inc(pv_done, 1)
            pe.wait_ge(cnt_ready, STEPS + 1)
            pe.matmul(totals[:, 8:16], ones, ends[:, 0:8], start=True, stop=True, skip_group_check=True)
            pe.matmul(totals[:, 16:24], earlier, ends[:, 8:16], start=True, stop=True, skip_group_check=True).then_inc(cnt_total, 1)
            pe_decode(pe)
            pe_tail(pe)

        def pe_decode(pe):
            def turn(b, par, j):
                n = A_LT + j
                pe.wait_ge(a_free, at(b, NPG, n - 1))
                for k in range(2):
                    mm = pe.transpose(sa(n)[:, 0, k * 128:(k + 1) * 128], pgs[:, par, j, k * 128:(k + 1) * 128], ident)
                mm.then_inc(a_full, 1)

            def expand(b, j):
                n = V_KX + j
                pe.wait_ge(a_free, at(b, NPG, A_LT + j + 1))
                pe.wait_ge(v_free, V_KX if isinstance(b, int) and b == 0 and j < 4 else at(b, NPG, n - 3))
                for k in range(2):
                    mm = pe.matmul(kx[j % 4], lT[:, j % 2, k, :], wukv[:, k, :].rearrange("p (h d) -> p h d", h=H)[:, :, 0:64],
                                   start=(k == 0), stop=(k == 1), skip_group_check=True)
                mm.then_inc(v_full, 1)

            def pages(b, par, loads, prev=None):
                pe.wait_ge(mla_pages[par], loads)
                for j in range(NPG + 1):
                    if j < NPG:
                        turn(b, par, j)
                    if j >= 1:
                        expand(b, j - 1)
                    if j == 9 and prev is not None:
                        weigh(prev, 1 - par)

            def weigh(b, par):
                pe.wait_ge(pm_ready, at(b, 1, 1))
                pe.wait_ge(lat_out, at(b, 1, -1)) if not (isinstance(b, int) and b < 2) else None
                for j in range(NPG + 1):
                    rows = pgs[:, par, j, 0:KVR] if j < NPG else tok[:, 4, 0:KVR]
                    mm = pe.matmul(psV[0:8, par, 1, 0:KVR], pm[par][:, j, :], rows, start=(j == 0), stop=(j == NPG), skip_group_check=True)
                mm.then_inc(lat_pv, 1)

            pe.wait_ge(totals_read, 1)
            pages(0, 0, 16)
            pages(1, 1, 16, 0)
            with pe.Fori(1, 4) as i:
                pages((i, 0), 0, i * 16 + 16, (i, -1))
                pages((i, 1), 1, i * 16 + 16, (i, 0))
            weigh(7, 1)
            n = A_OL
            pe.wait_ge(a_free, n - 1)
            pe.wait_ge(lat_out, NB)
            for k in range(2):
                for b in range(NB):
                    c = k * 64 + b * 8
                    mm = pe.transpose(sa(n)[:, 0, c:c + 8], olb[:, b, k * 128:(k + 1) * 128], ident[0:8, 0:8])
            mm.then_inc(a_full, 1)
            pe.wait_ge(a_free, n + 1)
            pe.wait_ge(v_free, V_OV - 1)
            for h in range(H):
                for k in range(2):
                    mm = pe.matmul(sv(V_OV)[(h % 2) * 64:(h % 2) * 64 + 64, 0, (h // 2) * 8:(h // 2) * 8 + 8],
                                   wukv[:, k, h * 128 + 64:(h + 1) * 128], olT[:, k, :].rearrange("p (b h) -> p h b", b=NB)[:, h, :],
                                   start=(k == 0), stop=(k == 1), skip_group_check=True)
            mm.then_inc(v_full, 1)

            pe.wait_ge(far_loaded, 16)
            pe.wait_ge(pn_ready, 2)
            pe.wait_ge(o_free, len(AT) // 2)
            for x in range(3):
                n = V_BF + x
                pe.wait_ge(v_free, n - 1)
                for b in range(2):
                    c = (x * 2 + b) * 512
                    if c < PAST + 1:
                        w = min(512, PAST + 1 - c)
                        mm = pe.matmul(sv(n)[0:64, b, 0:w], rb64[:], ohf[:, c:c + w], start=True, stop=True)
                mm.then_inc(v_full, 1)

            def k_turn(b, c4):
                n = A_KD + b * 4 + c4
                pe.wait_ge(kv_rows[b % 3], 16 * (b // 3 + 1))
                pe.wait_ge(a_free, n - 1)
                for x in range(4):
                    mm = pe.transpose(sa(n)[:, 0, x * 128:(x + 1) * 128], kvp[b % 3][:, c4 * 4 + x, 0:128], ident)
                mm.then_inc(a_full, 1)

            def k_product(b, c4):
                n = V_SD + c4 // 2
                if b == 0 and c4 % 2 == 0:
                    pe.wait_ge(v_free, n - 1)
                pe.wait_ge(a_free, A_KD + b * 4 + c4 + 1)
                mm = pe.matmul(sv(n)[0:64, c4 % 2, :], qdz[:, b * 64:(b + 1) * 64], kdT[:, c4 % 2, :], start=(b == 0), stop=(b == 7),
                               skip_group_check=True)
                if b == 7 and c4 % 2 == 1:
                    mm.then_inc(v_full, 1)

            pe.wait_ge(lat_out, NB)
            for x in range(33):
                if x < 32:
                    k_turn(*divmod(x, 4))
                if x >= 1:
                    k_product(*divmod(x - 1, 4))
            pe.wait_ge(v_free, V_SN - 1)
            pe.matmul(sv(V_SN)[0:64, 0, 0:8], qd[:], kT[:, SEQ:T], start=True, stop=True).then_inc(v_full, 1)
            pe.wait_ge(p64_ready, 1)
            for x in range(3):
                n = A_PD + x
                pe.wait_ge(a_free, n - 1)
                if x < 2:
                    for j in range(8):
                        mm = pe.transpose(sa(n)[:, 0, j * 64:(j + 1) * 64], s64[:, (x * 8 + j) * 128:(x * 8 + j + 1) * 128], ident[0:64, 0:64])
                else:
                    mm = pe.transpose(sa(n)[0:NB, 0, 0:64], small[0:64, 0:8], ident[0:64, 0:64])
                mm.then_inc(a_full, 1)

            for t in range(NB):
                par = t % 2
                pe.wait_ge(kv_rows[t % 3], V_LOADS[t])
                pe.wait_ge(ptb_ready, t + 1)
                if t >= 2:
                    pe.wait_ge(d_out, t - 1)
                for j in range(NPG):
                    pe.matmul(psV[0:8, par, 1, 0:128], ptb[:, par, j, :], kvp[t % 3][:, j, 128:256], start=(j == 0), stop=False, skip_group_check=True)
                pe.matmul(psV[0:8, par, 1, 0:128], ptb[0:NB, par, NPG, :], tok[0:NB, 4, 416:544], start=False, stop=True,
                          skip_group_check=True).then_inc(d_pv, 1)

            n = A_OD
            pe.wait_ge(a_free, n - 1)
            pe.wait_ge(d_out, NB)
            for b in range(NB):
                mm = pe.transpose(sa(n)[:, 0, b * 8:b * 8 + 8], od[:, b, :], ident[0:8, 0:8])
            mm.then_inc(a_full, 1)

        def pe_tail(pe):
            for g in range(2):
                n = A_MIX + g
                pe.wait_ge(sq2_written, 4 * g + 4)
                pe.wait_ge(a_free, n - 1)
                for hf in range(2):
                    for k in range(4):
                        mm = pe.matmul(sa(n)[:, hf, 0:HT], ones, sqx[:, 4 * g + k, hf * HT:(hf + 1) * HT], start=(k == 0), stop=(k == 3))
                mm.then_inc(a_full, 1)

            def passes(low, high, src, out, k0=0, nk=KD, last=KD, need=None):
                for k in range(nk):
                    if need is not None and k % need[1] == 0:
                        pe.wait_ge(need[0], need[2] + (k0 + k) // need[1] + 1)
                    xh, xl = src(k0 + k)
                    for w, x in ((high, xh), (high, xl), (low, xh)):
                        for hf in range(2):
                            mm = pe.matmul(out[:, hf, 0:HT], w[:, k, :], x[:, hf * HT:(hf + 1) * HT],
                                           start=(k0 + k == 0 and x is xh and w is high), stop=(k0 + k == last - 1 and w is low),
                                           skip_group_check=True)
                return mm

            proj = lambda k: (xhigh[:, k, :], xlow[:, k, :])

            def out_turn(i, need=None):
                for s in range(4):
                    pe.wait_ge(w_split, i * 4 + (s + 1))
                    pe.wait_ge(v_free, i * 4 + (V_OUT + s - 1))
                    passes(pieces(wlow[s]), pieces(whigh[s]), proj, sv(V_OUT + s), need=need if s == 0 else None).then_inc(v_full, 1)

            out_turn(0, (x_split, 4, 0))
            out_turn(1)
            n = A_SS2
            pe.wait_ge(a_free, n - 1)
            pe.wait_ge(sq2_written, 16)
            for hf in range(2):
                for k in range(KD):
                    mm = pe.matmul(sa(n)[:, hf, 0:HT], ones, sqx[:, k, hf * HT:(hf + 1) * HT], start=(k == 0), stop=(k == KD - 1))
            mm.then_inc(a_full, 1)
            if PADA:
                pe.wait_ge(a_free, n + 1)
                pe.matmul(sa(n + 1)[0:1, 0, 0:1], ones[:, 0:1], ones[:, 0:1], start=True, stop=True).then_inc(a_full, 1)
            if PADV:
                pe.wait_ge(v_free, V_OUT + 8)
                pe.matmul(sv(V_OUT + 8)[0:1, 0, 0:1], ones[:, 0:1], ones[:, 0:1], start=True, stop=True).then_inc(v_full, 1)

            def ffn_turn(i, need=None):
                for s in range(4):
                    ring, free, full, base = ((sa(A_G + s // 2), a_free, a_full, A_G), (sv(V_U + s // 2), v_free, v_full, V_U))[s % 2]
                    pe.wait_ge(w_split, i * 4 + (8 + s + 1))
                    pe.wait_ge(free, i * 2 + (base + s // 2 - 1))
                    passes(pieces(wlow[s]), pieces(whigh[s]), proj, ring, need=need if s == 0 else None).then_inc(full, 1)

            ffn_turn(0, (x_split, 4, 2))
            with pe.Fori(1, KF // 2) as i:
                ffn_turn(i)
            down = lambda k: (ahigh[k], alow[:, k, :])

            def down_turn(i, need=None):
                for s in range(4):
                    m, half = divmod(s, 2)
                    pe.wait_ge(w_split, i * 4 + (NT + s + 1))
                    if half == 0:
                        pe.wait_ge(v_free, i * 2 + (V_DN + m - 1))
                    passes(pieces(dlow[s]), pieces(dhigh[s]), down, sv(V_DN + m), half * (KF // 2), KF // 2, KF,
                           need if m == 0 else None).then_inc((down_used, v_full)[half], 1)

            down_turn(0, (a_split, 1, 0))
            with pe.Fori(1, 4) as i:
                down_turn(i)
            pe.wait_ge(x_new, 16)
            for t in range(5):
                n, w = A_Y + t, (128 if t < 4 else NB)
                pe.wait_ge(a_free, n - 1)
                out = sa(n).rearrange("p b n -> p (b n)")
                for k in range(KD):
                    mm = pe.transpose(out[0:w, k * 128:(k + 1) * 128], xT[:, k, t * 128:t * 128 + w], ident)
                mm.then_inc(a_full, 1)

        SQ, s = {}, 0
        for i in normed:
            SQ[i] = s
            s += U[i][1]
        widxT = r1[0:8, 7 * T:8 * T]

        def act_program(act):
            A = nc.scalar.activation
            act.wait_ge(in_loaded, 16 * 21)
            A(csil, cin, ACT.Silu).then_inc(c_silu, 1)
            for j, n in enumerate(A_XT):
                act.wait_ge(a_full, n + 1)
                src = sa(n).rearrange("p b n -> p (b n)")
                if j < 4:
                    dst, src = xT[:, :, j * 128:(j + 1) * 128], src.rearrange("p (k n) -> p k n", k=KD)
                elif j == 4:
                    dst, src = xT[:, :, SEQ:T], src[:, 0:64].rearrange("p (k n) -> p k n", k=KD)
                elif j == 5:
                    dst, src = cT, src[:, 0:72].rearrange("p (k n) -> p k n", k=KD)
                else:
                    dst, src = gT[:], src[:, 0:N_GAIN]
                A(dst, src, ACT.Identity).then_inc(a_free, 1)
            act.wait_ge(a_free, A_XT[4] + 1)
            for k in range(KD):
                A(sqx[:, k, :], xT[:, k, :], ACT.Square).then_inc(sq_written, 1)
            act.wait_ge(a_full, A_MOD + 1)
            A(modT[:], sa(A_MOD)[:, 0, 0:432].rearrange("p (m c) -> p m c", m=48), ACT.Identity).then_inc(a_free, 1)
            act.wait_ge(eps_set, 1)
            act.wait_ge(a_full, A_SS + 1)
            A(halves(sd[:, 0, :]), sa(A_SS)[:, :, 0:HT], ACT.Sqrt, scale=1.0 / D, bias=epsc[:]).then_inc(a_free, 1)
            for k in range(KD):
                act.wait_ge(hT_scaled, k + 1)
                A(hT[:, k, 0:SEQ], hT[:, k, 0:SEQ], ACT.Identity, bias=modT[:, k, 0:1]).then_inc(hT_done, 1)
            act.wait_ge(zeroed, 2)
            for i in range(len(U) + 1):
                if i < len(U):
                    name, nt, rows = U[i]
                    k = kind(name)
                    j = int(name[-1]) if name[-1].isdigit() else 0
                    for t in range(nt):
                        n = A_proj[i][t]
                        act.wait_ge(a_full, n + 1)
                        src = sa(n)[0:rows, :, 0:HT]
                        if k in NORMED:
                            A(halves(sq[0:rows, (SQ[i] + t) % 4, :]), src, ACT.Square)
                            m = normed.index(i)
                            if k == "qlat":
                                dst = qlatT[:, t, :]
                            elif k == "kvlat":
                                dst = latT[:, t, :]
                            else:
                                if m >= 2:
                                    act.wait_ge(norm_done, m - 1)
                                dst = raw[0:rows, m % 2, :]
                            A(halves(dst), src, ACT.Identity).then_inc(a_free, 1)
                        elif k == "qi":
                            A(halves(qiz[0:64, 2 * j, :]), src[0:64], ACT.Identity)
                            A(halves(qiz[64:128, 2 * j + 1, :]), src[64:128], ACT.Identity).then_inc(a_free, 1)
                        else:
                            dst = {"v": vT[:], "kidx": kidxT[:], "widx": widxT}[k]
                            A(halves(dst), src, ACT.Identity).then_inc(a_free, 1)
                if i - 1 in A_norm:
                    name, nt, rows = U[i - 1]
                    m = normed.index(i - 1)
                    k = kind(name)
                    if m >= 2:
                        act.wait_ge(norm_done, m - 1)
                    act.wait_ge(a_full, A_norm[i - 1] + 1)
                    sc = {"qlat": 1.0 / QR, "kvlat": 1.0 / KVR, "q": 1.0 / HD, "k": 1.0 / HD}.get(k, 1.0)
                    A(halves(sd[0:rows, m % 2, :]), sa(A_norm[i - 1])[0:rows, :, 0:HT], ACT.Sqrt, scale=sc,
                      bias=epsc[0:rows]).then_inc(a_free, 1)
            for t in range(5):
                n = A_TOK + t
                w = 128 if t < 4 else NB
                act.wait_ge(a_full, n + 1)
                A(tok[0:w, t, 0:256], sa(n)[0:w, 0, 0:256], ACT.Identity)
                A(tok[0:w, t, 256:288], sa(n)[0:w, 0, 256 + 64:256 + 96], ACT.Identity)
                A(tok[0:w, t, 288:608], sa(n)[0:w, 1, 0:320], ACT.Identity).then_inc(a_free, 1)
            act.wait_ge(a_full, A_WT + 1)
            A(wtok[:, 0:4, :], sa(A_WT)[:, 0, 0:32].rearrange("p (t h) -> p t h", t=4), ACT.Identity, scale=IDX_SCALE)
            A(wtok[0:NB, 4, :], sa(A_WT)[0:NB, 0, 32:40], ACT.Identity, scale=IDX_SCALE).then_inc(a_free, 1)

            for j, (qt, h) in enumerate(IQ):
                n, W = A_IQ + j, (qt + 1) * 128
                act.wait_ge(a_full, n + 1)
                if j >= 2:
                    act.wait_ge(idx_acc, j - 1)
                A(rb[:, j % 2, 0:W], sa(n)[:, 0, 0:W], ACT.Relu).then_inc(a_free, 1)
            for t in range(4):
                n = A_VM + t
                act.wait_ge(a_full, n + 1)
                A(vm[:, t, :], sa(n)[:, 0, :], ACT.Identity).then_inc(a_free, 1)
            act.wait_ge(a_full, A_QS + 1)
            A(qs8.rearrange("b (x n) -> b x n", x=2), sa(A_QS)[0:NB, :, 0:4 * QK], ACT.Identity).then_inc(a_free, 1)
            act.wait_ge(v_full, V_KN + 1)
            act.wait_ge(v_free, V_KN + 1)
            A(pnsq, knew, ACT.Square).then_inc(new_sums, 1)
            act.wait_ge(idx_acc, len(IQ))
            for n in range(16):
                act.wait_ge(a_full, A_IP + n + 1)
                A(kiT[:, n % 2, :], sa(A_IP + n)[:, 0, :], ACT.Identity).then_inc(a_free, 1)
            NA = len(AT)
            for u in range(NA + 2):
                if u < NA:
                    g, qt, h = AT[u]
                    W = (qt + 1) * 128
                    act.wait_ge(stats_ready, u + 1)
                    if u >= 3:
                        act.wait_ge(a_full, A_PT + u - 2)
                    A(sP[:, u % 3, 0:W], sS[:, u % 3, 0:W], ACT.Exp, scale=(MLA_SCALE if g == 0 else 1.0),
                      bias=stat[:, u % 3, 1:2], accum_out=stat[:, u % 3, 2:3]).then_inc(exp_done, 1)
                if 1 <= u <= NA:
                    n, W = A_PT + u - 1, (AT[u - 1][1] + 1) * 128
                    act.wait_ge(a_full, n + 1)
                    if u - 1 >= 3:
                        act.wait_ge(pv_done, u - 3)
                    A(sPT[:, (u - 1) % 3, 0:W], sa(n)[:, 0, 0:W], ACT.Identity).then_inc(a_free, 1)
                if u >= 3 and u % 2 == 1:
                    g, qt, h = AT[u - 2]
                    pair = (u - 2) // 2
                    act.wait_ge(pv_done, u - 1)
                    A(mixT[:, 4 * g + h // 2, qt * 128:(qt + 1) * 128], psV[:, pair % 2, 1, 0:128], ACT.Identity).then_inc(o_free, 1)
            act_decode(act)
            act_tail(act)

        def act_decode(act):
            A = nc.scalar.activation

            def evacuate(b, par, j):
                act.wait_ge(a_full, at(b, NPG, A_LT + j + 1))
                A(lT[:, j % 2].rearrange("p k n -> p (k n)"), sa(A_LT + j)[:, 0, 0:256], ACT.Identity).then_inc(a_free, 1)

            def square(b, j):
                act.wait_ge(v_full, at(b, NPG, V_KX + j + 1))
                if not (isinstance(b, int) and b == 0 and j < 4):
                    act.wait_ge(page_sums, at(b, NPG, j - 3))
                A(sqk[j % 4], heads(kx[j % 4]), ACT.Square).then_inc(squared, 1)

            def roots(b, par):
                act.wait_ge(page_sums, at(b, NPG, NPG))
                A(sums[par], sums[par], ACT.Sqrt, scale=1.0 / NOPE, bias=epsc[:]).then_inc(ss_ready, 1)

            def exps(b, par):
                act.wait_ge(shifted, at(b, 1, 1))
                A(pm[par], pm[par], ACT.Exp, scale=MLA_SCALE).then_inc(p_exp, 1)

            def take(b, par):
                act.wait_ge(lat_pv, at(b, 1, 1))
                dst = olb[:, b, :] if isinstance(b, int) else olb[:, bass.ds(at(b, 1, 0), 1), :].rearrange("p b r -> p (b r)")
                A(dst, psV[0:8, par, 1, 0:KVR], ACT.Identity).then_inc(lat_out, 1)

            def pages(b, par, prev):
                for j in range(NPG + 1):
                    if j < NPG:
                        evacuate(b, par, j)
                    if j >= 1:
                        square(b, j - 1)
                    if prev is not None and j == 2:
                        roots(prev, 1 - par)
                    if prev is not None and j == 6:
                        exps(prev, 1 - par)
                    if prev is not None and j == 10:
                        take(prev, 1 - par)

            pages(0, 0, None)
            pages(1, 1, 0)
            with act.Fori(1, 4) as i:
                pages((i, 0), 0, (i, -1))
                pages((i, 1), 1, (i, 0))
            roots(7, 1)
            exps(7, 1)
            take(7, 1)
            act.wait_ge(a_full, A_OL + 1)
            A(olT.rearrange("p k r -> p (k r)"), sa(A_OL)[:, 0, 0:128], ACT.Identity).then_inc(a_free, 1)
            for x in range(32):
                n = A_KD + x
                act.wait_ge(a_full, n + 1)
                A(kdT[:, x % 2, :], sa(n)[:, 0, :], ACT.Identity).then_inc(a_free, 1)
            act.wait_ge(s64_ready, 1)
            A(s64, s64, ACT.Exp, bias=small[0:64, 9:10], accum_out=small[0:64, 10:11]).then_inc(p64_exp, 1)
            for x in range(3):
                act.wait_ge(a_full, A_PD + x + 1)
                dst, rows = (ptd[:, x * 8:x * 8 + 8, :].rearrange("p j r -> p (j r)"), 128) if x < 2 else (ptd[0:NB, 16, :], NB)
                A(dst, sa(A_PD + x)[0:rows, 0, 0:(512 if x < 2 else 64)], ACT.Identity).then_inc(a_free, 1)

            for t, b in enumerate(V_ORDER):
                act.wait_ge(d_pv, t + 1)
                A(od[:, b, :], psV[0:8, t % 2, 1, 0:128], ACT.Identity).then_inc(d_out, 1)
            act.wait_ge(a_full, A_OD + 1)
            A(odT.rearrange("p b h -> p (b h)"), sa(A_OD)[:, 0, 0:64], ACT.Identity).then_inc(a_free, 1)

        def act_tail(act):
            A = nc.scalar.activation
            act.wait_ge(o_free, len(AT) // 2)
            act.wait_ge(mix_s, 1)
            for k in range(KD):
                A(sqx[:, k, :], mixT[:, k, :], ACT.Square).then_inc(sq2_written, 1)
            for g in range(2):
                act.wait_ge(a_full, A_MIX + g + 1)
                A(halves(sd[:, g, :]), sa(A_MIX + g)[:, :, 0:HT], ACT.Sqrt, scale=1.0 / 512, bias=epsc[:]).then_inc(a_free, 1)
            act.wait_ge(x_new, 8)
            for k in range(KD):
                A(sqx[:, k, :], xT[:, k, :], ACT.Square).then_inc(sq2_written, 1)
            act.wait_ge(a_full, A_SS2 + 1)
            A(halves(sd[:, 0, :]), sa(A_SS2)[:, :, 0:HT], ACT.Sqrt, scale=1.0 / D, bias=epsc[:]).then_inc(a_free, 1)
            for k in range(KD):
                act.wait_ge(h2_scaled, k + 1)
                A(hT[:, k, 0:SEQ], hT[:, k, 0:SEQ], ACT.Identity, bias=modT[:, 24 + k, 0:1]).then_inc(h2_done, 1)
            if PADA:
                act.wait_ge(a_full, A_SS2 + 2)
                A(stat[0:1, 0, 0:1], sa(A_SS2 + 1)[0:1, 0, 0:1], ACT.Identity).then_inc(a_free, 1)
            with act.Fori(0, KF // 2) as i:
                for s in range(2):
                    act.wait_ge(a_full, i * 2 + (A_G + s + 1))
                    A(actT[:, bass.ds(i * 2 + s, 1), :].rearrange("p a (h t) -> p (a h) t", h=2), sa(A_G + s)[:, :, 0:HT],
                      ACT.Silu).then_inc(a_free, 1)
            for t in range(5):
                n, w = A_Y + t, (128 if t < 4 else NB)
                act.wait_ge(a_full, n + 1)
                if t >= 2:
                    act.wait_ge(y_stored[t % 2], 16 * (t // 2))
                A(yt[0:w, t % 2, :], sa(n)[0:w].rearrange("p b n -> p (b n)"), ACT.Identity).then_inc(a_free, 1)

        def dve_program(v):
            link = Link(v)

            v.memset(gin, 0.0)
            v.memset(epsc[:], EPS).then_inc(eps_set, 1)
            v.wait_ge(bada_loaded, 16)
            v.wait_ge(v_full, 1)

            def ada_rows(s, col, full):
                v.wait_ge(v_full, full)
                v.tensor_tensor(ada9[:, bass.ds(col, 256)], psV[0:9, s, 0, 0:256], bada9[:, bass.ds(col, 256)],
                                ALU.add).then_inc(v_free, 1)

            with v.Fori(0, 12) as i:
                for s in range(2):
                    ada_rows(s, i * 512 + s * 256, i * 2 + (s + 1))
            v.wait_ge(a_free, A_MOD + 1)
            for w, sc in ((0, 8), (1, 32)):
                link(v.scalar_tensor_tensor(amod[:, w], modT[:, sc:sc + 8, :], 1.0,
                                            gT[:, w * 8:w * 8 + 8].unsqueeze(2).broadcast_to([128, 8, 9]), ALU.add, ALU.mult))
            modulate(v, link, 0)
            v.wait_ge(zeroed, 2)
            for i in range(1, len(U) + 2):
                if i - 1 in A_norm:
                    name, nt, rows = U[i - 1]
                    k = kind(name)
                    j = int(name[-1]) if name[-1].isdigit() else 0
                    m = normed.index(i - 1)
                    v.wait_ge(a_free, A_norm[i - 1] + 1)
                    r = sd[0:rows, m % 2, :]
                    link(v.reciprocal(r, r))
                    for t in range(nt):
                        g = gT[0:rows, gain_col(name, t):gain_col(name, t) + 1]
                        if k == "q":
                            for p0, hh in ((0, j), (64, j + 4)):
                                ins = v.scalar_tensor_tensor(qz[p0:p0 + 64, hh, :], raw[p0:p0 + 64, m % 2, :], g[p0:p0 + 64],
                                                             r[p0:p0 + 64], ALU.mult, ALU.mult)
                        elif k == "kn":
                            ins = v.scalar_tensor_tensor(kcat[0:64, j, :], raw[0:64, m % 2, :], g, r, ALU.mult, ALU.mult)
                        else:
                            if k == "qlat":
                                src = dst = qlatT[:, t, :]
                            elif k == "kvlat":
                                src = dst = latT[:, t, :]
                            else:
                                src = raw[0:rows, m % 2, :]
                                dst = {"krope": krF[:], "k": kT[:], "qc": qcat[0:QK, j, :]}[k]
                            ins = v.scalar_tensor_tensor(dst, src, g, r, ALU.mult, ALU.mult)
                    ins.then_inc(norm_done, 1)
                if i - 2 in V_rot:
                    n = V_rot[i - 2]
                    dst = (krF[64:96, :] if U[i - 2][0] == "krope" else qcat[64:96, int(U[i - 2][0][-1]), :])
                    v.wait_ge(v_full, n + 1)
                    v.tensor_tensor(halves(rtmp[64:96, :]), sv(n)[64:96, :, 0:HT], halves(rope[64:96, 1, :]),
                                    ALU.mult).then_inc(v_free, 1)
                    v.wait_ge(norm_done, normed.index(i - 2) + 1)
                    link(v.tensor_tensor(dst, dst, rope[64:96, 0, :], ALU.mult))
                    v.wait_ge(v_free, n + 1)
                    v.tensor_tensor(dst, dst, rtmp[64:96, :], ALU.add).then_inc(rope_done, 1)
            v.wait_ge(rope_done, 1)
            v.tensor_copy(kcat[64:96, :, :], krF[64:96, :].unsqueeze(1).broadcast_to([32, 8, T])).then_inc(kr_spread, 1)

            for j, (qt, h) in enumerate(IQ):
                m0, m1 = MQ[qt]
                v.wait_ge(a_free, A_IQ + j + 1)
                if h > 0:
                    v.wait_ge(idx_acc, j)
                    v.scalar_tensor_tensor(msk[:, m0:m1], rb[:, j % 2, 0:m1 - m0], wtok[:, qt, h:h + 1], msk[:, m0:m1],
                                           ALU.mult, ALU.add).then_inc(idx_acc, 1)
                else:
                    v.tensor_scalar(msk[:, m0:m1], rb[:, j % 2, 0:m1 - m0], wtok[:, qt, h:h + 1], None, ALU.mult).then_inc(idx_acc, 1)
            v.wait_ge(idx_acc, len(IQ))
            for qt in range(1, 4):
                m1 = MQ[qt][1]
                link(v.tensor_tensor(msk[:, m1 - 128:m1], msk[:, m1 - 128:m1], cext[:, 384:512], ALU.add))
            v.wait_ge(v_full, V_BIAS + 1)
            v.tensor_copy(g8, sv(V_BIAS)[0:8, 0, 0:384]).then_inc(v_free, 1)
            for j in range(2):
                n = V_BIAS + 1 + j
                v.wait_ge(v_full, n + 1)
                v.tensor_copy(toep[:, j * 1024:(j + 1) * 1024], sv(n).rearrange("p b n -> p (b n)")).then_inc(v_free, 1)

            v.wait_ge(ptab_loaded, 128)
            v.tensor_scalar(rows_of[:], ptab[:], 8.0, sel[:, 80:81], ALU.mult, ALU.add).then_inc(rows_ready, 1)
            link(v.memset(w1, 0.0))
            v.memset(ptd[:, NPG, :], 0.0)
            v.wait_ge(norm_done, len(normed))
            v.tensor_scalar(qcat[0:64, :, SEQ:T], qcat[0:64, :, SEQ:T], gT[0:64, G_KN:G_KN + 1], None, ALU.mult).then_inc(qs_gained, 1)
            w1v = w1.rearrange("p (b x) -> p b x", x=144)
            for p0, c in ((0, 0), (64, 8)):
                for odd in range(2):
                    v.tensor_copy(w1v[p0:p0 + 64, :, c + odd:c + 8:2],
                                  qiz[odd * 64:odd * 64 + 64, odd:8:2, SEQ:T].rearrange("p h b -> p b h")).then_inc(w1_ready, 1)
            link(v.tensor_copy(qd[:].rearrange("p (b h) -> p b h", b=NB), qz[:, :, SEQ:T].rearrange("p h b -> p b h")))
            link(v.memset(qdz[:], 0.0))
            v.tensor_copy(qdz[:].rearrange("p (b x) -> p b x", x=72)[:, :, 0:8], qd[:].rearrange("p (b h) -> p b h", b=NB)).then_inc(w1_ready, 1)
            v.wait_ge(v_full, V_KN + 1)
            v.tensor_copy(knew, sv(V_KN)[0:NB, 0, :]).then_inc(v_free, 1)
            v.wait_ge(const_loaded, 80)
            v.wait_ge(v_full, V_WC + 1)
            v.tensor_tensor_reduce(small[:, 0:8], sv(V_WC)[:, 0, 0:8], sel[:, 64:72], 1.0, 0.0, ALU.mult, ALU.add,
                                   small[:, 8:9]).then_inc(v_free, 1)
            v.wait_ge(v_free, V_WC + 1)
            v.tensor_scalar(wz[:], sel[:, 0:64], small[:, 8:9], None, ALU.mult).then_inc(wz_ready, 1)
            v.tensor_tensor(irel[:, 0:64].rearrange("p (h b) -> p h b", h=H), qiz[:, :, SEQ:T],
                            kidxT[:, SEQ:T].unsqueeze(1).broadcast_to([128, H, NB]), ALU.mult).then_inc(pn_ready, 1)
            v.wait_ge(v_full, V_WC + 2)
            v.tensor_scalar(small[0:NB, 16:24], sv(V_WC + 1)[0:NB, 0, 0:8], 0.0, None, ALU.max).then_inc(v_free, 1)
            v.wait_ge(v_free, V_WC + 2)
            link(v.tensor_tensor_reduce(small[0:NB, 24:32], small[0:NB, 16:24], wtok[0:NB, 4, :], 1.0, 0.0, ALU.mult, ALU.add,
                                        small[0:NB, 32:33]))
            v.memset(sct[:, :, NPG:NPG + 1], TAKEN).then_inc(new_score, 1)
            v.wait_ge(new_sums, 1)
            link(v.tensor_reduce(ssnew[:], pnsq.rearrange("p (h d) -> p h d", h=H), AXX, ALU.add))
            link(v.tensor_copy(rb64[:].rearrange("p (b h) -> p b h", b=NB), rbias.unsqueeze(1).broadcast_to([NBUCK, NB, 8])))
            v.tensor_scalar(small[:, 40:41], small[:, 8:9], 0.0, None, ALU.mult).then_inc(pn_ready, 1)
            v.wait_ge(v_full, V_IS + 1)
            v.tensor_scalar(irel, sv(V_IS).rearrange("p b n -> p (b n)"), 0.0, None, ALU.max).then_inc(v_free, 1)
            v.wait_ge(v_free, V_IS + 1)
            v.tensor_scalar(small[:, 41:42], small[:, 8:9], 0.0, None, ALU.mult).then_inc(irel_ready, 1)
            v.wait_ge(v_full, V_ISW + 1)
            v.tensor_copy(sct[:, :, 0:NPG].rearrange("p b (x two) -> p x b two", two=2),
                          sv(V_ISW)[:, 0, 0:128].rearrange("p (x b two) -> p x b two", x=8, two=2)).then_inc(v_free, 1)
            v.wait_ge(v_free, V_ISW + 1)
            v.wait_ge(new_in, 16)

            def top_rounds():
                for qt in range(1, 4):
                    m0, m1 = MQ[qt]
                    for r in range(TOPK_P // 8):
                        link(v.max(top8[:], msk[:, m0:m1]))
                        link(v.match_replace(msk[:, m0:m1], top8[:], msk[:, m0:m1], TAKEN))
                        yield
                    link(v.tensor_scalar(msk[:, m0:m1], msk[:, m0:m1], TAKEN / 2, NEG, ALU.is_gt, ALU.mult))

            over = lambda w: w.unsqueeze(2).broadcast_to([128, NB, NPG + 1])

            def search():
                link(v.tensor_scalar(sct, sct, 0.0, None, ALU.add))
                link(v.tensor_scalar(as_int(key_i), as_int(sct), 31, -2 ** 31, ALU.arith_shift_right, ALU.bitwise_or))
                link(v.tensor_tensor(as_int(key_i), as_int(sct), as_int(key_i), ALU.bitwise_xor))
                link(v.tensor_scalar(as_int(above), as_int(key_i), 16, 0xFFFF, ALU.arith_shift_right, ALU.bitwise_and))
                link(v.tensor_scalar(as_int(equal), as_int(key_i), 0xFFFF, None, ALU.bitwise_and))
                link(v.tensor_copy(key_hi, as_int(above)))
                link(v.tensor_copy(key_lo, as_int(equal)))
                link(v.tensor_scalar(earlier, cext[:, 384:512], -1.0, None, ALU.is_lt))
                link(v.memset(thr, 0.0))
                for k in range(STEPS):
                    keys, bit = (key_hi, key_lo)[k // 16], float(2 ** (15 - k % 16))
                    link(v.tensor_scalar(cand, thr, bit, None, ALU.add))
                    link(v.tensor_tensor(above, keys, over(cand), ALU.is_ge))
                    v.tensor_reduce(counts, above, AXX, ALU.add).then_inc(cnt_ready, 1)
                    yield
                    v.wait_ge(cnt_total, k + 1)
                    link(v.tensor_scalar(step_up, totals[:, 0:8], TOPK_S - 0.5, bit, ALU.is_gt, ALU.mult))
                    link(v.tensor_tensor(thr, thr, step_up, ALU.add))
                    if k == 15:
                        link(v.tensor_tensor(above, key_hi, over(thr), ALU.is_gt))
                        link(v.tensor_tensor(equal, key_hi, over(thr), ALU.is_equal))
                        link(v.scalar_tensor_tensor(key_lo, key_lo, 1.0, equal, ALU.add, ALU.mult))
                        link(v.scalar_tensor_tensor(key_lo, above, 65537.0, key_lo, ALU.mult, ALU.add))
                        link(v.tensor_scalar(key_lo, key_lo, -1.0, None, ALU.add))
                        link(v.memset(thr, 0.0))
                    yield
                link(v.tensor_tensor(above, key_lo, over(thr), ALU.is_gt))
                link(v.tensor_tensor(equal, key_lo, over(thr), ALU.is_equal))
                v.tensor_reduce(ends[:, 0:8], above, AXX, ALU.add)
                v.tensor_reduce(ends[:, 8:16], equal, AXX, ALU.add).then_inc(cnt_ready, 1)
                v.wait_ge(cnt_total, STEPS + 1)
                link(v.tensor_copy(room, totals[:, 8:16]))
                v.tensor_tensor(room, room, totals[:, 16:24], ALU.add).then_inc(totals_read, 1)
                v.wait_ge(totals_read, 1)
                link(v.memset(before[:, :, 0:1], 0.0))
                for s in range(NPG):
                    link(v.tensor_tensor(before[:, :, s + 1:s + 2], before[:, :, s:s + 1], equal[:, :, s:s + 1], ALU.add))
                link(v.tensor_scalar(room, room, -1.0, float(TOPK_S), ALU.mult, ALU.add))
                link(v.tensor_tensor(before, before, over(room), ALU.is_lt))
                link(v.tensor_tensor(before, before, equal, ALU.mult))
                link(v.tensor_tensor(before, before, above, ALU.add))
                v.tensor_scalar(sct, before, 0.5, NEG, ALU.is_lt, ALU.mult).then_inc(top_done, 1)

            rounds, steps = top_rounds(), search()
            v.wait_ge(qs_out, 16)
            NA = len(AT)
            for u in range(NA + 1):
                if u < NA:
                    g, qt, h = AT[u]
                    n, W, c = V_S + u, (qt + 1) * 128, u % 3
                    S = sS[:, c, 0:W]
                    v.wait_ge(v_full, n + 1)
                    if u >= 3:
                        v.wait_ge(exp_done, u - 2)
                    if g == 0:
                        v.tensor_tensor_reduce(S, sv(n)[:, 0, 0:W], cext[:, 512 - W:512], 1.0, TAKEN, ALU.add, ALU.max,
                                               stat[:, c, 0:1]).then_inc(v_free, 1)
                        v.wait_ge(v_free, n + 1)
                        v.tensor_scalar(stat[:, c, 1:2], stat[:, c, 0:1], -MLA_SCALE, None, ALU.mult).then_inc(stats_ready, 1)
                    else:
                        near = min(W, 256)
                        if W > near:
                            link(v.tensor_scalar(S[:, 0:W - near], sv(n)[:, 0, 0:W - near], DSA_SCALE, toepv[:, h, 0:1], ALU.mult, ALU.add))
                        v.scalar_tensor_tensor(S[:, W - near:W], sv(n)[:, 0, W - near:W], DSA_SCALE, toepv[:, h, 256 - near:256],
                                               ALU.mult, ALU.add).then_inc(v_free, 1)
                        v.wait_ge(v_free, n + 1)
                        mask = cext[:, 384:512] if qt == 0 else msk[:, MQ[qt][0]:MQ[qt][1]]
                        link(v.tensor_tensor_reduce(S, S, mask, 1.0, TAKEN, ALU.add, ALU.max, stat[:, c, 0:1]))
                        v.tensor_scalar(stat[:, c, 1:2], stat[:, c, 0:1], -1.0, None, ALU.mult).then_inc(stats_ready, 1)
                if u >= 1:
                    c, W = (u - 1) % 3, (AT[u - 1][1] + 1) * 128
                    v.wait_ge(exp_done, u)
                    link(v.reciprocal(stat[:, c, 3:4], stat[:, c, 2:3]))
                    v.tensor_scalar(sP[:, c, 0:W], sP[:, c, 0:W], stat[:, c, 3:4], None, ALU.mult).then_inc(p_ready, 1)
                for _ in range(2 if u % 2 or u == 0 else 1):
                    next(rounds, None)
                if u < NA:
                    next(steps)
            for _ in steps:
                pass
            dve_decode(v, link)
            dve_tail(v, link)

        def dve_decode(v, link):
            link(v.memset(small[:, 42:43], 0.0))
            v.wait_ge(qbc_loaded, 16)
            for x in range(2):
                v.memset(sfull[x][:, NPG, :], NEG)
                ins = v.memset(sums[x][:, NPG, :], 1.0)
            ins.then_inc(neg_set, 1)
            v.wait_ge(neg_set, 1)

            def query(b):
                return qbc[:, b] if isinstance(b, int) else qbc[:, bass.ds(at(b, 1, 0), 1)].rearrange("p a h d -> p (a h) d")

            def dot(b, par, j):
                n = V_KX + j
                v.wait_ge(squared, at(b, NPG, j + 1))
                if not (isinstance(b, int) and b == 0 and j < 4):
                    v.wait_ge(page_sums, at(b, NPG, j - 3))
                v.tensor_tensor(pr[j % 4], heads(kx[j % 4]), query(b)[:, :, 0:NOPE], ALU.mult).then_inc(v_free, 1)

            def head_sums(b, par, j):
                v.wait_ge(halved, at(b, NPG, j + 1))
                v.tensor_reduce(dots[par][:, j, :], pr[j % 4][:, :, 0:32], AXX, ALU.add)
                v.tensor_reduce(sums[par][:, j, :], sqk[j % 4][:, :, 0:32], AXX, ALU.add).then_inc(page_sums, 1)

            def rope_part(b, par, c):
                v.wait_ge(rope_mul, at(b, 4, c + 1))
                v.tensor_reduce(drope[par][:, 4 * c:4 * c + 4, :], rp[:, c % 2], AXX, ALU.add).then_inc(rope_sum, 1)

            def new_row(b, par):
                q = query(b)
                big = newp
                link(v.tensor_tensor(big[:, :, 0:64], knew.rearrange("p (h d) -> p h d", h=H), q[0:NB, :, 0:64], ALU.mult))
                link(v.tensor_reduce(dots[par][0:NB, NPG, :], big[:, :, 0:64], AXX, ALU.add))
                link(v.tensor_tensor(big[:, :, 0:32], tok[0:NB, 4, KVR:ROW].unsqueeze(1).broadcast_to([NB, H, ROPE]), q[0:NB, :, 64:96], ALU.mult))
                link(v.tensor_reduce(drope[par][0:NB, NPG, :], big[:, :, 0:32], AXX, ALU.add))
                v.tensor_copy(sums[par][0:NB, NPG, :], ssnew[:])

            def scores(b, par):
                v.wait_ge(ss_ready, at(b, 1, 1))
                link(v.reciprocal(sums[par], sums[par]))
                link(v.tensor_tensor(dots[par][:, 0:NPG], dots[par][:, 0:NPG], sums[par][:, 0:NPG], ALU.mult))
                link(v.tensor_tensor(dots[par][0:NB, NPG], dots[par][0:NB, NPG], sums[par][0:NB, NPG], ALU.mult))
                link(v.tensor_tensor(sfull[par][:, 0:NPG], dots[par][:, 0:NPG], drope[par][:, 0:NPG], ALU.add))
                link(v.tensor_tensor(sfull[par][0:NB, NPG], dots[par][0:NB, NPG], drope[par][0:NB, NPG], ALU.add))
                only = onlyc[0:NB, b:b + 1] if isinstance(b, int) else onlyc[0:NB, bass.ds(at(b, 1, 0), 1)]
                link(v.tensor_scalar(sfull[par][0:NB, NPG], sfull[par][0:NB, NPG], only, None, ALU.add))
                v.tensor_reduce(hstat[:, 0, :], sfull[par].rearrange("p j h -> p h j"), AXX, ALU.max).then_inc(smax, 1)

            def shift(b, par):
                v.wait_ge(gmax, at(b, 1, 1))
                v.tensor_tensor(pm[par], sfull[par], hstat[:, 1, :].unsqueeze(1).broadcast_to([128, NPG + 1, 8]), ALU.subtract).then_inc(shifted, 1)

            def row_sums(b, par):
                v.wait_ge(p_exp, at(b, 1, 1))
                v.tensor_reduce(hstat[:, 2, :], pm[par].rearrange("p j h -> p h j"), AXX, ALU.add).then_inc(psum_ready, 1)

            def normalise(b, par):
                v.wait_ge(gsum, at(b, 1, 1))
                link(v.reciprocal(hstat[:, 3, :], hstat[:, 3, :]))
                v.tensor_tensor(pm[par], pm[par], hstat[:, 3, :].unsqueeze(1).broadcast_to([128, NPG + 1, 8]), ALU.mult).then_inc(pm_ready, 1)

            def pages(b, par, prev):
                for j in range(NPG):
                    dot(b, par, j)
                    if j >= 2:
                        head_sums(b, par, j - 2)
                    elif prev is not None:
                        head_sums(prev, 1 - par, NPG - 2 + j)
                    if j % 4 == 3:
                        rope_part(b, par, j // 4)
                    if prev is not None:
                        for at_j, step in ((2, scores), (4, shift), (6, row_sums), (7, normalise)):
                            if j == at_j:
                                step(prev, 1 - par)
                    if j == 12:
                        new_row(b, par)

            pages(0, 0, None)
            pages(1, 1, 0)
            v.wait_ge(qbc_rest, 16)
            with v.Fori(1, 4) as i:
                link.per_loop(i, 1, lambda: (pages((i, 0), 0, (i, -1)), pages((i, 1), 1, (i, 0))))
            link.after_loop()
            for j in range(NPG - 2, NPG):
                head_sums(7, 1, j)
            for step in (scores, shift, row_sums, normalise):
                step(7, 1)
            v.wait_ge(v_full, V_OV + 1)
            v.tensor_copy(mixT[:, 0:4, SEQ:T], sv(V_OV)[:, 0, 0:32].rearrange("p (k b) -> p k b", k=4)).then_inc(v_free, 1)

            for x in range(3):
                n = V_BF + x
                v.wait_ge(v_full, n + 1)
                if x < 2:
                    v.tensor_copy(bm64[:, x * 1024:(x + 1) * 1024], sv(n)[0:64].rearrange("p b n -> p (b n)")).then_inc(v_free, 1)
                else:
                    v.tensor_copy(bm64[:, 2048:2049], sv(n)[0:64, 0, 0:1]).then_inc(v_free, 1)
            v.wait_ge(mask_back, 16)
            link(v.tensor_tensor(bm64, bm64, s64, ALU.add))
            by_slot = bm64[:, 0:PAST].rearrange("r (p j) -> r j p", j=NPG)
            for x in range(2):
                n = V_SD + x
                v.wait_ge(v_full, n + 1)
                for g in range(2):
                    c4 = 2 * x + g
                    ins = v.scalar_tensor_tensor(s64[:, c4 * 512:(c4 + 1) * 512].rearrange("r (j p) -> r j p", j=4),
                                                 sv(n)[0:64, g, :].rearrange("r (j p) -> r j p", j=4), DSA_SCALE,
                                                 by_slot[:, 4 * c4:4 * c4 + 4, :], ALU.mult, ALU.add)
                ins.then_inc(v_free, 1)
            v.wait_ge(v_full, V_SN + 1)
            v.tensor_tensor_reduce(small[0:64, 0:8], sv(V_SN)[0:64, 0, 0:8], sel[0:64, 72:80], 1.0, 0.0, ALU.mult, ALU.add,
                                   small[0:64, 8:9]).then_inc(v_free, 1)
            v.wait_ge(v_free, V_SN + 1)
            link(v.scalar_tensor_tensor(s64[:, PAST:PAST + 1], small[0:64, 8:9], DSA_SCALE, bm64[:, PAST:PAST + 1], ALU.mult, ALU.add))
            link(v.tensor_reduce(small[0:64, 11:12], s64, AXX, ALU.max))
            v.tensor_scalar(small[0:64, 9:10], small[0:64, 11:12], -1.0, None, ALU.mult).then_inc(s64_ready, 1)
            v.wait_ge(p64_exp, 1)
            link(v.reciprocal(small[0:64, 12:13], small[0:64, 10:11]))
            link(v.tensor_scalar(s64, s64, small[0:64, 12:13], None, ALU.mult))
            v.tensor_scalar(small[0:64, 0:8], sel[0:64, 72:80], s64[:, PAST:PAST + 1], None, ALU.mult).then_inc(p64_ready, 1)
            split_tile(v, 0, 0)
            split_tile(v, 0, 1)
            v.wait_ge(a_free, A_OD + 1)
            for c in range(2):
                for par in range(2):
                    ins = v.tensor_copy(mixT[par * 64:par * 64 + 64, 4 + 2 * c:6 + 2 * c, SEQ:T],
                                        odT[c * 64:c * 64 + 64, :, 4 * c + par:4 * c + 4:2].rearrange("p b h -> p h b"))
            ins.then_inc(mix_s, 1)

        def split(v, raw, low, high, need, count, n):
            v.wait_ge(need, count)
            v.tensor_copy(high, raw).then_inc(w_high, 1)
            v.wait_ge(w_high, n + 1)
            v.tensor_tensor(low, raw, high.bitcast(F32), ALU.subtract).then_inc(w_split, 1)

        def split_tile(v, i, s):
            split(v, wraw[s], wlow[s], whigh[s], tail_w[s], i * 16 + 16, i * 4 + s)

        def split_down(v, i, s):
            split(v, draw[s], dlow[s], dhigh[s], down_w[s], i * 16 + 16, i * 4 + (NT + s))

        def split_input(v, n, k):
            v.tensor_copy(xhigh[:, k:k + 4, :], hT[:, k:k + 4, :]).then_inc(x_high, 1)
            v.wait_ge(x_high, n + 1)
            v.tensor_tensor(xlow[:, k:k + 4, :], hT[:, k:k + 4, :], xhigh[:, k:k + 4, :].bitcast(F32), ALU.subtract).then_inc(x_split, 1)

        def dve_tail(v, link):
            for g in range(2):
                v.wait_ge(a_free, A_MIX + g + 1)
                link(v.reciprocal(sd[:, g, :], sd[:, g, :]))
                for k in range(4 * g, 4 * g + 4):
                    v.scalar_tensor_tensor(mixT[:, k, :], mixT[:, k, :], gT[:, G_OUT + k:G_OUT + k + 1], sd[:, g, :],
                                           ALU.mult, ALU.mult).then_inc(mixed, 1)
                v.wait_ge(mixed, 4 * g + 4)
                split_input(v, g, 4 * g)

            def add_gated(slot, m, gate, count, s):
                x = xT[:, bass.ds(m, 1), :].rearrange("p a t -> p (a t)")
                gt = modT[:, bass.ds(m + gate, 1), :].rearrange("p a c -> p (a c)")
                v.wait_ge(v_full, count)
                v.scalar_tensor_tensor(x[:, 0:HT], slot[:, 0, 0:HT], gt[:, 0:1], x[:, 0:HT], ALU.mult, ALU.add)
                v.scalar_tensor_tensor(x[:, HT:SEQ], slot[:, 1, 0:SEQ - HT], gt[:, 0:1], x[:, HT:SEQ], ALU.mult, ALU.add)
                v.tensor_tensor(gated[:, s, :], slot[:, 1, SEQ - HT:HT], gt[:, 1:9], ALU.mult).then_inc(v_free, 1)
                v.wait_ge(v_free, count)
                v.tensor_tensor(x[:, SEQ:T], x[:, SEQ:T], gated[:, s, :], ALU.add).then_inc(x_new, 1)

            with v.Fori(0, 2) as i:
                for s in range(4):
                    split_tile(v, i + (s + 2) // 4, (s + 2) % 4)
                    add_gated(sv(V_OUT + s), i * 4 + s, 16, i * 4 + (V_OUT + s + 1), s % 2)
            v.wait_ge(a_free, A_SS2 + 1)
            modulate(v, link, 1)
            for g in range(2):
                v.wait_ge(h2_done, 4 * g + 5)
                split_input(v, 2 + g, 4 * g)
            if PADV:
                v.wait_ge(v_full, V_OUT + 9)
                v.tensor_copy(stat[0:1, 0, 1:2], sv(V_OUT + 8)[0:1, 0, 0:1]).then_inc(v_free, 1)

            def gate_turn(i, ahead):
                for s in range(2):
                    if s == 0 or ahead:
                        for c in range(2):
                            split_tile(v, i + (2 + (s + 1) // 2), (s + 1) % 2 * 2 + c)
                    v.wait_ge(v_full, i * 2 + (V_U + s + 1))
                    v.wait_ge(a_free, i * 2 + (A_G + s + 1))
                    t = actT[:, bass.ds(i * 2 + s, 1), :].rearrange("p a (h t) -> p (a h) t", h=2)
                    v.tensor_tensor(t, t, sv(V_U + s)[:, :, 0:HT], ALU.mult).then_inc(v_free, 1)

            with v.Fori(0, KF // 2 - 1) as i:
                gate_turn(i, True)
            gate_turn(KF // 2 - 1, False)
            v.wait_ge(v_free, V_U + KF)
            v.wait_ge(tokens_stored, 16 * 15)
            split_down(v, 0, 0)
            for k in range(KF):
                v.tensor_copy(ahigh[k], actT[:, k, :]).then_inc(a_high, 1)
                v.wait_ge(a_high, k + 1)
                v.tensor_tensor(alow[:, k, :], actT[:, k, :], ahigh[k].bitcast(F32), ALU.subtract).then_inc(a_split, 1)
                if k == KF // 2 - 1:
                    split_down(v, 0, 1)

            def down_turn(i, ahead):
                for s in range(4):
                    if s < 2 or ahead:
                        split_down(v, i + (s + 2) // 4, (s + 2) % 4)
                    if s % 2 == 1:
                        add_gated(sv(V_DN + s // 2), i * 2 + s // 2, 40, i * 2 + (V_DN + s // 2 + 1), s // 2)

            with v.Fori(0, 3) as i:
                down_turn(i, True)
            down_turn(3, False)

        def modulate(v, link, w):
            v.wait_ge(a_free, (A_SS, A_SS2)[w] + 1)
            scaled, done = ((hT_scaled, hT_done), (h2_scaled, h2_done))[w]
            link(v.reciprocal(sd[:, 0, :], sd[:, 0, :]))
            hs = hT[:, :, SEQ:T]
            link(v.tensor_tensor(hs, xT[:, :, SEQ:T], amod[:, w, :, 1:9], ALU.mult))
            link(v.tensor_tensor(hs, hs, sd[:, 0, SEQ:T].unsqueeze(1).broadcast_to([128, 8, NB]), ALU.mult))
            v.tensor_tensor(hs, hs, modT[:, w * 24:w * 24 + 8, 1:9], ALU.add).then_inc(done, 1)
            v.wait_ge(done, 1)
            for k in range(KD):
                v.scalar_tensor_tensor(hT[:, k, 0:SEQ], xT[:, k, 0:SEQ], amod[:, w, k, 0:1], sd[:, 0, 0:SEQ],
                                       ALU.mult, ALU.mult).then_inc(scaled, 1)

        def pool_program(g):
            g.memset(tok[:, 4, :], 0.0).then_inc(zeroed, 1)
            g.wait_ge(a_free, A_MOD + 1)
            g.wait_ge(a_full, A_XT[6] + 1)
            g.memset(qiz[:], 0.0)
            g.memset(qz, 0.0).then_inc(zeroed, 1)
            for t in range(5):
                g.wait_ge(a_free, A_TOK + t + 1)
                w = 128 if t < 4 else NB
                tt = slice(t * 128, t * 128 + w)
                if t < 4:
                    outs = (o["mla_p"][0, 0, tt, :], o["kv_p"][0, 0, tt].rearrange("t a c d -> t (a c d)"), o["idx_p"][0, 0, tt, :])
                else:
                    outs = (o["mla_s"][0, :, 0, :], o["kv_s"][0, :, 0].rearrange("t a c d -> t (a c d)"), o["idx_s"][0, :, 0, :])
                for (c0, c1), dst in zip(((0, 288), (288, 544), (544, 608)), outs):
                    g.dma_start(dst, tok[0:w, t, c0:c1]).then_inc(tokens_stored, 16)
            def fetch(dst, name, width, b, done):
                n = a[name].shape[1]
                src = bass.AP(a[name].tensor, 0, [[16 * width, n * 8], [1, 16 * width]])
                g.indirect_dma_start(out=dst, out_offset=None, in_=src,
                                     in_offset=bass.IndirectOffsetOnAxis(ap=rows_of[:, b:b + 1], axis=0)).then_inc(done, 16)

            g.wait_ge(rows_ready, 1)
            g.wait_ge(v_free, V_BIAS + 1)
            for b in range(NB):
                if b >= 2:
                    g.wait_ge(a_full, A_IP + 2 * b - 2)
                fetch(ip[:, b % 2, :], "cache_idx", IDX, b, idx_pages[b % 2])
            mla_rows = lambda b: fetch(pgs[:, b % 2].rearrange("p j n -> p (j n)"), "cache_mla", ROW, b, mla_pages[b % 2])
            kv_rows_of = lambda b, s: fetch(kvp[s].rearrange("p j n -> p (j n)"), "cache_kv", 256, b, kv_rows[s])
            g.wait_ge(v_full, V_S + len(AT) // 2)
            mla_rows(0)
            g.wait_ge(v_full, V_S + len(AT))
            mla_rows(1)
            g.wait_ge(pv_done, len(AT))
            kv_rows_of(0, 0)
            g.wait_ge(qbc_loaded, 16)

            def rope_pages(b, par, loads, c):
                q = qbc[:, b]
                g.wait_ge(mla_pages[par], loads)
                if b > 0 or c >= 2:
                    g.wait_ge(rope_sum, 4 * b + c - 1)
                g.tensor_tensor(rp[:, c % 2], pgs[:, par, 4 * c:4 * c + 4, KVR:ROW].unsqueeze(2).broadcast_to([128, 4, H, ROPE]),
                                q[:, :, NOPE:QK].unsqueeze(1).broadcast_to([128, 4, H, ROPE]), ALU.mult).then_inc(rope_mul, 1)

            def head_max(b):
                g.wait_ge(smax, b + 1)
                g.partition_all_reduce(hstat[:, 1, :], hstat[:, 0, :], 128, RMAX).then_inc(gmax, 1)

            def head_sum(b):
                g.wait_ge(psum_ready, b + 1)
                g.partition_all_reduce(hstat[:, 3, :], hstat[:, 2, :], 128, RADD).then_inc(gsum, 1)

            def halve(b, j):
                g.wait_ge(squared, b * NPG + j + 1)
                g.tensor_tensor(sqk[j % 4][:, :, 0:32], sqk[j % 4][:, :, 0:32], sqk[j % 4][:, :, 32:64], ALU.add)
                g.wait_ge(v_free, V_KX + b * NPG + j + 1)
                g.tensor_tensor(pr[j % 4][:, :, 0:32], pr[j % 4][:, :, 0:32], pr[j % 4][:, :, 32:64], ALU.add).then_inc(halved, 1)

            for b in range(NB):
                if b == 2:
                    g.wait_ge(qbc_rest, 16)
                for j in range(NPG):
                    if j in (0, 3, 8, 11):
                        rope_pages(b, b % 2, 16 * (b // 2 + 1), (0, 3, 8, 11).index(j))
                    halve(b, j)
                    if b >= 1 and j == 2:
                        head_max(b - 1)
                    if b >= 1 and j == 6:
                        head_sum(b - 1)
                    if 1 <= b < NB - 1 and j == 9:
                        g.wait_ge(lat_pv, b)
                        mla_rows(b + 1)
                    if b == NB - 1 and j == 10:
                        g.wait_ge(lat_pv, b)
                        kv_rows_of(1, 1)
            head_max(NB - 1)
            head_sum(NB - 1)
            g.wait_ge(lat_pv, NB)
            for b in range(2, NB):
                if b >= 3:
                    g.wait_ge(a_full, A_KD + 4 * b - 8)
                kv_rows_of(b, b % 3)
            g.wait_ge(a_free, A_PD + 3)
            for t, b in enumerate(V_ORDER):
                if t >= 2:
                    g.wait_ge(d_pv, t - 1)
                g.tensor_copy(ptb[:, t % 2], ptd[:, :, b * 8:b * 8 + 8]).then_inc(ptb_ready, 1)
                if 1 <= t and t + 2 < NB:
                    g.wait_ge(d_pv, t)
                    kv_rows_of(V_ORDER[t + 2], (t + 2) % 3)
            g.wait_ge(tokens_stored, 16 * 15)

        block = ctx.enter_context(nc.Block())
        block.sync(lambda e: sp_program(e))
        block.tensor(lambda e: pe_program(e))
        block.scalar(lambda e: act_program(e))
        block.vector(lambda e: dve_program(e))
        block.gpsimd(lambda e: pool_program(e))


_INS = ["x_prompt", "x_sample", "c_prompt", "c_sample", "cache_mla", "cache_kv", "cache_idx", "page_table",
        "rel_bias", "w_ada", "b_ada", "g_norm_mix", "g_norm_ffn", "w_in", "g_q_lat", "w_uq", "g_kv_lat", "w_ukv",
        "g_mla_q_nope", "g_mla_q_rope", "g_mla_k_nope", "g_mla_k_rope", "g_dsa_q", "g_dsa_k", "g_out", "w_out",
        "w_ffn_in", "w_ffn_out"]
_OUTS = [("y_p", (1, SEQ, D)), ("y_s", (NB, 1, D)),
         ("mla_p", (1, 1, SEQ, ROW)), ("kv_p", (1, 1, SEQ, 2, 2, HD)), ("idx_p", (1, 1, SEQ, IDX)),
         ("mla_s", (1, NB, 1, ROW)), ("kv_s", (1, NB, 1, 2, 2, HD)), ("idx_s", (1, NB, 1, IDX))]


def kernel(**inputs):
    import concourse.bacc as _bacc
    from concourse.bass_utils import run_bass_kernel_spmd as _run

    nc = _bacc.Bacc("TRN2", target_bir_lowering=False, num_devices=1)
    arrays = {name: np.ascontiguousarray(inputs[name]) for name in _INS}
    arrays.update(shape_constants())
    ins = {k: nc.dram_tensor(k, v.shape, mybir.dt.from_np(v.dtype), kind="ExternalInput").ap() for k, v in arrays.items()}
    outs = {k: nc.dram_tensor(k, shape, F32, kind="ExternalOutput").ap() for k, shape in _OUTS}
    build(nc, ins, outs)
    r = _run(nc, [arrays], core_ids=[0])
    return tuple(r.results[0][k] for k, _ in _OUTS)
```
